# Optimizing a Trainium2 kernel written in Bass

```python
import jax
import jax.numpy as jnp
from jax import lax
import numpy as np

D_MODEL = 1024
BATCH = 1
SEQ = 512
DEPTH = 2
DEC_BATCH = 8
DEC_SEQ = 4
PAST_LEN = 256
PAGE_SIZE = 128

N_MIXERS = 2
CONV_EXPAND = 2
D_CONV = CONV_EXPAND * D_MODEL
CONV_WIDTH = 31
CONV_STATE = CONV_WIDTH - 1
N_HEADS = 16
HEAD_DIM = D_MODEL // N_HEADS
N_KV_GROUPS = 4
HEADS_PER_GROUP = N_HEADS // N_KV_GROUPS
D_ATTN = N_HEADS * HEAD_DIM
D_KV = N_KV_GROUPS * HEAD_DIM
CMP_BLOCK = 32
CMP_STRIDE = 16
CMP_HIDDEN = 2 * HEAD_DIM
SEL_BLOCK = 64
N_SELECT = 16
WINDOW = 512
N_BRANCH = 3
N_KV_SLOTS = 6
N_PAGED_SLOTS = 4
Q_BLOCK = 64
NSA_IN = 2 * D_ATTN + N_KV_SLOTS * D_KV + N_BRANCH * N_HEADS
N_CONV_LAYERS = (DEPTH + 1) // 2
N_NSA_LAYERS = DEPTH // 2
NORM_EPS = 1e-6
FORCE_SCORE = 1e4

kernel_name = "conformer_conv_nsa_hybrid_step"

def rms_norm(x, g):
    xf = x.astype(jnp.float32)
    y = xf * lax.rsqrt(jnp.mean(xf * xf, axis=-1, keepdims=True) + NORM_EPS)
    return (y * g.astype(jnp.float32)).astype(x.dtype)

def layer_norm(x, g, b):
    xf = x.astype(jnp.float32)
    xc = xf - jnp.mean(xf, axis=-1, keepdims=True)
    var = jnp.mean(xc * xc, axis=-1, keepdims=True)
    y = xc * lax.rsqrt(var + NORM_EPS) * g.astype(jnp.float32) + b.astype(jnp.float32)
    return y.astype(x.dtype)

def alibi_slopes():
    h = jnp.arange(1, N_HEADS + 1, dtype=jnp.float32)
    return jnp.exp2(-8.0 * h / N_HEADS).reshape(1, 1, N_KV_GROUPS, HEADS_PER_GROUP, 1)

def masked_softmax(s, mask):
    s = jnp.where(mask, s, -jnp.inf)
    m = jnp.max(s, axis=-1, keepdims=True)
    m = jnp.where(jnp.isfinite(m), m, 0.0)
    e = jnp.where(mask, jnp.exp(s - m), 0.0)
    return e / jnp.maximum(jnp.sum(e, axis=-1, keepdims=True), 1e-30)

def conv_mixer(h, buf, w_in, dw_w, dw_b, ln_g, ln_b, w_out):
    a, gl, z = jnp.split(h @ w_in, 3, axis=-1)
    v = a * jax.nn.sigmoid(gl)
    vp = jnp.concatenate([buf.astype(v.dtype), v], axis=1)
    c = lax.conv_general_dilated(vp, dw_w[:, None, :].astype(vp.dtype), window_strides=(1,), padding="VALID",
                                 dimension_numbers=("NWC", "WIO", "NWC"), feature_group_count=D_CONV) + dw_b
    c = jax.nn.silu(layer_norm(c, ln_g, ln_b))
    y = (c * jax.nn.silu(z)) @ w_out
    return y, vp[:, -CONV_STATE:]

def nsa_project(h, w_in):
    b, t = h.shape[:2]
    u = h @ w_in
    q, z, kv, gl = jnp.split(u, [D_ATTN, 2 * D_ATTN, 2 * D_ATTN + N_KV_SLOTS * D_KV], axis=-1)
    return (q.reshape(b, t, N_HEADS, HEAD_DIM), z,
            kv.reshape(b, t, N_KV_SLOTS, N_KV_GROUPS, HEAD_DIM),
            gl.reshape(b, t, N_HEADS, N_BRANCH))

def compress(k, pe, w1, w2):
    n_cmp = (k.shape[1] - CMP_BLOCK) // CMP_STRIDE + 1
    idx = jnp.arange(n_cmp)[:, None] * CMP_STRIDE + jnp.arange(CMP_BLOCK)[None, :]
    kb = k[:, idx] + pe[:, None, :]
    hid = jax.nn.silu(jnp.einsum("bclgd,ldh->bcgh", kb, w1))
    c_end = jnp.arange(n_cmp) * CMP_STRIDE + (CMP_BLOCK - 1)
    return jnp.einsum("bcgh,hd->bcgd", hid, w2), c_end

def to_blocks(k):
    b, t = k.shape[:2]
    return k.reshape(b, t // SEL_BLOCK, SEL_BLOCK, N_KV_GROUPS, HEAD_DIM).transpose(0, 3, 1, 2, 4)

def nsa_core(q, gate_logit, q_pos, kc, vc, c_end, ks_blk, vs_blk, kw, vw, w_pos):
    b, nq = q.shape[:2]
    n_sb = ks_blk.shape[2]
    scale = HEAD_DIM ** -0.5
    slopes = alibi_slopes()
    qg = q.reshape(b, nq, N_KV_GROUPS, HEADS_PER_GROUP, HEAD_DIM)

    dist_c = q_pos[:, None] - c_end[None, :]
    s_c = (jnp.einsum("bqghd,bcgd->bqghc", qg, kc).astype(jnp.float32) * scale
           - slopes * dist_c[None, :, None, None, :].astype(jnp.float32))
    p_c = masked_softmax(s_c, (dist_c >= 0)[None, :, None, None, :])
    o_c = jnp.einsum("bqghc,bcgd->bqghd", p_c.astype(vc.dtype), vc)

    blk = jnp.arange(n_sb)
    c_start = c_end - (CMP_BLOCK - 1)
    overlap = ((c_start[:, None] < (blk[None, :] + 1) * SEL_BLOCK)
               & (c_end[:, None] >= blk[None, :] * SEL_BLOCK)).astype(jnp.float32)
    imp = jnp.einsum("bqghc,cj->bqgj", p_c, overlap)
    cur = (q_pos // SEL_BLOCK)[:, None]
    forced = (blk[None, :] == 0) | (blk[None, :] == cur) | (blk[None, :] == cur - 1)
    eligible = blk[None, :] <= cur
    score = jnp.where(forced[None, :, None, :], FORCE_SCORE, imp)
    score = jnp.where(eligible[None, :, None, :], score, -jnp.inf)
    top_s, top_i = lax.top_k(score, min(N_SELECT, n_sb))
    bi = jnp.arange(b)[:, None, None, None]
    gi = jnp.arange(N_KV_GROUPS)[None, None, :, None]
    k_sel = ks_blk[bi, gi, top_i]
    v_sel = vs_blk[bi, gi, top_i]
    n_keys = top_i.shape[-1] * SEL_BLOCK
    key_pos = top_i[..., None] * SEL_BLOCK + jnp.arange(SEL_BLOCK)
    dist_s = q_pos[None, :, None, None, None] - key_pos
    s_s = (jnp.einsum("bqghd,bqgnld->bqghnl", qg, k_sel).astype(jnp.float32) * scale
           - slopes[..., None] * dist_s[:, :, :, None].astype(jnp.float32))
    mask_s = (jnp.isfinite(top_s)[..., None] & (dist_s >= 0)).reshape(b, nq, N_KV_GROUPS, 1, n_keys)
    p_s = masked_softmax(s_s.reshape(b, nq, N_KV_GROUPS, HEADS_PER_GROUP, n_keys), mask_s)
    o_s = jnp.einsum("bqghm,bqgmd->bqghd", p_s.astype(v_sel.dtype),
                     v_sel.reshape(b, nq, N_KV_GROUPS, n_keys, HEAD_DIM))

    dist_w = q_pos[:, None] - w_pos[None, :]
    s_w = (jnp.einsum("bqghd,bwgd->bqghw", qg, kw).astype(jnp.float32) * scale
           - slopes * dist_w[None, :, None, None, :].astype(jnp.float32))
    mask_w = ((dist_w >= 0) & (dist_w <= WINDOW) & (w_pos[None, :] >= 0))[None, :, None, None, :]
    p_w = masked_softmax(s_w, mask_w)
    o_w = jnp.einsum("bqghw,bwgd->bqghd", p_w.astype(vw.dtype), vw)

    g = jax.nn.sigmoid(gate_logit.astype(jnp.float32)).reshape(b, nq, N_KV_GROUPS, HEADS_PER_GROUP, N_BRANCH, 1)
    o = g[..., 0, :] * o_c + g[..., 1, :] * o_s + g[..., 2, :] * o_w
    return o.reshape(b, nq, D_ATTN).astype(q.dtype)

def nsa_prompt(h, w_in, w_out, pe, w1, w2):
    bsz, t = h.shape[:2]
    q, z, kv, gl = nsa_project(h, w_in)
    kc, c_end = compress(kv[:, :, 0], pe[0], w1[0], w2[0])
    vc, _ = compress(kv[:, :, 1], pe[1], w1[1], w2[1])
    ks_blk = to_blocks(kv[:, :, 2])
    vs_blk = to_blocks(kv[:, :, 3])
    kvw = jnp.concatenate([jnp.zeros((bsz, WINDOW, 2, N_KV_GROUPS, HEAD_DIM), kv.dtype), kv[:, :, 4:6]], axis=1)
    n_qb = t // Q_BLOCK
    qb = q.reshape(bsz, n_qb, Q_BLOCK, N_HEADS, HEAD_DIM).swapaxes(0, 1)
    glb = gl.reshape(bsz, n_qb, Q_BLOCK, N_HEADS, N_BRANCH).swapaxes(0, 1)

    def block(args):
        i, q_i, g_i = args
        qs = i * Q_BLOCK
        q_pos = qs + jnp.arange(Q_BLOCK)
        w = lax.dynamic_slice_in_dim(kvw, qs, WINDOW + Q_BLOCK, axis=1)
        w_pos = qs - WINDOW + jnp.arange(WINDOW + Q_BLOCK)
        return nsa_core(q_i, g_i, q_pos, kc, vc, c_end, ks_blk, vs_blk, w[:, :, 0], w[:, :, 1], w_pos)

    o = lax.map(block, (jnp.arange(n_qb), qb, glb)).swapaxes(0, 1).reshape(bsz, t, D_ATTN)
    y = (o * jax.nn.silu(z)) @ w_out
    return y, kv[:, :, :N_PAGED_SLOTS], kv[:, t - min(WINDOW, t):, 4:6]

def nsa_sample(h, cache_kv, li, page_table, win_buf, w_in, w_out, pe, w1, w2):
    s = h.shape[1]
    past = page_table.shape[1] * PAGE_SIZE
    q, z, kv, gl = nsa_project(h, w_in)
    q_pos = past + jnp.arange(s)
    total = past + s
    n_sb = -(-total // SEL_BLOCK)
    sel_pad = n_sb * SEL_BLOCK - total
    win_keep = win_buf.shape[1]
    w_pos = past - win_keep + jnp.arange(win_keep + s)

    def one_seq(args):
        pages, kv_i, q_i, g_i, wb_i = args
        past_kv = cache_kv[li, pages].reshape(past, N_PAGED_SLOTS, N_KV_GROUPS, HEAD_DIM)
        full = jnp.concatenate([past_kv.astype(kv_i.dtype), kv_i[:, :N_PAGED_SLOTS]], axis=0)[None]
        kc, c_end = compress(full[:, :, 0], pe[0], w1[0], w2[0])
        vc, _ = compress(full[:, :, 1], pe[1], w1[1], w2[1])
        sel = jnp.pad(full[:, :, 2:4], ((0, 0), (0, sel_pad), (0, 0), (0, 0), (0, 0)))
        w = jnp.concatenate([wb_i.astype(kv_i.dtype), kv_i[:, 4:6]], axis=0)[None]
        o = nsa_core(q_i[None], g_i[None], q_pos, kc, vc, c_end, to_blocks(sel[:, :, 0]), to_blocks(sel[:, :, 1]),
                     w[:, :, 0], w[:, :, 1], w_pos)
        return o[0]

    o = lax.map(one_seq, (page_table, kv, q, gl, win_buf))
    y = (o * jax.nn.silu(z)) @ w_out
    new_win = jnp.concatenate([win_buf.astype(kv.dtype), kv[:, :, 4:6]], axis=1)[:, -win_keep:]
    return y, kv[:, :, :N_PAGED_SLOTS], new_win

def setup_inputs(seed: int = 0) -> dict:
    key = jax.random.key(seed)
    ks = jax.random.split(key, 24)
    nrm = lambda k, shape, sc: jax.random.normal(k, shape, jnp.float32) * sc
    n_pages = PAST_LEN // PAGE_SIZE
    n_used = DEC_BATCH * n_pages
    n_pool = (5 * n_used + 3) // 4
    perm = jax.random.permutation(ks[0], n_pool)
    page_table = perm[:n_used].reshape(DEC_BATCH, n_pages).astype(jnp.int32)
    win_keep = min(WINDOW, PAST_LEN)
    return {
        "x_prompt": nrm(ks[1], (BATCH, SEQ, D_MODEL), 1.0),
        "x_sample": nrm(ks[2], (DEC_BATCH, DEC_SEQ, D_MODEL), 1.0),
        "cache_kv": nrm(ks[3], (N_NSA_LAYERS, n_pool, PAGE_SIZE, N_PAGED_SLOTS, N_KV_GROUPS, HEAD_DIM), 1.0),
        "state_kv_win": nrm(ks[4], (N_NSA_LAYERS, DEC_BATCH, win_keep, 2, N_KV_GROUPS, HEAD_DIM), 1.0),
        "state_conv": nrm(ks[5], (N_CONV_LAYERS, DEC_BATCH, CONV_STATE, D_CONV), 0.5),
        "page_table": page_table,
        "norm_g": 1.0 + nrm(ks[6], (DEPTH, D_MODEL), 0.02),
        "final_norm_g": 1.0 + nrm(ks[7], (D_MODEL,), 0.02),
        "conv_w_in": nrm(ks[8], (N_CONV_LAYERS, D_MODEL, 3 * D_CONV), D_MODEL ** -0.5),
        "conv_dw_w": nrm(ks[9], (N_CONV_LAYERS, CONV_WIDTH, D_CONV), CONV_WIDTH ** -0.5),
        "conv_dw_b": nrm(ks[10], (N_CONV_LAYERS, D_CONV), 0.02),
        "conv_ln_g": 1.0 + nrm(ks[11], (N_CONV_LAYERS, D_CONV), 0.02),
        "conv_ln_b": nrm(ks[12], (N_CONV_LAYERS, D_CONV), 0.02),
        "conv_w_out": nrm(ks[13], (N_CONV_LAYERS, D_CONV, D_MODEL), D_CONV ** -0.5),
        "nsa_w_in": nrm(ks[14], (N_NSA_LAYERS, D_MODEL, NSA_IN), D_MODEL ** -0.5),
        "nsa_w_out": nrm(ks[15], (N_NSA_LAYERS, D_ATTN, D_MODEL), D_ATTN ** -0.5),
        "nsa_cmp_pe": nrm(ks[16], (N_NSA_LAYERS, 2, CMP_BLOCK, HEAD_DIM), 0.1),
        "nsa_cmp_w1": nrm(ks[17], (N_NSA_LAYERS, 2, CMP_BLOCK, HEAD_DIM, CMP_HIDDEN), (CMP_BLOCK * HEAD_DIM) ** -0.5),
        "nsa_cmp_w2": nrm(ks[18], (N_NSA_LAYERS, 2, CMP_HIDDEN, HEAD_DIM), CMP_HIDDEN ** -0.5),
    }

def reference(x_prompt, x_sample, cache_kv, state_kv_win, state_conv, page_table, norm_g, final_norm_g,
              conv_w_in, conv_dw_w, conv_dw_b, conv_ln_g, conv_ln_b, conv_w_out,
              nsa_w_in, nsa_w_out, nsa_cmp_pe, nsa_cmp_w1, nsa_cmp_w2):
    xp, xs = x_prompt, x_sample
    kv_p, kv_s, win_p, win_s, conv_p, conv_s = [], [], [], [], [], []
    for layer in range(DEPTH):
        j = layer // N_MIXERS
        hp = rms_norm(xp, norm_g[layer])
        hs = rms_norm(xs, norm_g[layer])
        if layer % N_MIXERS == 0:
            conv_args = (conv_w_in[j], conv_dw_w[j], conv_dw_b[j], conv_ln_g[j], conv_ln_b[j], conv_w_out[j])
            zero_buf = jnp.zeros((xp.shape[0], CONV_STATE, D_CONV), xp.dtype)
            yp, cp = conv_mixer(hp, zero_buf, *conv_args)
            ys, cs = conv_mixer(hs, state_conv[j], *conv_args)
            conv_p.append(cp)
            conv_s.append(cs)
        else:
            nsa_args = (nsa_w_in[j], nsa_w_out[j], nsa_cmp_pe[j], nsa_cmp_w1[j], nsa_cmp_w2[j])
            yp, kp, wp = nsa_prompt(hp, *nsa_args)
            ys, kq, wq = nsa_sample(hs, cache_kv, j, page_table, state_kv_win[j], *nsa_args)
            kv_p.append(kp)
            kv_s.append(kq)
            win_p.append(wp)
            win_s.append(wq)
        xp = xp + yp
        xs = xs + ys
    y_prompt = rms_norm(xp, final_norm_g)
    y_sample = rms_norm(xs, final_norm_g)
    kv_prompt = jnp.stack(kv_p)
    kv_sample = jnp.stack(kv_s)
    win_prompt = jnp.stack(win_p)
    win_sample = jnp.stack(win_s)
    conv_prompt = jnp.stack(conv_p)
    conv_sample = jnp.stack(conv_s)
    return (y_prompt, y_sample, kv_prompt, kv_sample, win_prompt, win_sample, conv_prompt, conv_sample)


_drawn_inputs = setup_inputs


def setup_inputs(seed=0):
    import zlib

    import numpy as np

    out = dict(_drawn_inputs(seed))
    spreads = {}
    factors = {'final_norm_g': 2.865,
     'conv_dw_b': 3.995,
     'conv_ln_g': 7.023,
     'conv_ln_b': 8.0,
     'nsa_cmp_pe': 3.658}
    for name, (base, spread) in spreads.items():
        noise = np.random.default_rng([zlib.crc32(name.encode()), seed]).standard_normal(out[name].shape)
        drawn = base * np.exp(spread * noise) if base else spread * noise
        out[name] = jnp.asarray(drawn.astype(out[name].dtype))
    for name, factor in factors.items():
        out[name] = (out[name] * factor).astype(out[name].dtype)
    return out
```

```python
import numpy as np
import concourse.bass as bass
from concourse import mybir
from contextlib import ExitStack

F32 = mybir.dt.float32
I32 = mybir.dt.int32
ACT = mybir.ActivationFunctionType
ALU = mybir.AluOpType
AX = mybir.AxisListType

P = 128
D = 1024
KT = D // P
NP_, NS_ = 512, 32
T = NP_ + NS_
TA = 256
TB = T - TA
SEQS, STEPS = 8, 4
DC = 2048
CT = DC // P
TAPS = 31
STATE = TAPS - 1
EPS = 1e-6
HEADS, HD, GROUPS = 16, 64, 4
HPG = HEADS // GROUPS
PAST, PAGE = 256, 128
NPG = PAST // PAGE
SEL = 64
CSTRIDE, CBLK = 16, 32
NCP = (NP_ - CBLK) // CSTRIDE + 1
NCS = (PAST + STEPS - CBLK) // CSTRIDE + 1
NEG = -1e30
FLOOR = -1e28
GL = HEADS * 3
VTOK = 2 * GROUPS * HD + GL
VH = VTOK // 2
FT_KV, FT_Q, FT_Z = 8, 8, 8
FT = FT_KV + FT_Q + FT_Z
NKEY = PAST + NS_

BASE = 16512


def reaches(i, n):
    return not isinstance(i, int) or i >= n


def build(nc, io):
    ctx = ExitStack()
    with ctx:
        used = {}

        def at(name, shape, offset, dt=F32):
            size = 4 * int(np.prod(shape[1:]))
            used[name] = (offset, size)
            return nc.alloc_sbuf_tensor_at(name, shape, dt, offset=offset)

        def sem(name):
            return ctx.enter_context(nc.semaphore(name))

        ROW = T * 4
        o = BASE
        X = at("X", [P, KT, T], o); o += KT * ROW
        SM = o; o += 12288
        HR = o; o += KT * ROW
        W1R = o; o += 16384
        G0 = o; o += 2 * KT * ROW
        G1 = o
        NR = 229344 - 4 * ROW
        s = SM
        ones = at("ones", [P, P], s); s += P * 4
        ident = at("ident", [P, P], s); s += P * 4
        gains = at("gains", [P, 3, KT], s); s += 96
        lng = at("lng", [P, CT], s); s += 64
        lnb = at("lnb", [P, CT], s); s += 64
        SMT = s
        taps = at("taps", [P, CT, 32], s); s += CT * 128
        tapc = at("tapc", [P, 2, 32], s); s += 256
        ctail = at("ctail", [P, CT, STATE], s); s += CT * STATE * 4
        SMX = s
        mean = at("mean", [P, T], NR)
        rstd = at("rstd", [P, T], NR + ROW)
        sq = at("sq", [P, 2, T], NR + 2 * ROW)
        H = at("H", [P, KT, T], HR)
        C = at("C", [P, CT, T], G0)
        s = G1
        Z1 = at("Z1", [P, CT, T], s); s += CT * ROW
        ringA = at("ringA", [P, 2, 3, KT, P], s); RINGA = s; s += 2 * 3 * KT * P * 4
        VS = at("VS", [P, CT, SEQS, STATE + STEPS], s); s += CT * SEQS * (STATE + STEPS) * 4
        VP = at("VP", [P, 2, STATE + NP_], s); s += 2 * 2176
        sig = at("sig", [P, 2, T], s); s += 2 * ROW
        acc = at("acc", [P, 2, NP_], s); s += 2 * NP_ * 4
        prod = at("prod", [P, 32, NS_], s); s += 32 * NS_ * 4
        assert s <= NR
        ringC = at("ringC", [P, 2, CT, P], RINGA)
        s = VSR = RINGA + 2 * 3 * KT * P * 4
        ringE = at("ringE", [P, 3, KT, P], s); s += 3 * KT * P * 4
        bias = at("bias", [P, 2, NP_], s); s += 2 * NP_ * 4
        rowsel = at("rowsel", [NS_, 2, P], s)
        vcs = at("vcs", [P, GROUPS * HD], s); s += GROUPS * HD * 4
        assert s <= VSR + 17408
        s = VSR + 17408
        wtok = at("wtok", [P, KT, VTOK], s)
        O = at("O", [P, 4, D], s); s += KT * VTOK * 4
        KK = at("KK", [P, 2, GROUPS, NP_ // 2], s)
        S = at("S", [P, 4, NP_], s); s += 4 * NP_ * 4
        assert s <= NR - 2048
        cache_cmp = at("cache_cmp", [P, 2, SEQS * GROUPS, P], G1)
        cache_sel = at("cache_sel", [P, SEQS, NPG, 4 * P], G1)
        s = RINGA - 2048
        KTm = at("KTm", [P, 2, 2, T], s); s += 4 * ROW
        V = at("V", [P, 5, VTOK], s); s += 5 * VTOK * 4
        PT = at("PT", [P, 2, NP_], s); s += 2 * NP_ * 4
        kcs = at("kcs", [P, 2, P], s); s += 2 * P * 4
        kcp = at("kcp", [P, 2, 32], s); s += 2 * 32 * 4
        KN = at("KN", [P, 4, NS_], s); s += 4 * NS_ * 4
        assert s <= VSR
        QT = at("QT", [P, 8, T], G0)
        ZT = at("ZT", [P, 8, T], G0 + KT * ROW)
        Y = at("Y", [P, KT, T], G0)
        W1 = at("W1", [P, 2, CBLK // 2, P], W1R)
        cbias = at("cbias", [P, 4, NP_], W1R)
        cache_win = at("cache_win", [P, SEQS, 8 * P], HR)
        s = NR
        hp = at("hp", [P, 2, GROUPS, 32], s); s += 2 * GROUPS * 32 * 4
        hs = at("hs", [P, 2, GROUPS, SEQS * 16], s); s += 2 * SEQS * GROUPS * 16 * 4
        sbias = at("sbias", [P, 2, 2, NKEY + P], NR)
        s = SMT
        vcd = at("vcd", [P, GROUPS, HPG * HD], s)
        s = SMX
        dist = at("dist", [P, NP_], s); s += NP_ * 4
        qblk = at("qblk", [P, SEQS, 2, 32], s); s += SEQS * 2 * 32 * 4
        slopes = at("slopes", [P, 8, 2], s); s += 64
        pe_in = at("pe_in", [P, 2, CBLK // 2], s); s += 128
        pe_hid = at("pe_hid", [P, 2], s); s += 32
        W2 = at("W2", [P, 2, HD], s); s += 512
        headsel = at("headsel", [P, 2, GL], s); s += 2 * GL * 4
        gates = at("gates", [P, 4, HEADS, 3], s); s += 4 * GL * 4
        nmax = at("nmax", [P, 16], s); s += 64
        rsum = at("rsum", [P, 16], s); s += 64
        gsc = at("gsc", [P, 2, 8], s); s += 64
        m16 = at("m16", [P, HEADS], s); s += 64
        s16 = at("s16", [P, HEADS], s); s += 64
        grow = at("grow", [P, 2, 2, 3], s); s += 64
        tick = at("tick", [1, 16], s); s += 64
        pages = at("pages", [1, SEQS * NPG], s, I32); s += 64
        assert s <= HR, (s, HR)
        qb = at("qb", [P, NP_], NR - 2048)
        gtmp = at("gtmp", [P, 2, 2, GL], NR - 2048)
        otmp = at("otmp", [P, 8, HD], VSR + 2 * KT * P * 4)

        ps = ctx.enter_context(nc.psum_tensor("ps", [P, 8, 512], F32))

        def halves(i):
            return ((ps[:, 2 * i, 0:TA], slice(0, TA)), (ps[:, 2 * i + 1, 0:TB], slice(TA, T)))

        def prompt_of(i):
            return ps[:, 2 * i:2 * i + 2, 0:TA]

        def sample_of(i):
            return ps[:, 2 * i + 1, TA:TB]

        x_in = sem("x_in")
        consts_in = sem("consts_in")
        gains_in = sem("gains_in")
        taps_in = sem("taps_in")
        state_in = sem("state_in")
        wA_in = [sem(f"wA_in{i}") for i in range(2)]
        wC_in = [sem(f"wC_in{i}") for i in range(2)]
        store_p = sem("store_p")
        store_s = sem("store_s")
        stored = sem("stored")
        squared = sem("squared")
        sq_summed = sem("sq_summed")
        mean_sq = sem("mean_sq")
        inv_var = sem("inv_var")
        rstd_ready = sem("rstd_ready")
        h_ready = sem("h_ready")
        ones_set = sem("ones_set")
        pads_set = sem("pads_set")
        prod_row = sem("prod_row")
        gate_done = sem("gate_done")
        lin_done = sem("lin_done")
        z_done = sem("z_done")
        sig_ready = sem("sig_ready")
        z_kept = sem("z_kept")
        tail_kept = sem("tail_kept")
        tap_set = sem("tap_set")
        v_ready = sem("v_ready")
        conv_step = sem("conv_step")
        pool_step = sem("pool_step")
        c_summed = sem("c_summed")
        mean_ready = sem("mean_ready")
        centered = sem("centered")
        scaled = sem("scaled")
        activated = sem("activated")
        z_act = sem("z_act")
        c_gated = sem("c_gated")
        out1_done = sem("out1_done")
        x_added = sem("x_added")

        wtok_in = sem("wtok_in")
        w1_in = sem("w1_in")
        small_in = sem("small_in")
        pages_in = sem("pages_in")
        cmp_in = sem("cmp_in")
        sel_in = sem("sel_in")
        win_in = sem("win_in")
        cbias_in = sem("cbias_in")
        sbias_in = sem("sbias_in")
        wE_in = [sem(f"wE_in{i}") for i in range(3)]
        wO_in = [sem(f"wO_in{i}") for i in range(2)]
        h2_ready = sem("h2_ready")
        f_done = sem("f_done")
        kv_kept = sem("kv_kept")
        tok_done = sem("tok_done")
        v_kept = sem("v_kept")
        grow_done = sem("grow_done")
        grow_kept = sem("grow_kept")
        zeros_set = sem("zeros_set")
        kk_stored = sem("kk_stored")
        grow_ready = sem("grow_ready")
        gates_ready = sem("gates_ready")
        hid_done = sem("hid_done")
        pe_kept = sem("pe_kept")
        hid_ready = sem("hid_ready")
        pads2_set = sem("pads2_set")
        comp_done = sem("comp_done")
        comp_kept = sem("comp_kept")
        q_kept = sem("q_kept")
        qblk_ready = sem("qblk_ready")
        zt_ready = sem("zt_ready")
        cs_done = sem("cs_done")
        cs_step = sem("cs_step")
        cs_exp = sem("cs_exp")
        cs_t = sem("cs_t")
        cs_pt = sem("cs_pt")
        cs_pv = sem("cs_pv")
        o_set = sem("o_set")
        qb_set = sem("qb_set")
        bias_set = sem("bias_set")
        qk_done = sem("qk_done")
        sc_ready = sem("sc_ready")
        exp_ready = sem("exp_ready")
        t_done = sem("t_done")
        pt_even = sem("pt_even")
        pt_odd = sem("pt_odd")
        pv_done = sem("pv_done")
        o_step = sem("o_step")
        ss_done = sem("ss_done")
        ss_ready = sem("ss_ready")
        ss_exp = sem("ss_exp")
        ss_step = sem("ss_step")
        ss_t = sem("ss_t")
        ss_pt = sem("ss_pt")
        ss_pv = sem("ss_pv")
        og_sample = sem("og_sample")
        o_t = sem("o_t")
        og = sem("og")
        out2_done = sem("out2_done")
        x2_added = sem("x2_added")
        y_ready = sem("y_ready")

        def split(ap):
            return ap.rearrange("p (b t) -> p b t", b=2)

        block = ctx.enter_context(nc.Block())

        @block.sync
        def _(sp):
            sp.dma_start(X[:], io["x"]).then_inc(x_in, 16)
            sp.dma_start(gains[:], io["gains"]).then_inc(gains_in, 16)

            def load_wA(c, par, turn):
                if turn is not None:
                    sp.wait_ge(z_done, c - 1)
                sp.dma_start(ringA[:, par], io["w_a"][c]).then_inc(wA_in[par], 16)

            load_wA(0, 0, None)
            sp.dma_start(pages[:], io["pages"]).then_inc(pages_in, 16)
            sp.dma_start(taps[:], io["taps"]).then_inc(taps_in, 16)
            load_wA(1, 1, None)
            sp.dma_start(VS[:], io["state"]).then_inc(state_in, 16)
            sp.dma_start(ident[:], io["ident"]).then_inc(consts_in, 16)
            sp.dma_start(lng[:], io["lng"]).then_inc(consts_in, 16)
            sp.dma_start(lnb[:], io["lnb"]).then_inc(consts_in, 16)
            with sp.Fori(1, CT // 2) as j:
                load_wA(2 * j, 0, j)
                load_wA(2 * j + 1, 1, j)
            for n in range(KT):
                if n < 2:
                    sp.wait_ge(z_done, CT)
                else:
                    sp.wait_ge(out1_done, n - 1)
                sp.dma_start(ringC[:, n % 2], io["w_c"][n]).then_inc(wC_in[n % 2], 16)
                if n == 1:
                    sp.wait_ge(tail_kept, CT)
                    sp.dma_start(io["conv_p"], ctail[:]).then_inc(store_p, 16)
                    sp.wait_ge(v_ready, 2 * CT)
                    sp.dma_start(io["conv_s"], VS[:]).then_inc(store_s, 16)
            sp.dma_start(W1[:], io["w1"]).then_inc(w1_in, 16)
            for name, tile in (("slopes", slopes), ("dist", dist), ("pe", pe_in), ("w2", W2), ("headsel", headsel), ("rowsel", rowsel)):
                sp.dma_start(tile[:], io[name]).then_inc(small_in, 16)
            sp.wait_ge(store_s, 16)
            sp.wait_ge(pool_step, 7 * CT)
            for n in range(3):
                sp.dma_start(ringE[:, n], io["w_f"][n]).then_inc(wE_in[n], 16)
            sp.dma_start(wtok[:], io["w_t"]).then_inc(wtok_in, 16)
            sp.wait_ge(c_gated, CT)
            sp.wait_ge(pages_in, 16)
            for i in range(SEQS * NPG):
                page = sp.value_load(pages[0:1, i:i + 1], min_val=0, max_val=io["cache_cmp"].shape[0] - 1)
                q, pg = divmod(i, NPG)
                for kv in range(2):
                    sp.dma_start(cache_cmp[:, kv, q::SEQS, pg * SEL:(pg + 1) * SEL],
                                 io["cache_cmp"][bass.ds(page, 1), :, kv].rearrange("o p g t -> (o p) g t")).then_inc(cmp_in, 16)
            for n in range(3, FT):
                sp.wait_ge(f_done, n - 2)
                sp.dma_start(ringE[:, n % 3], io["w_f"][n]).then_inc(wE_in[n % 3], 16)
                if n == FT_KV + 1:
                    sp.wait_ge(kv_kept, FT_KV)
                    sp.wait_ge(v_kept, 5)
                    sp.dma_start(io["kv_cmp"], KK[:]).then_inc(kk_stored, 16)
                    sp.dma_start(io["kv_cmp_s"], KN[:]).then_inc(stored, 16)
                    sp.dma_start(io["k_new"], KTm[:]).then_inc(stored, 16)
                    sp.dma_start(io["v_new"][:, 0:4], V[:, 0:4, 0:2 * GROUPS * HD]).then_inc(stored, 16)
                    sp.dma_start(io["v_new"][0:NS_, 4], V[0:NS_, 4, 0:2 * GROUPS * HD]).then_inc(stored, 16)
                    sp.wait_ge(hid_done, 2)
                    sp.dma_start(cbias[:], io["cbias"]).then_inc(cbias_in, 16)
                    for i in range(SEQS * NPG):
                        page = sp.value_load(pages[0:1, i:i + 1], min_val=0, max_val=io["cache_sel"].shape[0] - 1)
                        sp.dma_start(cache_sel[:, i // NPG, i % NPG, :],
                                     io["cache_sel"][bass.ds(page, 1)].rearrange("o p n -> (o p) n")).then_inc(sel_in, 16)
            sp.wait_ge(f_done, FT)
            for n in range(2):
                sp.dma_start(ringE[:, n], io["w_o"][n]).then_inc(wO_in[n], 16)
            sp.wait_ge(cs_step, 9 * 4)
            sp.dma_start(cache_win[:], io["cache_win"]).then_inc(win_in, 16)
            sp.wait_ge(comp_done, 1)
            sp.dma_start(sbias[:], io["sbias"]).then_inc(sbias_in, 16)
            sp.dma_start(io["win_s"], io["win_state"]).then_inc(stored, 16)
            for n in range(2, KT):
                sp.wait_ge(out2_done, n - 1)
                sp.dma_start(ringE[:, n % 2], io["w_o"][n]).then_inc(wO_in[n % 2], 16)
            for k in range(KT):
                sp.wait_ge(y_ready, k + 1)
                sp.dma_start(io["y"][:, k], Y[:, k]).then_inc(stored, 16)
            sp.wait_ge(stored, 16 * (5 + KT))
            sp.wait_ge(store_p, 16)

        @block.tensor
        def _(pe):
            def sum_squares(n):
                for k in range(KT):
                    pe.wait_ge(squared, n * KT + k + 1)
                    for dst, cols in halves(3):
                        mm = nc.tensor.matmul(dst, ones[:], sq[:, k % 2, cols], start=(k == 0), stop=(k == KT - 1))
                    mm.then_inc(sq_summed, 1)

            pe.wait_ge(ones_set, 1)
            sum_squares(0)

            def project(par, j, pair, done):
                for k in range(KT):
                    for dst, cols in halves(pair):
                        mm = nc.tensor.matmul(dst, ringA[:, par, j, k, :], H[:, k, cols],
                                              start=(k == 0), stop=(k == KT - 1))
                mm.then_inc(done, 1)

            def add_to_mean(c, first, last):
                pe.wait_ge(conv_step, 32 * c + 32)
                pe.wait_ge(pool_step, 7 * c + 7)
                for dst, cols in halves(3):
                    rhs = C[:, c, cols]
                    mm = nc.tensor.matmul(dst, ones[:], rhs, start=first, stop=last)
                mm.then_inc(c_summed, 1)

            def tile(c, par, turn):
                pe.wait_ge(wA_in[par], 16 * (turn + 1))
                if reaches(c, 1):
                    pe.wait_ge(sig_ready, c)
                project(par, 0, 0, gate_done)
                if reaches(c, 1):
                    pe.wait_ge(v_ready, 2 * c)
                project(par, 1, 1, lin_done)
                if reaches(c, 1):
                    pe.wait_ge(z_kept, c)
                project(par, 2, 2, z_done)

            pe.wait_ge(h_ready, KT)
            tile(0, 0, 0)
            tile(1, 1, 0)
            add_to_mean(0, True, False)
            tile(2, 0, 1)
            add_to_mean(1, False, False)
            tile(3, 1, 1)
            with pe.Fori(2, CT // 2) as j:
                add_to_mean(2 * j - 2, False, False)
                tile(2 * j, 0, j)
                add_to_mean(2 * j - 1, False, False)
                tile(2 * j + 1, 1, j)
            add_to_mean(CT - 2, False, False)
            add_to_mean(CT - 1, False, True)

            for c in range(CT):
                pe.wait_ge(squared, KT + c + 1)
                if c == 0:
                    pe.wait_ge(sig_ready, CT)
                for dst, cols in halves(0):
                    mm = nc.tensor.matmul(dst, ones[:], sq[:, c % 2, cols], start=(c == 0), stop=(c == CT - 1))
                mm.then_inc(sq_summed, 1)

            for n in range(KT):
                pe.wait_ge(wC_in[n % 2], 16 * (n // 2 + 1))
                if n >= 3:
                    pe.wait_ge(x_added, n - 2)
                for k in range(CT):
                    if n == 0:
                        pe.wait_ge(c_gated, k + 1)
                    for dst, cols in halves(1 + n % 3):
                        mm = nc.tensor.matmul(dst, ringC[:, n % 2, k, :], C[:, k, cols],
                                              start=(k == 0), stop=(k == CT - 1))
                mm.then_inc(out1_done, 1)

            pe.wait_ge(x_added, KT)
            for k in range(KT):
                pe.wait_ge(squared, KT + CT + k + 1)
                for dst, cols in halves(3):
                    mm = nc.tensor.matmul(dst, ones[:], sq[:, k % 2, cols], start=(k == 0), stop=(k == KT - 1))
                mm.then_inc(sq_summed, 1)
            pe.wait_ge(h2_ready, KT)

            def f_tile(n, pair):
                pe.wait_ge(wE_in[n % 3], 16 * (n // 3 + 1))
                for k in range(KT):
                    for dst, cols in halves(pair):
                        mm = nc.tensor.matmul(dst, ringE[:, n % 3, k, :], H[:, k, cols],
                                              start=(k == 0), stop=(k == KT - 1))
                mm.then_inc(f_done, 1)

            for n in range(FT_KV):
                if n >= 4:
                    pe.wait_ge(kv_kept, n - 3)
                f_tile(n, n % 4)
            pe.wait_ge(wtok_in, 16)
            for i in range(5):
                if i < 4:
                    pe.wait_ge(kv_kept, 5 + i)
                else:
                    pe.wait_ge(v_kept, 1)
                rows = min(P, T - i * P)
                for k in range(KT):
                    for b in range(2):
                        mm = nc.tensor.matmul(ps[0:rows, 2 * (i % 4) + b, 0:VH], H[:, k, i * P:i * P + rows],
                                              wtok[:, k, b * VH:(b + 1) * VH], start=(k == 0), stop=(k == KT - 1))
                mm.then_inc(tok_done, 1)
            pe.wait_ge(v_kept, 5)
            pe.wait_ge(small_in, 96)
            for sg in range(2):
                mm = nc.tensor.matmul(ps[:, 2 + sg, 0:GL], rowsel[:, sg, :], V[0:NS_, 4, 2 * GROUPS * HD:VTOK],
                                      start=True, stop=True)
            mm.then_inc(grow_done, 1)
            pe.wait_ge(w1_in, 16)
            pe.wait_ge(cmp_in, 32 * SEQS * NPG)
            for kv in range(2):
                for m in range(CBLK // 2):
                    w, first, last = W1[:, kv, m, :], m == 0, m == CBLK // 2 - 1
                    nc.tensor.matmul(ps[:, kv, 0:GROUPS * NCP], w, KK[:, kv, :, m:m + 8 * (NCP - 1) + 1:8],
                                     start=first, stop=last)
                    nc.tensor.matmul(ps[:, 4 + kv, 0:SEQS * GROUPS * NCS], w,
                                     cache_cmp[:, kv, :, m:m + 8 * (NCS - 1) + 1:8], start=first, stop=last)
                    mm = nc.tensor.matmul(ps[:, 6 + kv, 0:1], w, pe_in[:, kv, m:m + 1], start=first, stop=last)
                mm.then_inc(hid_done, 1)

            def q_or_z(n):
                i = n - FT_KV
                if i < FT_Q:
                    if i == 0:
                        pe.wait_ge(grow_kept, 2)
                    if i == 1:
                        pe.wait_ge(pe_kept, 1)
                    if i >= 2:
                        pe.wait_ge(q_kept, i - 1)
                    f_tile(n, 3 if i % 2 else 1)
                else:
                    i -= FT_Q
                    if i < 2:
                        pe.wait_ge(comp_kept, 4)
                        pe.wait_ge(q_kept, FT_Q)
                    else:
                        pe.wait_ge(zt_ready, i - 1)
                    f_tile(n, i % 2)

            q_or_z(FT_KV)
            q_or_z(FT_KV + 1)
            pe.wait_ge(hid_ready, 4)
            pe.wait_ge(pads2_set, 1)
            for g in range(GROUPS):
                rows = slice(HD * (g % 2), HD * (g % 2) + HD)
                nc.tensor.matmul(ps[rows, 0, 32 * (g // 2):32 * (g // 2) + 32], W2[:, 0, :], hp[:, 0, g, :],
                                 start=True, stop=True)
                nc.tensor.matmul(ps[rows, 1, P * (g // 2):P * (g // 2) + P], W2[:, 0, :], hs[:, 0, g],
                                 start=True, stop=True)
                for j in range(HPG):
                    nc.tensor.matmul(ps[32 * j:32 * j + 32, 4, HD * g:HD * g + HD], hp[:, 1, g, :], W2[:, 1, :],
                                     start=True, stop=True)
                mm = nc.tensor.matmul(ps[:, 5, HD * g:HD * g + HD], hs[:, 1, g], W2[:, 1, :],
                                      start=True, stop=True)
            mm.then_inc(comp_done, 1)
            for i in range(2, FT_Q):
                q_or_z(FT_KV + i)
            pe.wait_ge(q_kept, FT_Q)
            pe.wait_ge(comp_kept, 4)
            for t in range(4):
                if t >= 1:
                    pe.wait_ge(cs_step, 9 * t - 8)
                for h in range(HEADS):
                    g, j = divmod(h, HPG)
                    rows = slice(HD * (g % 2), HD * (g % 2) + HD)
                    col = P * (g // 2) + 32 * j
                    mm = nc.tensor.matmul(ps[:, 4 + g % 2, col:col + 32], QT[rows, HPG * (g // 2) + j, t * P:(t + 1) * P],
                                          kcp[rows, g // 2, :], start=True, stop=True)
                mm.then_inc(cs_done, 1)
                q_or_z(FT_KV + FT_Q + 2 * t)
                pe.wait_ge(cs_step, 9 * t + 9)
                if t >= 1:
                    pe.wait_ge(o_set, t)
                for g in range(GROUPS):
                    mm = nc.tensor.transpose(ps[:, 6, P * g:P * g + P], S[:, 0, P * g:P * g + P], ident[:])
                mm.then_inc(cs_t, 1)
                q_or_z(FT_KV + FT_Q + 2 * t + 1)
                pe.wait_ge(cs_pt, t + 1)
                for g in range(GROUPS):
                    mm = nc.tensor.matmul(ps[:, 6 + g // 2, 256 * (g % 2):256 * (g % 2) + 256], PT[:, 0, P * g:P * g + P],
                                          vcd[:, g, :], start=True, stop=True)
                mm.then_inc(cs_pv, 1)

            pe.wait_ge(zt_ready, FT_Z)
            pe.wait_ge(o_set, 4)

            def qk(i, u, gp):
                r, t, b = u // 8, u % 8 // 2, u % 2
                rows, n = slice(HD * r, HD * r + HD), (t + 1) * P
                if u % 8 == 0:
                    pe.wait_ge(qb_set, 2 * i + r + 1)
                if u >= 4 or reaches(i, 1):
                    pe.wait_ge(sc_ready, 16 * i + u - 3)
                nc.tensor.matmul(ps[:, u % 4, 0:n], qb[rows, t * P:(t + 1) * P], KTm[rows, b, gp, 0:n],
                                 start=True, stop=True).then_inc(qk_done, 1)

            def transpose(i, u):
                t = u % 8 // 2
                pe.wait_ge(exp_ready, 16 * i + u + 1)
                if u >= 2 or reaches(i, 1):
                    pe.wait_ge(pt_odd if u % 2 else pt_even, 8 * i + u // 2)
                for k in range(t + 1):
                    mm = nc.tensor.transpose(ps[:, 4 + u % 2, P * k:P * k + P], S[:, u % 4, P * k:P * k + P], ident[:])
                mm.then_inc(t_done, 1)

            def pv(i, u, gp):
                r, t, b = u // 8, u % 8 // 2, u % 2
                pe.wait_ge(pt_odd if b else pt_even, 8 * i + u // 2 + 1)
                if u % 8 == 0 and reaches(i, 1):
                    pe.wait_ge(o_step, 10 * i + 5 * r - 7)
                v = b * GROUPS * HD + (2 * gp + r) * HD
                for k in range(t + 1):
                    mm = nc.tensor.matmul(ps[:, 6 + r, HD * (u % 8):HD * (u % 8) + HD], PT[:, b, P * k:P * k + P],
                                          V[:, k, v:v + HD], start=(k == 0), stop=(k == t))
                mm.then_inc(pv_done, 1)

            def attend(i, gp, last_gp):
                for u in range(16):
                    qk(i, u, gp)
                    if u >= 3:
                        transpose(i, u - 3)
                    elif reaches(i, 1):
                        transpose(i - 1, u + 13)
                    if u >= 4:
                        pv(i, u - 4, gp)
                    elif reaches(i, 1):
                        pv(i - 1, u + 12, last_gp)

            attend(0, 0, 0)
            with pe.Fori(1, 4) as i:
                attend(i, 0, 0)
            attend(4, 1, 0)
            with pe.Fori(5, 8) as i:
                attend(i, 1, 1)
            for u in range(13, 16):
                pv(7, u - 1, 1)
                transpose(7, u)
            pv(7, 15, 1)

            pe.wait_ge(qblk_ready, 1)
            pe.wait_ge(sel_in, 16 * SEQS * NPG)
            pe.wait_ge(win_in, 16)

            def sample_scores(v):
                (gp, sg), br = divmod(v // 3, 2), v % 3
                if v < 4:
                    pe.wait_ge(sc_ready, 16 * 8)
                else:
                    pe.wait_ge(ss_ready, v - 3)
                for q in range(4):
                    s_ = 4 * sg + q
                    rows = slice(32 * q, 32 * q + 32)
                    if br == 0:
                        mm = nc.tensor.matmul(ps[rows, v % 4, 0:P], qblk[:, s_, gp, :], kcs[:, gp, :], start=True, stop=True)
                        continue
                    keys = (cache_sel[:, s_, :, gp * P:gp * P + P] if br == 1
                            else cache_win[:, s_, gp * PAST:(gp + 1) * PAST])
                    nc.tensor.matmul(ps[rows, v % 4, 0:PAST], qblk[:, s_, gp, :], keys, start=True, stop=True)
                    mm = nc.tensor.matmul(ps[rows, v % 4, PAST:NKEY], qblk[:, s_, gp, :], KTm[:, br - 1, gp, NP_:T],
                                          start=True, stop=True)
                mm.then_inc(ss_done, 1)

            def sample_transpose(v):
                br = v % 3
                pe.wait_ge(ss_step, 3 * v + 3)
                if v < 2:
                    pe.wait_ge(pt_odd, 64)
                    pe.wait_ge(pt_even, 64)
                else:
                    pe.wait_ge(ss_pt, v - 1)
                for k in range(1 if br == 0 else 2):
                    mm = nc.tensor.transpose(ps[:, 4 + v % 2, P * k:P * k + P], S[:, v % 4, P * k:P * k + P], ident[:])
                if br:
                    mm = nc.tensor.transpose(ps[0:NS_, 4 + v % 2, PAST:PAST + P], S[:, v % 4, PAST:NKEY], ident[:])
                mm.then_inc(ss_t, 1)

            def sample_pv(v):
                (gp, sg), br = divmod(v // 3, 2), v % 3
                bank = 6 + v // 3 % 2
                pe.wait_ge(ss_pt, v + 1)
                if br == 0 and v < 6:
                    pe.wait_ge(o_step, 80)
                elif br == 0:
                    pe.wait_ge(og_sample, v // 3 - 1)
                if br == 0:
                    mm = nc.tensor.matmul(ps[:, bank, 0:P], vcs[:, gp * P:(gp + 1) * P], PT[:, v % 2, 0:P],
                                          start=True, stop=False)
                else:
                    for q in range(4):
                        s_ = 4 * sg + q
                        for c in range(2):
                            vals = (cache_sel[:, s_, c, PAST + gp * P:PAST + gp * P + P] if br == 1
                                    else cache_win[:, s_, (2 + c) * PAST + gp * P:(2 + c) * PAST + gp * P + P])
                            nc.tensor.matmul(ps[:, bank, 32 * q:32 * q + 32], vals,
                                             PT[:, v % 2, P * c + 32 * q:P * c + 32 * q + 32], start=False, stop=False)
                    vnew = (br - 1) * GROUPS * HD + gp * P
                    mm = nc.tensor.matmul(ps[:, bank, 0:P], V[0:NS_, 4, vnew:vnew + P], PT[0:NS_, v % 2, PAST:PAST + P],
                                          start=False, stop=(br == 2))
                mm.then_inc(ss_pv, 1)

            for v in range(12 + 3):
                if v < 12:
                    sample_scores(v)
                if 2 <= v < 14:
                    sample_transpose(v - 2)
                if v >= 3:
                    sample_pv(v - 3)

            for k in range(KT):
                if k >= 4:
                    pe.wait_ge(og, k - 3)
                else:
                    pe.wait_ge(ss_ready, 12)
                for t in range(4):
                    mm = nc.tensor.transpose(ps[:, k % 4, P * t:P * t + P], O[:, t, P * k:P * k + P], ident[:])
                mm.then_inc(o_t, 1)
            for n in range(KT):
                pair = 2 + n % 2
                pe.wait_ge(wO_in[n % 2], 16 * (n // 2 + 1))
                if n == 0:
                    pe.wait_ge(og_sample, 4)
                if n >= 2:
                    pe.wait_ge(x2_added, n - 1)
                for k in range(KT):
                    if n == 0:
                        pe.wait_ge(og, k + 1)
                    for dst, cols in halves(pair):
                        mm = nc.tensor.matmul(dst, ringE[:, n % 2, k, :], ZT[:, k, cols],
                                              start=(k == 0), stop=(k == KT - 1))
                mm.then_inc(out2_done, 1)
            for k in range(KT):
                pe.wait_ge(squared, 2 * KT + CT + k + 1)
                for dst, cols in halves(0):
                    mm = nc.tensor.matmul(dst, ones[:], sq[:, k % 2, cols], start=(k == 0), stop=(k == KT - 1))
                mm.then_inc(sq_summed, 1)

        @block.scalar
        def _(act):
            act.wait_ge(x_in, 16)
            for k in range(KT):
                if k >= 2:
                    act.wait_ge(sq_summed, k - 1)
                nc.scalar.activation(sq[:, k % 2, :], X[:, k, :], ACT.Square).then_inc(squared, 1)
            act.wait_ge(inv_var, 1)
            nc.scalar.activation(rstd[:], rstd[:], ACT.Sqrt).then_inc(rstd_ready, 1)

            def tile(c, par):
                act.wait_ge(gate_done, c + 1)
                if reaches(c, 2):
                    act.wait_ge(v_ready, 2 * c - 2)
                nc.scalar.activation(sig[:, par, 0:NP_].rearrange("p (b t) -> p b t", b=2), prompt_of(0), ACT.Sigmoid)
                nc.scalar.activation(sig[:, par, NP_:T], sample_of(0), ACT.Sigmoid).then_inc(sig_ready, 1)
                act.wait_ge(v_ready, 2 * c + 2)
                nc.scalar.activation(ctail[:, c, :], VP[:, par, NP_:NP_ + STATE], ACT.Copy).then_inc(tail_kept, 1)
                act.wait_ge(z_done, c + 1)
                nc.scalar.activation(Z1[:, c, 0:NP_].rearrange("p (b t) -> p b t", b=2), prompt_of(2), ACT.Copy)
                nc.scalar.activation(Z1[:, c, NP_:T], sample_of(2), ACT.Copy).then_inc(z_kept, 1)

            tile(0, 0)
            tile(1, 1)
            with act.Fori(1, CT // 2) as j:
                tile(2 * j, 0)
                tile(2 * j + 1, 1)

            act.wait_ge(z_kept, CT)
            for c in range(CT):
                act.wait_ge(centered, c + 1)
                if c >= 2:
                    act.wait_ge(sq_summed, KT + c - 1)
                nc.scalar.activation(sq[:, c % 2, :], C[:, c, :], ACT.Square).then_inc(squared, 1)
            act.wait_ge(inv_var, 2)
            nc.scalar.activation(rstd[:], rstd[:], ACT.Sqrt).then_inc(rstd_ready, 1)
            act.wait_ge(consts_in, 48)
            for c in range(CT):
                nc.scalar.activation(Z1[:, c, :], Z1[:, c, :], ACT.Silu).then_inc(z_act, 1)
                act.wait_ge(scaled, c + 1)
                nc.scalar.activation(C[:, c, :], C[:, c, :], ACT.Silu, scale=lng[:, c:c + 1],
                                     bias=lnb[:, c:c + 1]).then_inc(activated, 1)

            def square_x(added, done):
                for k in range(KT):
                    act.wait_ge(added, k + 1)
                    act.wait_ge(sq_summed, done + k - 1)
                    nc.scalar.activation(sq[:, k % 2, :], X[:, k, :], ACT.Square).then_inc(squared, 1)

            square_x(x_added, KT + CT)
            act.wait_ge(inv_var, 3)
            nc.scalar.activation(rstd[:], rstd[:], ACT.Sqrt).then_inc(rstd_ready, 1)
            for i in range(5):
                rows = min(P, T - i * P)
                act.wait_ge(tok_done, i + 1)
                nc.scalar.activation(V[0:rows, i, :].rearrange("p (b n) -> p b n", b=2),
                                     ps[0:rows, 2 * (i % 4):2 * (i % 4) + 2, 0:VH], ACT.Copy).then_inc(v_kept, 1)
            act.wait_ge(v_kept, 5)
            nc.scalar.activation(gates[:].rearrange("p t h b -> p t (h b)"), V[:, 0:4, 2 * GROUPS * HD:VTOK],
                                 ACT.Sigmoid).then_inc(gates_ready, 1)
            act.wait_ge(grow_kept, 3)
            nc.scalar.activation(grow[:], grow[:], ACT.Sigmoid).then_inc(grow_ready, 1)
            act.wait_ge(hid_done, 2)
            act.wait_ge(pe_kept, 1)
            for kv in range(2):
                nc.scalar.activation(hp[:, kv, :, 0:NCP],
                                     ps[:, kv, 0:GROUPS * NCP].rearrange("p (g c) -> p g c", g=GROUPS),
                                     ACT.Silu, bias=pe_hid[:, kv:kv + 1]).then_inc(hid_ready, 1)
                nc.scalar.activation(hs[:, kv].rearrange("p g (s c) -> p (g s) c", c=16)[:, :, 0:NCS],
                                     ps[:, 4 + kv, 0:SEQS * GROUPS * NCS].rearrange("p (g c) -> p g c", c=NCS),
                                     ACT.Silu, bias=pe_hid[:, kv:kv + 1]).then_inc(hid_ready, 1)
            for i in range(FT_Q):
                pair = 3 if i % 2 else 1
                act.wait_ge(f_done, FT_KV + i + 1)
                nc.scalar.activation(split(QT[:, i, 0:NP_]), prompt_of(pair), ACT.Copy, scale=HD ** -0.5)
                nc.scalar.activation(QT[:, i, NP_:T], sample_of(pair), ACT.Copy, scale=HD ** -0.5).then_inc(q_kept, 1)

            def z_tile(i):
                act.wait_ge(f_done, FT_KV + FT_Q + i + 1)
                nc.scalar.activation(split(ZT[:, i, 0:NP_]), prompt_of(i % 2), ACT.Silu)
                nc.scalar.activation(ZT[:, i, NP_:T], sample_of(i % 2), ACT.Silu).then_inc(zt_ready, 1)

            for t in range(4):
                act.wait_ge(cs_step, 9 * t + 4)
                nc.scalar.activation(S[:, 0, :], S[:, 0, :], ACT.Exp).then_inc(cs_exp, 1)
                z_tile(2 * t)
                z_tile(2 * t + 1)
                act.wait_ge(cs_pv, t + 1)
                nc.scalar.activation(split(O[:, t, :]), ps[:, 6:8, :], ACT.Copy).then_inc(o_set, 1)

            def exp(i, u):
                n = (u % 8 // 2 + 1) * P
                act.wait_ge(sc_ready, 16 * i + u + 1)
                nc.scalar.activation(S[:, u % 4, 0:n], S[:, u % 4, 0:n], ACT.Exp, scale=-1.0, bias=nmax[:, u:u + 1],
                                     accum_out=rsum[:, u:u + 1]).then_inc(exp_ready, 1)

            def copy_even(i, u):
                n = (u % 8 // 2 + 1) * P
                act.wait_ge(t_done, 16 * i + u + 1)
                if u >= 2 or reaches(i, 1):
                    act.wait_ge(pv_done, 16 * i + u - 1)
                nc.scalar.activation(PT[:, 0, 0:n], ps[:, 4, 0:n], ACT.Copy).then_inc(pt_even, 1)

            def attend(i):
                for u in range(16):
                    if u == 0 and reaches(i, 1):
                        act.wait_ge(o_step, 10 * i - 9)
                    if u == 8 and reaches(i, 1):
                        act.wait_ge(o_step, 10 * i - 4)
                    exp(i, u)
                    if u >= 3 and (u - 3) % 2 == 0:
                        copy_even(i, u - 3)
                    if u < 3 and (u + 13) % 2 == 0 and reaches(i, 1):
                        copy_even(i - 1, u + 13)

            attend(0)
            with act.Fori(1, 8) as i:
                attend(i)
            copy_even(7, 14)

            act.wait_ge(o_step, 80)
            for v in range(12):
                n = P if v % 3 == 0 else NKEY
                act.wait_ge(ss_ready, v + 1)
                nc.scalar.activation(S[:, v % 4, 0:n], S[:, v % 4, 0:n], ACT.Exp, scale=-1.0, bias=nmax[:, v:v + 1],
                                     accum_out=rsum[:, v:v + 1]).then_inc(ss_exp, 1)
            square_x(x2_added, 2 * KT + CT)
            act.wait_ge(inv_var, 4)
            nc.scalar.activation(rstd[:], rstd[:], ACT.Sqrt).then_inc(rstd_ready, 1)

        @block.vector
        def _(dve):
            nc.vector.memset(ones[:], 1.0).then_inc(ones_set, 1)
            nc.vector.memset(VP[:, :, 0:STATE], 0.0).then_inc(pads_set, 1)

            def inverse_variance(pair, count, n):
                nc.vector.tensor_scalar(rstd[:, 0:NP_].rearrange("p (b t) -> p b t", b=2), prompt_of(pair),
                                        1.0 / count, EPS, ALU.mult, ALU.add)
                nc.vector.tensor_scalar(rstd[:, NP_:T], sample_of(pair), 1.0 / count, EPS,
                                        ALU.mult, ALU.add).then_inc(mean_sq, 1)
                dve.wait_ge(mean_sq, n)
                nc.vector.reciprocal(rstd[:], rstd[:]).then_inc(inv_var, 1)

            dve.wait_ge(sq_summed, KT)
            inverse_variance(3, D, 1)
            dve.wait_ge(rstd_ready, 1)
            dve.wait_ge(gains_in, 16)
            for k in range(KT):
                nc.vector.scalar_tensor_tensor(H[:, k, :], X[:, k, :], gains[:, 0, k:k + 1], rstd[:],
                                               ALU.mult, ALU.mult).then_inc(h_ready, 1)
            dve.wait_ge(taps_in, 16)
            dve.wait_ge(state_in, 16)
            dve.wait_ge(pads_set, 1)

            def tile(c, par):
                if reaches(c, 2):
                    dve.wait_ge(pool_step, 7 * c - 7)
                nc.vector.tensor_copy(tapc[:, par, :], taps[:, c, :]).then_inc(tap_set, 1)
                dve.wait_ge(sig_ready, c + 1)
                dve.wait_ge(lin_done, c + 1)
                if reaches(c, 2):
                    dve.wait_ge(tail_kept, c - 1)
                nc.vector.tensor_tensor(VP[:, par, STATE:].rearrange("p (b t) -> p b t", b=2), prompt_of(1),
                                        sig[:, par, 0:NP_].rearrange("p (b t) -> p b t", b=2),
                                        ALU.mult).then_inc(v_ready, 1)
                nc.vector.tensor_tensor(VS[:, c, :, STATE:], sample_of(1).rearrange("p (s t) -> p s t", s=SEQS),
                                        sig[:, par, NP_:T].rearrange("p (s t) -> p s t", s=SEQS),
                                        ALU.mult).then_inc(v_ready, 1)
                dve.wait_ge(tap_set, c + 1)
                dve.wait_ge(v_ready, 2 * c + 1)
                for k in range(TAPS):
                    src, w = VP[:, par, k:k + NP_], tapc[:, par, k:k + 1]
                    if k == 0:
                        op = nc.vector.tensor_scalar(acc[:, 0, :], src, w, tapc[:, par, TAPS:TAPS + 1], ALU.mult, ALU.add)
                    elif k == 1:
                        op = nc.vector.tensor_scalar(acc[:, 1, :], src, w, None, ALU.mult)
                    else:
                        dve.wait_ge(conv_step, 32 * c + k - 1)
                        op = nc.vector.scalar_tensor_tensor(acc[:, k % 2, :], src, w, acc[:, k % 2, :], ALU.mult, ALU.add)
                    op.then_inc(conv_step, 1)
                dve.wait_ge(conv_step, 32 * c + TAPS)
                nc.vector.tensor_tensor(C[:, c, 0:NP_], acc[:, 0, :], acc[:, 1, :], ALU.add).then_inc(conv_step, 1)
                dve.wait_ge(conv_step, 32 * c + 32)

            tile(0, 0)
            tile(1, 1)
            with dve.Fori(1, CT // 2) as j:
                tile(2 * j, 0)
                tile(2 * j + 1, 1)

            dve.wait_ge(c_summed, CT)
            nc.vector.tensor_scalar(mean[:, 0:NP_].rearrange("p (b t) -> p b t", b=2), prompt_of(3),
                                    1.0 / DC, None, ALU.mult)
            nc.vector.tensor_scalar(mean[:, NP_:T], sample_of(3), 1.0 / DC, None, ALU.mult).then_inc(mean_ready, 1)
            dve.wait_ge(mean_ready, 1)
            dve.wait_ge(pool_step, 7 * CT)
            for c in range(CT):
                nc.vector.tensor_tensor(C[:, c, :], C[:, c, :], mean[:], ALU.subtract).then_inc(centered, 1)
            dve.wait_ge(sq_summed, KT + CT)
            inverse_variance(0, DC, 2)
            dve.wait_ge(rstd_ready, 2)
            dve.wait_ge(squared, KT + CT)

            def scale(c):
                nc.vector.tensor_tensor(C[:, c, :], C[:, c, :], rstd[:], ALU.mult).then_inc(scaled, 1)

            scale(0)
            scale(1)
            for c in range(CT):
                if c + 2 < CT:
                    scale(c + 2)
                dve.wait_ge(activated, c + 1)
                dve.wait_ge(z_act, c + 1)
                nc.vector.tensor_tensor(C[:, c, :], C[:, c, :], Z1[:, c, :], ALU.mult).then_inc(c_gated, 1)
            for n in range(KT):
                dve.wait_ge(out1_done, n + 1)
                nc.vector.tensor_tensor(X[:, n, 0:NP_].rearrange("p (b t) -> p b t", b=2), prompt_of(1 + n % 3),
                                        X[:, n, 0:NP_].rearrange("p (b t) -> p b t", b=2), ALU.add)
                nc.vector.tensor_tensor(X[:, n, NP_:T], sample_of(1 + n % 3), X[:, n, NP_:T],
                                        ALU.add).then_inc(x_added, 1)

            dve.wait_ge(sq_summed, 2 * KT + CT)
            inverse_variance(3, D, 3)
            dve.wait_ge(rstd_ready, 3)
            dve.wait_ge(x_added, KT)
            for k in range(KT):
                nc.vector.scalar_tensor_tensor(H[:, k, :], X[:, k, :], gains[:, 1, k:k + 1], rstd[:],
                                               ALU.mult, ALU.mult).then_inc(h2_ready, 1)
            for n in range(FT_KV):
                dve.wait_ge(f_done, n + 1)
                if n < 4:
                    kv, gp = divmod(n, 2)
                    for r in range(2):
                        for par in range(2):
                            nc.vector.tensor_copy(split(KK[HD * par:HD * par + HD, kv, 2 * gp + r, :]),
                                                  ps[HD * r:HD * r + HD, 2 * n:2 * n + 2, par:TA:2])
                    nc.vector.tensor_copy(KN[:, n, :], sample_of(n)).then_inc(kv_kept, 1)
                else:
                    b, gp = divmod(n - 4, 2)
                    nc.vector.tensor_copy(split(KTm[:, b, gp, 0:NP_]), prompt_of(n % 4))
                    nc.vector.tensor_copy(KTm[:, b, gp, NP_:T], sample_of(n % 4)).then_inc(kv_kept, 1)
            dve.wait_ge(small_in, 96)
            dve.wait_ge(grow_done, 1)
            for sg in range(2):
                nc.vector.tensor_tensor(gtmp[:, sg], ps[:, 2 + sg:3 + sg, 0:GL].to_broadcast([P, 2, GL]), headsel[:],
                                        ALU.mult).then_inc(grow_kept, 1)
            dve.wait_ge(grow_kept, 2)
            nc.vector.tensor_reduce(grow[:].rearrange("p a g b -> p (a g) b"),
                                    gtmp[:].rearrange("p a g (h b) -> p (a g) b h", b=3), AX.X, ALU.add).then_inc(grow_kept, 1)
            dve.wait_ge(hid_done, 2)
            nc.vector.tensor_copy(pe_hid[:], ps[:, 6:8, 0]).then_inc(pe_kept, 1)
            dve.wait_ge(comp_done, 1)
            dve.wait_ge(zeros_set, 1)
            nc.vector.tensor_copy(kcp[:], ps[:, 0, 0:64].rearrange("p (g c) -> p g c", g=2)).then_inc(comp_kept, 1)
            nc.vector.tensor_copy(kcs[:], ps[:, 1, 0:2 * P].rearrange("p (g c) -> p g c", g=2)).then_inc(comp_kept, 1)
            for j in range(HPG):
                rows = slice(32 * j, 32 * j + 32)
                op = nc.vector.tensor_copy(vcd[rows, :, HD * j:HD * j + HD],
                                           ps[rows, 4, 0:GROUPS * HD].rearrange("p (g d) -> p g d", g=GROUPS))
            op.then_inc(comp_kept, 1)
            nc.vector.tensor_copy(vcs[:], ps[:, 5, 0:GROUPS * HD]).then_inc(comp_kept, 1)
            dve.wait_ge(q_kept, FT_Q)
            for gp in range(2):
                for r in range(2):
                    rows = slice(HD * r, HD * r + HD)
                    for j in range(HPG):
                        op = nc.vector.tensor_copy(qblk[rows, :, gp, 16 * r + 4 * j:16 * r + 4 * j + 4],
                                                   QT[rows, HPG * gp + j, NP_:T].rearrange("p (s t) -> p s t", s=SEQS))
            op.then_inc(qblk_ready, 1)

            dve.wait_ge(kk_stored, 16)
            dve.wait_ge(cbias_in, 16)
            dve.wait_ge(gates_ready, 1)
            Sh = S[:, 0, :].rearrange("p (h c) -> p h c", h=HEADS)
            for t in range(4):
                dve.wait_ge(cs_done, t + 1)
                if t >= 1:
                    dve.wait_ge(cs_t, t)
                nc.vector.tensor_tensor(S[:, 0, :].rearrange("p (a r c) -> p a r c", a=2, r=2),
                                        ps[:, 4:6, 0:2 * P].rearrange("p r (a c) -> p a r c", a=2),
                                        cbias[:, t, :].rearrange("p (a r c) -> p a r c", a=2, r=2), ALU.add).then_inc(cs_step, 1)
                dve.wait_ge(cs_step, 9 * t + 1)
                nc.vector.tensor_reduce(m16[:], Sh, AX.X, ALU.max).then_inc(cs_step, 1)
                dve.wait_ge(cs_step, 9 * t + 2)
                nc.vector.tensor_scalar(m16[:], m16[:], FLOOR, None, ALU.max).then_inc(cs_step, 1)
                dve.wait_ge(cs_step, 9 * t + 3)
                nc.vector.tensor_tensor(Sh, Sh, m16[:].unsqueeze(2).to_broadcast([P, HEADS, 32]),
                                        ALU.subtract).then_inc(cs_step, 1)
                dve.wait_ge(cs_exp, t + 1)
                nc.vector.tensor_reduce(s16[:], Sh, AX.X, ALU.add).then_inc(cs_step, 1)
                dve.wait_ge(cs_step, 9 * t + 5)
                nc.vector.tensor_scalar(s16[:], s16[:], 1e-30, None, ALU.max).then_inc(cs_step, 1)
                dve.wait_ge(cs_step, 9 * t + 6)
                nc.vector.reciprocal(s16[:], s16[:]).then_inc(cs_step, 1)
                dve.wait_ge(cs_step, 9 * t + 7)
                nc.vector.tensor_tensor(s16[:], s16[:], gates[:, t, :, 0], ALU.mult).then_inc(cs_step, 1)
                dve.wait_ge(cs_step, 9 * t + 8)
                nc.vector.tensor_tensor(Sh, Sh, s16[:].unsqueeze(2).to_broadcast([P, HEADS, 32]),
                                        ALU.mult).then_inc(cs_step, 1)
                dve.wait_ge(cs_t, t + 1)
                if t >= 1:
                    dve.wait_ge(cs_pv, t)
                nc.vector.tensor_copy(PT[:, 0, :], ps[:, 6, :]).then_inc(cs_pt, 1)

            dve.wait_ge(o_set, 4)
            dve.wait_ge(cs_pv, 4)

            def score(i, u):
                r, t = u // 8, u % 8 // 2
                n = (t + 1) * P
                if u % 8 == 0:
                    dve.wait_ge(bias_set, 2 * i + r + 1)
                dve.wait_ge(qk_done, 16 * i + u + 1)
                if u >= 4 or reaches(i, 1):
                    dve.wait_ge(t_done, 16 * i + u - 3)
                nc.vector.memset(tick[:, u:u + 1], 0.0)
                nc.vector.tensor_tensor_reduce(S[:, u % 4, 0:n], ps[:, u % 4, 0:n], bias[:, r, NP_ - n:NP_], -1.0, 3e38,
                                               ALU.add, ALU.min, nmax[:, u:u + 1]).then_inc(sc_ready, 1)

            def copy_odd(i, u):
                n = (u % 8 // 2 + 1) * P
                dve.wait_ge(t_done, 16 * i + u + 1)
                if u >= 2 or reaches(i, 1):
                    dve.wait_ge(pv_done, 16 * i + u - 1)
                nc.vector.tensor_copy(PT[:, 1, 0:n], ps[:, 5, 0:n]).then_inc(pt_odd, 1)

            def add_head(i, r, gp):
                h, done = i + 4 * gp + 4 * r, 10 * i + 5 * r
                dve.wait_ge(pv_done, 16 * i + 8 * r + 8)
                nc.vector.reciprocal(gsc[:, r, :], rsum[:, 8 * r:8 * r + 8]).then_inc(o_step, 1)
                dve.wait_ge(o_step, done + 1)
                g8 = gsc[:, r, :].rearrange("p (t b) -> p t b", b=2)
                nc.vector.tensor_tensor(g8, g8, gates[:, :, h, 1:3], ALU.mult).then_inc(o_step, 1)
                dve.wait_ge(o_step, done + 2)
                nc.vector.tensor_tensor(otmp[:], ps[:, 6 + r, :].rearrange("p (u d) -> p u d", d=HD),
                                        gsc[:, r, :].unsqueeze(2).to_broadcast([P, 8, HD]), ALU.mult).then_inc(o_step, 1)
                dve.wait_ge(o_step, done + 3)
                oh = O[:, :, bass.ds(h * HD, HD)]
                nc.vector.tensor_tensor(oh, oh, otmp[:, 0:8:2, :], ALU.add).then_inc(o_step, 1)
                dve.wait_ge(o_step, done + 4)
                nc.vector.tensor_tensor(oh, oh, otmp[:, 1:8:2, :], ALU.add).then_inc(o_step, 1)

            def attend(i, gp, last_gp):
                for u in range(16):
                    score(i, u)
                    if u >= 3 and (u - 3) % 2:
                        copy_odd(i, u - 3)
                    if u < 3 and (u + 13) % 2 and reaches(i, 1):
                        copy_odd(i - 1, u + 13)
                    if u == 4 and reaches(i, 1):
                        add_head(i - 1, 1, last_gp)
                    if u == 12:
                        add_head(i, 0, gp)

            attend(0, 0, 0)
            with dve.Fori(1, 4) as i:
                attend(i, 0, 0)
            attend(4, 1, 0)
            with dve.Fori(5, 8) as i:
                attend(i, 1, 1)
            copy_odd(7, 13)
            copy_odd(7, 15)
            add_head(7, 1, 1)

            dve.wait_ge(sbias_in, 16)
            dve.wait_ge(grow_ready, 1)
            dve.wait_ge(t_done, 128)
            dve.wait_ge(o_step, 80)

            def sample_softmax_in(v):
                (gp, sg), br = divmod(v // 3, 2), v % 3
                n, at_ = (P, NKEY) if br == 0 else (NKEY, 0)
                dve.wait_ge(ss_done, v + 1)
                if v >= 4:
                    dve.wait_ge(ss_t, v - 3)
                nc.vector.tensor_tensor_reduce(S[:, v % 4, 0:n], ps[:, v % 4, 0:n], sbias[:, gp, sg, at_:at_ + n], -1.0, 3e38,
                                               ALU.add, ALU.min, nmax[:, v:v + 1]).then_inc(ss_ready, 1)

            def sample_softmax_out(v):
                (gp, sg), br = divmod(v // 3, 2), v % 3
                n = P if br == 0 else NKEY
                dve.wait_ge(ss_exp, v + 1)
                nc.vector.reciprocal(s16[:, v:v + 1], rsum[:, v:v + 1]).then_inc(ss_step, 1)
                dve.wait_ge(ss_step, 3 * v + 1)
                nc.vector.tensor_tensor(m16[:, v:v + 1], s16[:, v:v + 1], grow[:, sg, gp, br:br + 1], ALU.mult).then_inc(ss_step, 1)
                dve.wait_ge(ss_step, 3 * v + 2)
                nc.vector.tensor_scalar(S[:, v % 4, 0:n], S[:, v % 4, 0:n], m16[:, v:v + 1], None, ALU.mult).then_inc(ss_step, 1)

            def sample_copy(v):
                dve.wait_ge(ss_t, v + 1)
                if v >= 2:
                    dve.wait_ge(ss_pv, v - 1)
                if v % 3 == 0:
                    nc.vector.tensor_copy(PT[:, v % 2, 0:P], ps[:, 4 + v % 2, 0:P]).then_inc(ss_pt, 1)
                else:
                    nc.vector.tensor_copy(PT[:, v % 2, 0:PAST], ps[:, 4 + v % 2, 0:PAST])
                    nc.vector.tensor_copy(PT[0:NS_, v % 2, PAST:PAST + P], ps[0:NS_, 4 + v % 2, PAST:PAST + P]).then_inc(ss_pt, 1)

            def sample_gate(w):
                gp, sg = divmod(w, 2)
                dve.wait_ge(ss_pv, 3 * w + 3)
                for r in range(2):
                    o4 = ps[HD * r:HD * r + HD, 6 + w % 2, 0:P].rearrange("p (s r j t) -> p s r j t", s=4, r=2, j=HPG)
                    for jp in range(2):
                        for jj in range(2):
                            zt = ZT[HD * jp:HD * jp + HD, 2 * (2 * gp + r) + jj, NP_ + 16 * sg:NP_ + 16 * sg + 16]
                            zt = zt.rearrange("p (s t) -> p s t", s=4)
                            op = nc.vector.tensor_tensor(zt, o4[:, :, r, 2 * jj + jp, :], zt, ALU.mult)
                op.then_inc(og_sample, 1)

            for v in range(12 + 3):
                if v < 12:
                    sample_softmax_in(v)
                if 1 <= v < 13:
                    sample_softmax_out(v - 1)
                if 2 <= v < 14:
                    sample_copy(v - 2)
                if v >= 3 and (v - 3) % 3 == 2:
                    sample_gate((v - 3) // 3)

            for k in range(KT):
                dve.wait_ge(o_t, k + 1)
                nc.vector.tensor_tensor(ZT[:, k, 0:NP_], ps[:, k % 4, :], ZT[:, k, 0:NP_], ALU.mult).then_inc(og, 1)
            for n in range(KT):
                dve.wait_ge(out2_done, n + 1)
                nc.vector.tensor_tensor(split(X[:, n, 0:NP_]), prompt_of(2 + n % 2), split(X[:, n, 0:NP_]), ALU.add)
                nc.vector.tensor_tensor(X[:, n, NP_:T], sample_of(2 + n % 2), X[:, n, NP_:T], ALU.add).then_inc(x2_added, 1)
            dve.wait_ge(sq_summed, 3 * KT + CT)
            inverse_variance(0, D, 4)
            dve.wait_ge(rstd_ready, 4)
            dve.wait_ge(x2_added, KT)
            for k in range(KT):
                nc.vector.scalar_tensor_tensor(Y[:, k, :], X[:, k, :], gains[:, 2, k:k + 1], rstd[:],
                                               ALU.mult, ALU.mult).then_inc(y_ready, 1)

        @block.gpsimd
        def _(pool):
            def tile(c, par):
                pool.wait_ge(v_ready, 2 * c + 2)
                pool.wait_ge(tap_set, c + 1)
                if reaches(c, 1):
                    pool.wait_ge(pool_step, 7 * c)
                for s0 in range(STEPS):
                    win = VS[:, c, :, s0:s0 + TAPS].rearrange("p s k -> p k s")
                    dst = prod[:, 0:TAPS, s0:NS_:STEPS]
                    w = tapc[:, par, 0:TAPS].unsqueeze(2).to_broadcast([P, TAPS, SEQS])
                    op = nc.gpsimd.tensor_tensor(dst, win, w, ALU.mult)
                op.then_inc(pool_step, 1)
                nc.gpsimd.tensor_tensor(prod[:, TAPS, :], ones[:, 0:NS_],
                                        tapc[:, par, TAPS:TAPS + 1].to_broadcast([P, NS_]), ALU.mult).then_inc(pool_step, 1)
                for i, n in enumerate((16, 8, 4, 2)):
                    pool.wait_ge(pool_step, 7 * c + 2 + i)
                    nc.gpsimd.tensor_tensor(prod[:, 0:n, :], prod[:, 0:n, :], prod[:, n:2 * n, :],
                                            ALU.add).then_inc(pool_step, 1)
                pool.wait_ge(pool_step, 7 * c + 6)
                nc.gpsimd.tensor_tensor(C[:, c, NP_:T], prod[:, 0, :], prod[:, 1, :], ALU.add).then_inc(pool_step, 1)

            pool.wait_ge(ones_set, 1)
            pool.wait_ge(state_in, 16)
            tile(0, 0)
            tile(1, 1)
            with pool.Fori(1, CT // 2) as j:
                tile(2 * j, 0)
                tile(2 * j + 1, 1)

            pool.wait_ge(h2_ready, KT)
            nc.gpsimd.memset(hp[:, :, :, NCP:32], 0.0)
            nc.gpsimd.memset(hs[:].rearrange("p v g (s c) -> p (v g s) c", c=16)[:, :, NCS:16], 0.0).then_inc(pads2_set, 1)
            pool.wait_ge(store_p, 16)
            pool.wait_ge(conv_step, 32 * CT)
            nc.gpsimd.memset(vcd[:], 0.0)
            nc.gpsimd.memset(qblk[:], 0.0).then_inc(zeros_set, 1)
            pool.wait_ge(small_in, 96)
            pool.wait_ge(q_kept, FT_Q)
            pool.wait_ge(grow_kept, 3)

            def head(i, r):
                rows = slice(HD * r, HD * r + HD)
                if reaches(i, 1):
                    pool.wait_ge(qk_done, 16 * i + 8 * r - 8)
                if r or reaches(i, 1):
                    pool.wait_ge(bias_set, 2 * i + r)
                nc.gpsimd.tensor_copy(qb[rows, :], QT[rows, i, 0:NP_]).then_inc(qb_set, 1)
                if reaches(i, 1):
                    pool.wait_ge(sc_ready, 16 * i + 8 * r - 8)
                pool.wait_ge(qb_set, 2 * i + r + 1)
                nc.gpsimd.tensor_tensor(bias[:, r, :], dist[:], slopes[:, i, r:r + 1].to_broadcast([P, NP_]),
                                        ALU.mult).then_inc(bias_set, 1)

            head(0, 0)
            head(0, 1)
            with pool.Fori(1, 8) as i:
                head(i, 0)
                head(i, 1)


def feature_major(xp, xs):
    x = np.concatenate([xp.reshape(NP_, D), xs.reshape(NS_, D)], axis=0)
    return np.ascontiguousarray(x.T.reshape(KT, P, T).transpose(1, 0, 2))


def by_partition(v, n):
    return np.ascontiguousarray(v.reshape(n, P).T)


def shape_constants():
    out = {}
    slope = np.exp2(-8.0 * np.arange(1, HEADS + 1) / HEADS).astype(np.float32)
    by_step = np.array([[slope[8 * (i // 4) + 4 * r + i % 4] for r in range(2)] for i in range(8)], np.float32)
    out["slopes"] = np.ascontiguousarray(np.broadcast_to(by_step, (P, 8, 2)))
    q, k = np.arange(P)[:, None], np.arange(NP_)[None, :] - (NP_ - P)
    out["dist"] = np.where(k <= q, k - q, NEG).astype(np.float32)
    q = (np.arange(4) * P)[None, :, None, None] + np.arange(P)[:, None, None, None]
    blk = np.arange(32)[None, None, None, :]
    d = q - (blk * CSTRIDE + CBLK - 1)
    cb = np.where((d >= 0) & (blk < NCP), -slope[None, None, :, None] * d, NEG)
    out["cbias"] = np.ascontiguousarray(cb.reshape(P, 4, HEADS * 32).astype(np.float32))
    q_, r, j, t = np.unravel_index(np.arange(P), (4, 2, HPG, STEPS))
    sb = np.full((P, 2, 2, NKEY + P), NEG, np.float32)
    sel = np.zeros((P, 2, HEADS, 3), np.float32)
    for gp in range(2):
        head = HPG * (2 * gp + r) + j
        sel[np.arange(P), gp, head] = 1.0
        m = slope[head][:, None]
        for sg in range(2):
            seq = (4 * sg + q_)[:, None]
            sb[:, gp, sg, :PAST] = m * (np.arange(PAST)[None] - PAST - t[:, None])
            s_new, t_new = np.divmod(np.arange(NS_)[None], STEPS)
            sb[:, gp, sg, PAST:NKEY] = np.where((s_new == seq) & (t_new <= t[:, None]), m * (t_new - t[:, None]), NEG)
            s_c, c = np.divmod(np.arange(P)[None], 16)
            sb[:, gp, sg, NKEY:] = np.where((s_c == seq) & (c < NCS), m * (c * CSTRIDE + CBLK - 1 - PAST - t[:, None]), NEG)
    row = np.zeros((NS_, 2, P), np.float32)
    for sg in range(2):
        row[STEPS * (4 * sg + q_) + t, sg, np.arange(P)] = 1.0
    out["rowsel"] = row
    out["sbias"], out["headsel"] = sb, sel.reshape(P, 2, GL)
    return out


def kernel(x_prompt, x_sample, cache_kv, state_kv_win, state_conv, page_table, norm_g, final_norm_g,
           conv_w_in, conv_dw_w, conv_dw_b, conv_ln_g, conv_ln_b, conv_w_out,
           nsa_w_in, nsa_w_out, nsa_cmp_pe, nsa_cmp_w1, nsa_cmp_w2):
    import concourse.bacc as bacc
    from concourse.bass_utils import run_bass_kernel_spmd

    A = np.asarray
    arrays = {}
    arrays["x"] = feature_major(A(x_prompt), A(x_sample))
    g = np.concatenate([A(norm_g), A(final_norm_g)[None]], axis=0)
    arrays["gains"] = np.ascontiguousarray(g.reshape(3, KT, P).transpose(2, 0, 1))
    w = A(conv_w_in)[0].reshape(KT, P, 3, CT, P)[:, :, [1, 0, 2]]
    arrays["w_a"] = np.ascontiguousarray(w.transpose(3, 1, 2, 0, 4))
    taps = np.concatenate([A(conv_dw_w)[0], A(conv_dw_b)], axis=0)
    arrays["taps"] = np.ascontiguousarray(taps.reshape(32, CT, P).transpose(2, 1, 0))
    state = A(state_conv)[0].reshape(SEQS, STATE, CT, P).transpose(3, 2, 0, 1)
    arrays["state"] = np.ascontiguousarray(np.pad(state, ((0, 0), (0, 0), (0, 0), (0, STEPS))))
    arrays["ident"] = np.eye(P, dtype=np.float32)
    arrays["lng"] = by_partition(A(conv_ln_g)[0], CT)
    arrays["lnb"] = by_partition(A(conv_ln_b)[0], CT)
    arrays["w_c"] = np.ascontiguousarray(A(conv_w_out)[0].reshape(CT, P, KT, P).transpose(2, 1, 0, 3))
    w = A(nsa_w_in)[0]
    wq, wz, wkv, wgl = np.split(w, [D, 2 * D, 2 * D + 6 * GROUPS * HD], axis=1)
    wq = wq.reshape(D, 2, 2, HPG, HD).transpose(0, 1, 3, 2, 4).reshape(D, D)
    wkv = wkv.reshape(D, 6, GROUPS * HD)
    w_f = np.concatenate([wkv[:, 0], wkv[:, 1], wkv[:, 2], wkv[:, 4], wq, wz], axis=1)
    arrays["w_f"] = np.ascontiguousarray(w_f.reshape(KT, P, FT, P).transpose(2, 1, 0, 3))
    w_t = np.concatenate([wkv[:, 3], wkv[:, 5], wgl], axis=1)
    arrays["w_t"] = np.ascontiguousarray(w_t.reshape(KT, P, VTOK).transpose(1, 0, 2))
    arrays["w_o"] = np.ascontiguousarray(A(nsa_w_out)[0].reshape(KT, P, KT, P).transpose(2, 1, 0, 3))
    arrays["w1"] = np.ascontiguousarray(A(nsa_cmp_w1)[0].reshape(2, CBLK // 2, P, P).transpose(2, 0, 1, 3))
    arrays["w2"] = np.ascontiguousarray(A(nsa_cmp_w2)[0].transpose(1, 0, 2))
    arrays["pe"] = np.ascontiguousarray(A(nsa_cmp_pe)[0].reshape(2, CBLK // 2, P).transpose(2, 0, 1))
    cache = A(cache_kv)[0]
    pool = cache.shape[0]
    c01 = cache[:, :, 0:2].reshape(pool, SEL, 2, 2, GROUPS, HD)
    arrays["cache_cmp"] = np.ascontiguousarray(c01.transpose(0, 2, 5, 3, 4, 1).reshape(pool, P, 2, GROUPS, SEL))
    k2 = cache[:, :, 2].reshape(pool, PAGE, 2, 2, HD).transpose(0, 3, 4, 2, 1).reshape(pool, P, 2 * P)
    arrays["cache_sel"] = np.ascontiguousarray(np.concatenate([k2, cache[:, :, 3].reshape(pool, P, 2 * P)], axis=2))
    win = A(state_kv_win)[0]
    kw = win[:, :, 0].reshape(SEQS, PAST, 2, 2, HD).transpose(3, 4, 0, 2, 1).reshape(P, SEQS, 2 * PAST)
    vw = win[:, :, 1].reshape(SEQS, 2, P, GROUPS * HD).transpose(2, 0, 1, 3).reshape(P, SEQS, 2 * PAST)
    arrays["cache_win"] = np.ascontiguousarray(np.concatenate([kw, vw], axis=2))
    arrays["win_state"] = np.ascontiguousarray(win[:, STEPS:].reshape(SEQS, -1))
    arrays["pages"] = np.ascontiguousarray(A(page_table).reshape(1, SEQS * NPG).astype(np.int32))
    arrays.update(shape_constants())
    outs = {"y": (P, KT, T), "conv_p": (P, CT, STATE), "conv_s": (P, CT, SEQS, STATE + STEPS),
            "kv_cmp": (P, 2, GROUPS, NP_ // 2), "kv_cmp_s": (P, 4, NS_), "k_new": (P, 2, 2, T),
            "v_new": (P, 5, 2 * GROUPS * HD), "win_s": (SEQS, (PAST - STEPS) * 2 * GROUPS * HD)}

    nc = bacc.Bacc("TRN2", target_bir_lowering=False, num_devices=1)
    io = {}
    for n, a in arrays.items():
        io[n] = nc.dram_tensor(f"in_{n}", a.shape, mybir.dt.from_np(a.dtype), kind="ExternalInput").ap()
    for n, shape in outs.items():
        io[n] = nc.dram_tensor(f"out_{n}", shape, F32, kind="ExternalOutput").ap()
    build(nc, io)
    r = run_bass_kernel_spmd(nc, [{f"in_{n}": a for n, a in arrays.items()}], core_ids=[0])
    r = r.results[0]
    y = r["out_y"].transpose(2, 1, 0).reshape(T, D)
    conv_p = r["out_conv_p"].transpose(2, 1, 0).reshape(1, 1, STATE, DC)
    conv_s = r["out_conv_s"][:, :, :, STEPS:].transpose(2, 3, 1, 0).reshape(1, SEQS, STATE, DC)
    kv = np.empty((T, 6, GROUPS, HD), np.float32)
    kv[:NP_, 0:2] = r["out_kv_cmp"].reshape(2, HD, 2, GROUPS, NP_ // 2).transpose(4, 0, 2, 3, 1).reshape(NP_, 2, GROUPS, HD)
    kv[NP_:, 0:2] = r["out_kv_cmp_s"].reshape(2, HD, 2, 2, NS_).transpose(4, 2, 3, 0, 1).reshape(NS_, 2, GROUPS, HD)
    k = r["out_k_new"].reshape(2, HD, 2, 2, T).transpose(4, 2, 3, 0, 1).reshape(T, 2, GROUPS, HD)
    v = r["out_v_new"].reshape(P, 5, 2, GROUPS, HD)
    v = np.concatenate([v[:, 0:4].transpose(1, 0, 2, 3, 4).reshape(NP_, 2, GROUPS, HD), v[:NS_, 4]], axis=0)
    kv[:, 2::2], kv[:, 3::2] = k, v
    kv_prompt = kv[:NP_, :4].reshape(1, 1, NP_, 4, GROUPS, HD)
    kv_sample = kv[NP_:, :4].reshape(1, SEQS, STEPS, 4, GROUPS, HD)
    win_prompt = kv[:NP_, 4:].reshape(1, 1, NP_, 2, GROUPS, HD)
    win_sample = np.concatenate([r["out_win_s"].reshape(SEQS, PAST - STEPS, 2, GROUPS, HD),
                                 kv[NP_:, 4:].reshape(SEQS, STEPS, 2, GROUPS, HD)], axis=1)[None]
    return (y[:NP_].reshape(1, NP_, D), y[NP_:].reshape(SEQS, STEPS, D), kv_prompt, kv_sample,
            win_prompt, win_sample, conv_p, conv_s)
```

```python
import numpy as np
import concourse.bass as bass
from concourse import mybir
from contextlib import ExitStack

F32 = mybir.dt.float32
F32R = mybir.dt.float32r
I32 = mybir.dt.int32
ACT = mybir.ActivationFunctionType
ALU = mybir.AluOpType
AX = mybir.AxisListType

P = 128
D = 1024
KT = D // P
NP_, NS_ = 512, 32
T = NP_ + NS_
TA = 256
TB = T - TA
SEQS, STEPS = 8, 4
DC = 2048
CT = DC // P
TAPS = 31
STATE = TAPS - 1
EPS = 1e-6
HEADS, HD, GROUPS = 16, 64, 4
HPG = HEADS // GROUPS
PAST, PAGE = 256, 128
NPG = PAST // PAGE
SEL = 64
CSTRIDE, CBLK = 16, 32
NCP = (NP_ - CBLK) // CSTRIDE + 1
NCS = (PAST + STEPS - CBLK) // CSTRIDE + 1
NEG = -1e30
FLOOR = -1e28
GL = HEADS * 3
VTOK = 2 * GROUPS * HD + GL
VH = VTOK // 2
FT_KV, FT_Q, FT_Z = 8, 8, 8
FT = FT_KV + FT_Q + FT_Z
NKEY = PAST + NS_

BASE = 16512


def reaches(i, n):
    return not isinstance(i, int) or i >= n


SAMPLE_WIN = 8


def sample_unit(v):
    w, br = divmod(v, 2) if v < SAMPLE_WIN else (v - SAMPLE_WIN, 2)
    return w // 2, w % 2, br


def build(nc, io):
    ctx = ExitStack()
    with ctx:
        used = {}

        def at(name, shape, offset, dt=F32):
            size = 4 * int(np.prod(shape[1:]))
            used[name] = (offset, size)
            return nc.alloc_sbuf_tensor_at(name, shape, dt, offset=offset)

        def sem(name):
            return ctx.enter_context(nc.semaphore(name))

        ROW = T * 4
        o = BASE
        X = at("X", [P, KT, T], o); o += KT * ROW
        SM = o; o += 12288
        HR = o; o += KT * ROW
        W1R = o; o += 16384
        G0 = o; o += 2 * KT * ROW
        G1 = o
        NR = 229344 - 4 * ROW
        s = SM
        ones = at("ones", [P, P], s); s += P * 4
        ident = at("ident", [P, P], s); s += P * 4
        gains = at("gains", [P, 3, KT], s); s += 96
        lng = at("lng", [P, CT], s); s += 64
        lnb = at("lnb", [P, CT], s); s += 64
        SMT = s
        taps = at("taps", [P, CT, 32], s); s += CT * 128
        tapc = at("tapc", [P, 2, 32], s); s += 256
        ctail = at("ctail", [P, CT, STATE], s); s += CT * STATE * 4
        SMX = s
        mean = at("mean", [P, T], NR)
        rstd = at("rstd", [P, T], NR + ROW)
        sq = at("sq", [P, 2, T], NR + 2 * ROW)
        H = at("H", [P, KT, T], HR)
        C = at("C", [P, CT, T], G0)
        s = G1
        Z1 = at("Z1", [P, CT, T], s); s += CT * ROW
        ringA = at("ringA", [P, 2, 3, KT, P], s); RINGA = s; s += 2 * 3 * KT * P * 4
        VS = at("VS", [P, CT, SEQS, STATE + STEPS], s); s += CT * SEQS * (STATE + STEPS) * 4
        VP = at("VP", [P, 2, STATE + NP_], s); s += 2 * 2176
        sig = at("sig", [P, 2, T], s); s += 2 * ROW
        acc = at("acc", [P, 2, NP_], s); s += 2 * NP_ * 4
        prod = at("prod", [P, 32, NS_], s); s += 32 * NS_ * 4
        assert s <= NR
        Ch = at("Ch", [P, CT, T], G1, F32R)
        Cl = at("Cl", [P, CT, T], G0, F32R)
        ringC = at("ringC", [P, 2, CT, P], RINGA)
        ringCl = at("ringCl", [P, 2, CT, P], RINGA, F32R)
        ringCh = at("ringCh", [P, 2, CT, P], W1R, F32R)
        s = VSR = RINGA + 2 * 3 * KT * P * 4
        ringE = at("ringE", [P, 3, KT, P], s); s += 3 * KT * P * 4
        bias = at("bias", [P, 2, NP_], s); s += 2 * NP_ * 4
        rowsel = at("rowsel", [NS_, 2, P], s)
        vcs = at("vcs", [P, GROUPS * HD], s); s += GROUPS * HD * 4
        assert s <= VSR + 17408
        s = VSR + 17408
        wtok = at("wtok", [P, KT, VTOK], s)
        PCT = at("PCT", [HD, 8, NP_], s); s += KT * VTOK * 4
        KK = at("KK", [P, 2, GROUPS, NP_ // 2], s)
        S = at("S", [P, 4, NP_], s); s += 4 * NP_ * 4
        assert s <= NR - 2048
        cache_cmp = at("cache_cmp", [P, 2, SEQS * GROUPS, P], G1)
        cache_sel = at("cache_sel", [P, SEQS, NPG, 4 * P], G1)
        s = RINGA - 2048
        KTm = at("KTm", [P, 2, 2, T], s); s += 4 * ROW
        V = at("V", [P, 5, VTOK], s); s += 5 * VTOK * 4
        PT = at("PT", [P, 2, NP_], s); s += 2 * NP_ * 4
        kcs = at("kcs", [P, 2, P], s); s += 2 * P * 4
        kcp = at("kcp", [P, 2, 32], s); s += 2 * 32 * 4
        KN = at("KN", [P, 4, NS_], s); s += 4 * NS_ * 4
        assert s <= VSR
        QT = at("QT", [P, 8, T], G0)
        ZT = at("ZT", [P, 8, T], G0 + KT * ROW)
        Y = at("Y", [P, KT, T], G0)
        W1 = at("W1", [P, 2, CBLK // 2, P], W1R)
        cbias = at("cbias", [P, 4, NP_], W1R)
        SX = at("SX", [P, 4, NP_], W1R + 4 * NP_ * 4)
        PTB = at("PTB", [P, 2, 4, NP_], HR)
        cache_win = at("cache_win", [P, SEQS, 8 * P], HR)
        s = NR
        hp = at("hp", [P, 2, GROUPS, 32], s); s += 2 * GROUPS * 32 * 4
        hs = at("hs", [P, 2, GROUPS, SEQS * 16], s); s += 2 * SEQS * GROUPS * 16 * 4
        sbias = at("sbias", [P, 2, 2, NKEY + P], NR)
        s = SMT
        vcd = at("vcd", [HD, 2, P], s)
        s = SMX
        dist = at("dist", [P, NP_], s); s += NP_ * 4
        qblk = at("qblk", [P, SEQS, 2, 32], s); s += SEQS * 2 * 32 * 4
        slopes = at("slopes", [P, 8, 2], s); s += 64
        pe_in = at("pe_in", [P, 2, CBLK // 2], s); s += 128
        pe_hid = at("pe_hid", [P, 2], s); s += 32
        W2 = at("W2", [P, 2, HD], s); s += 512
        headsel = at("headsel", [P, 2, GL], s); s += 2 * GL * 4
        gates_c = at("gates_c", [P, 4, HEADS], s); s += 4 * HEADS * 4
        gates_sw = at("gates_sw", [P, 4, HEADS * 2], s); s += 4 * HEADS * 8
        gpair = at("gpair", [P, 4, 2, 2], s); s += 64
        nmax = at("nmax", [P, 16], s); s += 64
        rsum = at("rsum", [P, 16], s); s += 64
        gsc = at("gsc", [P, 16], s); s += 64
        m16 = at("m16", [P, HEADS], s); s += 64
        s16 = at("s16", [P, HEADS], s); s += 64
        grow = at("grow", [P, 2, 2, 3], s); s += 64
        tick = at("tick", [1, 16], s); s += 64
        pages = at("pages", [1, SEQS * NPG], s, I32); s += 64
        assert s <= HR, (s, HR)
        qb = at("qb", [P, NP_], NR - 2048)
        gtmp = at("gtmp", [P, 2, 2, GL], NR - 2048)

        ps = ctx.enter_context(nc.psum_tensor("ps", [P, 8, 512], F32))

        def halves(i):
            return ((ps[:, 2 * i, 0:TA], slice(0, TA)), (ps[:, 2 * i + 1, 0:TB], slice(TA, T)))

        def prompt_of(i):
            return ps[:, 2 * i:2 * i + 2, 0:TA]

        def sample_of(i):
            return ps[:, 2 * i + 1, TA:TB]

        x_in = sem("x_in")
        consts_in = sem("consts_in")
        gains_in = sem("gains_in")
        taps_in = sem("taps_in")
        state_in = sem("state_in")
        wA_in = [sem(f"wA_in{i}") for i in range(2)]
        wC_in = [sem(f"wC_in{i}") for i in range(2)]
        store_p = sem("store_p")
        store_s = sem("store_s")
        stored = sem("stored")
        squared = sem("squared")
        sq_summed = sem("sq_summed")
        mean_sq = sem("mean_sq")
        inv_var = sem("inv_var")
        rstd_ready = sem("rstd_ready")
        h_ready = sem("h_ready")
        ones_set = sem("ones_set")
        pads_set = sem("pads_set")
        prod_row = sem("prod_row")
        gate_done = sem("gate_done")
        lin_done = sem("lin_done")
        z_done = sem("z_done")
        sig_ready = sem("sig_ready")
        z_kept = sem("z_kept")
        tail_kept = sem("tail_kept")
        tap_set = sem("tap_set")
        v_ready = sem("v_ready")
        conv_step = sem("conv_step")
        pool_step = sem("pool_step")
        c_summed = sem("c_summed")
        mean_ready = sem("mean_ready")
        centered = sem("centered")
        scaled = sem("scaled")
        activated = sem("activated")
        c_gated = sem("c_gated")
        ch_ready = sem("ch_ready")
        cl_ready = sem("cl_ready")
        wCh_ready = sem("wCh_ready")
        wCl_ready = sem("wCl_ready")
        out1_done = sem("out1_done")
        x_added = sem("x_added")

        wtok_in = sem("wtok_in")
        w1_in = sem("w1_in")
        small_in = sem("small_in")
        pages_in = sem("pages_in")
        cmp_in = sem("cmp_in")
        sel_in = sem("sel_in")
        win_in = sem("win_in")
        cbias_in = sem("cbias_in")
        sbias_in = sem("sbias_in")
        wE_in = [sem(f"wE_in{i}") for i in range(3)]
        wO_in = [sem(f"wO_in{i}") for i in range(2)]
        h2_ready = sem("h2_ready")
        f_done = sem("f_done")
        kv_kept = sem("kv_kept")
        tok_done = sem("tok_done")
        v_kept = sem("v_kept")
        grow_done = sem("grow_done")
        grow_kept = sem("grow_kept")
        zeros_set = sem("zeros_set")
        kk_stored = sem("kk_stored")
        grow_ready = sem("grow_ready")
        gates_ready = sem("gates_ready")
        hid_done = sem("hid_done")
        pe_kept = sem("pe_kept")
        hid_ready = sem("hid_ready")
        pads2_set = sem("pads2_set")
        comp_done = sem("comp_done")
        comp_kept = sem("comp_kept")
        q_kept = sem("q_kept")
        qblk_ready = sem("qblk_ready")
        zt_ready = sem("zt_ready")
        cs_done = sem("cs_done")
        cs_step = sem("cs_step")
        cs_exp = sem("cs_exp")
        cs_t = sem("cs_t")
        cs_kept = sem("cs_kept")
        qb_set = sem("qb_set")
        pc_set = sem("pc_set")
        bias_set = sem("bias_set")
        qk_done = sem("qk_done")
        sc_ready = sem("sc_ready")
        exp_ready = sem("exp_ready")
        gate_set = sem("gate_set")
        inv_ready = sem("inv_ready")
        p_ready = sem("p_ready")
        t_done = sem("t_done")
        pt_kept = sem("pt_kept")
        pv_done = sem("pv_done")
        ss_done = sem("ss_done")
        ss_ready = sem("ss_ready")
        ss_exp = sem("ss_exp")
        ss_step = sem("ss_step")
        ss_t = sem("ss_t")
        ss_pt = sem("ss_pt")
        ss_pv = sem("ss_pv")
        og_sample = sem("og_sample")
        og = sem("og")
        out2_done = sem("out2_done")
        x2_added = sem("x2_added")
        y_ready = sem("y_ready")

        def weights_at(u):
            return S[:, u % 8] if u % 8 < 4 else SX[:, u % 8 - 4]

        def split(ap):
            return ap.rearrange("p (b t) -> p b t", b=2)

        block = ctx.enter_context(nc.Block())

        @block.sync
        def _(sp):
            sp.dma_start(X[:], io["x"]).then_inc(x_in, 16)
            sp.dma_start(gains[:], io["gains"]).then_inc(gains_in, 16)

            def load_wA(c, par, turn):
                if turn is not None:
                    sp.wait_ge(z_done, c - 1)
                sp.dma_start(ringA[:, par], io["w_a"][c]).then_inc(wA_in[par], 16)

            load_wA(0, 0, None)
            sp.dma_start(pages[:], io["pages"]).then_inc(pages_in, 16)
            sp.dma_start(taps[:], io["taps"]).then_inc(taps_in, 16)
            load_wA(1, 1, None)
            sp.dma_start(VS[:], io["state"]).then_inc(state_in, 16)
            sp.dma_start(ident[:], io["ident"]).then_inc(consts_in, 16)
            sp.dma_start(lng[:], io["lng"]).then_inc(consts_in, 16)
            sp.dma_start(lnb[:], io["lnb"]).then_inc(consts_in, 16)
            with sp.Fori(1, CT // 2) as j:
                load_wA(2 * j, 0, j)
                load_wA(2 * j + 1, 1, j)
            for n in range(KT):
                if n < 2:
                    sp.wait_ge(z_done, CT)
                else:
                    sp.wait_ge(out1_done, n - 1)
                sp.dma_start(ringC[:, n % 2], io["w_c"][n]).then_inc(wC_in[n % 2], 16)
                if n == 1:
                    sp.wait_ge(tail_kept, CT)
                    sp.dma_start(io["conv_p"], ctail[:]).then_inc(store_p, 16)
                    sp.wait_ge(v_ready, 2 * CT)
                    sp.dma_start(io["conv_s"], VS[:]).then_inc(store_s, 16)
            for name, tile in (("slopes", slopes), ("dist", dist), ("pe", pe_in), ("w2", W2), ("headsel", headsel), ("rowsel", rowsel)):
                sp.dma_start(tile[:], io[name]).then_inc(small_in, 16)
            sp.wait_ge(store_s, 16)
            sp.wait_ge(pool_step, 7 * CT)
            for n in range(3):
                sp.dma_start(ringE[:, n], io["w_f"][n]).then_inc(wE_in[n], 16)
            sp.dma_start(wtok[:], io["w_t"]).then_inc(wtok_in, 16)
            sp.wait_ge(out1_done, KT)
            sp.dma_start(W1[:], io["w1"]).then_inc(w1_in, 16)
            sp.wait_ge(pages_in, 16)
            for i in range(SEQS * NPG):
                page = sp.value_load(pages[0:1, i:i + 1], min_val=0, max_val=io["cache_cmp"].shape[0] - 1)
                q, pg = divmod(i, NPG)
                for kv in range(2):
                    sp.dma_start(cache_cmp[:, kv, q::SEQS, pg * SEL:(pg + 1) * SEL],
                                 io["cache_cmp"][bass.ds(page, 1), :, kv].rearrange("o p g t -> (o p) g t")).then_inc(cmp_in, 16)
            for n in range(3, FT):
                sp.wait_ge(f_done, n - 2)
                sp.dma_start(ringE[:, n % 3], io["w_f"][n]).then_inc(wE_in[n % 3], 16)
                if n == FT_KV + 1:
                    sp.wait_ge(kv_kept, FT_KV)
                    sp.wait_ge(v_kept, 5)
                    sp.dma_start(io["kv_cmp"], KK[:]).then_inc(kk_stored, 16)
                    sp.dma_start(io["kv_cmp_s"], KN[:]).then_inc(stored, 16)
                    sp.dma_start(io["k_new"], KTm[:]).then_inc(stored, 16)
                    sp.dma_start(io["v_new"][:, 0:4], V[:, 0:4, 0:2 * GROUPS * HD]).then_inc(stored, 16)
                    sp.dma_start(io["v_new"][0:NS_, 4], V[0:NS_, 4, 0:2 * GROUPS * HD]).then_inc(stored, 16)
                    sp.wait_ge(hid_done, 2)
                    sp.dma_start(cbias[:], io["cbias"]).then_inc(cbias_in, 16)
                    for i in range(SEQS * NPG):
                        page = sp.value_load(pages[0:1, i:i + 1], min_val=0, max_val=io["cache_sel"].shape[0] - 1)
                        sp.dma_start(cache_sel[:, i // NPG, i % NPG, :],
                                     io["cache_sel"][bass.ds(page, 1)].rearrange("o p n -> (o p) n")).then_inc(sel_in, 16)
            sp.wait_ge(f_done, FT)
            for n in range(2):
                sp.dma_start(ringE[:, n], io["w_o"][n]).then_inc(wO_in[n], 16)
            sp.wait_ge(comp_done, 1)
            sp.dma_start(sbias[:], io["sbias"]).then_inc(sbias_in, 16)
            sp.dma_start(io["win_s"], io["win_state"]).then_inc(stored, 16)
            sp.wait_ge(pv_done, 32)
            sp.dma_start(cache_win[:], io["cache_win"]).then_inc(win_in, 16)
            for n in range(2, KT):
                sp.wait_ge(out2_done, n - 1)
                sp.dma_start(ringE[:, n % 2], io["w_o"][n]).then_inc(wO_in[n % 2], 16)
            for k in range(KT):
                sp.wait_ge(y_ready, k + 1)
                sp.dma_start(io["y"][:, k], Y[:, k]).then_inc(stored, 16)
            sp.wait_ge(stored, 16 * (5 + KT))
            sp.wait_ge(store_p, 16)

        @block.tensor
        def _(pe):
            def sum_squares(n):
                for k in range(KT):
                    pe.wait_ge(squared, n * KT + k + 1)
                    for dst, cols in halves(3):
                        mm = nc.tensor.matmul(dst, ones[:], sq[:, k % 2, cols], start=(k == 0), stop=(k == KT - 1))
                    mm.then_inc(sq_summed, 1)

            pe.wait_ge(ones_set, 1)
            sum_squares(0)

            def project(par, j, pair, done):
                for k in range(KT):
                    for dst, cols in halves(pair):
                        mm = nc.tensor.matmul(dst, ringA[:, par, j, k, :], H[:, k, cols],
                                              start=(k == 0), stop=(k == KT - 1))
                mm.then_inc(done, 1)

            def add_to_mean(c, first, last):
                pe.wait_ge(conv_step, 32 * c + 32)
                pe.wait_ge(pool_step, 7 * c + 7)
                for dst, cols in halves(3):
                    rhs = C[:, c, cols]
                    mm = nc.tensor.matmul(dst, ones[:], rhs, start=first, stop=last)
                mm.then_inc(c_summed, 1)

            def tile(c, par, turn):
                pe.wait_ge(wA_in[par], 16 * (turn + 1))
                if reaches(c, 1):
                    pe.wait_ge(sig_ready, c)
                project(par, 0, 0, gate_done)
                if reaches(c, 1):
                    pe.wait_ge(v_ready, 2 * c)
                project(par, 1, 1, lin_done)
                if reaches(c, 1):
                    pe.wait_ge(z_kept, c)
                project(par, 2, 2, z_done)

            pe.wait_ge(h_ready, KT)
            tile(0, 0, 0)
            tile(1, 1, 0)
            add_to_mean(0, True, False)
            tile(2, 0, 1)
            add_to_mean(1, False, False)
            tile(3, 1, 1)
            with pe.Fori(2, CT // 2) as j:
                add_to_mean(2 * j - 2, False, False)
                tile(2 * j, 0, j)
                add_to_mean(2 * j - 1, False, False)
                tile(2 * j + 1, 1, j)
            add_to_mean(CT - 2, False, False)
            add_to_mean(CT - 1, False, True)

            for c in range(CT):
                pe.wait_ge(squared, KT + c + 1)
                if c == 0:
                    pe.wait_ge(sig_ready, CT)
                for dst, cols in halves(0):
                    mm = nc.tensor.matmul(dst, ones[:], sq[:, c % 2, cols], start=(c == 0), stop=(c == CT - 1))
                mm.then_inc(sq_summed, 1)

            def split_product(dst_of, wh, wl, xh, xl, first, last):
                for w, x, begins, ends in ((wh, xh, first, False), (wh, xl, False, False), (wl, xh, False, last)):
                    for dst, cols in dst_of:
                        mm = nc.tensor.matmul(dst, w, x[:, cols], start=begins, stop=ends)
                return mm

            def out1(n, k):
                return split_product(halves(1 + n % 3), ringCh[:, n % 2, k, :], ringCl[:, n % 2, k, :],
                                     Ch[:, k, :], Cl[:, k, :], k == 0, k == CT - 1)

            pe.wait_ge(wCh_ready, 2)
            pe.wait_ge(wCl_ready, 2)
            for k in range(CT):
                pe.wait_ge(ch_ready, k + 1)
                pe.wait_ge(cl_ready, k + 1)
                for n in range(2):
                    mm = out1(n, k)
                    if k == CT - 1:
                        mm.then_inc(out1_done, 1)
            for n in range(2, KT):
                pe.wait_ge(wCh_ready, n + 1)
                pe.wait_ge(wCl_ready, n + 1)
                if n >= 3:
                    pe.wait_ge(x_added, n - 2)
                for k in range(CT):
                    mm = out1(n, k)
                mm.then_inc(out1_done, 1)

            pe.wait_ge(x_added, KT)
            for k in range(KT):
                pe.wait_ge(squared, KT + CT + k + 1)
                for dst, cols in halves(3):
                    mm = nc.tensor.matmul(dst, ones[:], sq[:, k % 2, cols], start=(k == 0), stop=(k == KT - 1))
                mm.then_inc(sq_summed, 1)
            pe.wait_ge(h2_ready, KT)

            def f_tile(n, pair):
                pe.wait_ge(wE_in[n % 3], 16 * (n // 3 + 1))
                for k in range(KT):
                    for dst, cols in halves(pair):
                        mm = nc.tensor.matmul(dst, ringE[:, n % 3, k, :], H[:, k, cols],
                                              start=(k == 0), stop=(k == KT - 1))
                mm.then_inc(f_done, 1)

            for n in range(FT_KV):
                if n >= 4:
                    pe.wait_ge(kv_kept, n - 3)
                f_tile(n, n % 4)
            pe.wait_ge(wtok_in, 16)
            for i in range(5):
                if i < 4:
                    pe.wait_ge(kv_kept, 5 + i)
                else:
                    pe.wait_ge(v_kept, 1)
                rows = min(P, T - i * P)
                for k in range(KT):
                    for b in range(2):
                        mm = nc.tensor.matmul(ps[0:rows, 2 * (i % 4) + b, 0:VH], H[:, k, i * P:i * P + rows],
                                              wtok[:, k, b * VH:(b + 1) * VH], start=(k == 0), stop=(k == KT - 1))
                mm.then_inc(tok_done, 1)
            pe.wait_ge(v_kept, 5)
            pe.wait_ge(small_in, 96)
            for sg in range(2):
                mm = nc.tensor.matmul(ps[:, 2 + sg, 0:GL], rowsel[:, sg, :], V[0:NS_, 4, 2 * GROUPS * HD:VTOK],
                                      start=True, stop=True)
            mm.then_inc(grow_done, 1)
            pe.wait_ge(w1_in, 16)
            pe.wait_ge(cmp_in, 32 * SEQS * NPG)
            for kv in range(2):
                for m in range(CBLK // 2):
                    w, first, last = W1[:, kv, m, :], m == 0, m == CBLK // 2 - 1
                    nc.tensor.matmul(ps[:, kv, 0:GROUPS * NCP], w, KK[:, kv, :, m:m + 8 * (NCP - 1) + 1:8],
                                     start=first, stop=last)
                    nc.tensor.matmul(ps[:, 4 + kv, 0:SEQS * GROUPS * NCS], w,
                                     cache_cmp[:, kv, :, m:m + 8 * (NCS - 1) + 1:8], start=first, stop=last)
                    mm = nc.tensor.matmul(ps[:, 6 + kv, 0:1], w, pe_in[:, kv, m:m + 1], start=first, stop=last)
                mm.then_inc(hid_done, 1)

            def q_or_z(n):
                i = n - FT_KV
                if i < FT_Q:
                    if i == 0:
                        pe.wait_ge(grow_kept, 2)
                    if i == 1:
                        pe.wait_ge(pe_kept, 1)
                    if i >= 2:
                        pe.wait_ge(q_kept, i - 1)
                    f_tile(n, 3 if i % 2 else 1)
                else:
                    i -= FT_Q
                    if i < 2:
                        pe.wait_ge(comp_kept, 4)
                        pe.wait_ge(q_kept, FT_Q)
                    else:
                        pe.wait_ge(zt_ready, i - 1)
                    f_tile(n, i % 2)

            q_or_z(FT_KV)
            q_or_z(FT_KV + 1)
            pe.wait_ge(hid_ready, 4)
            pe.wait_ge(pads2_set, 1)
            for g in range(GROUPS):
                rows = slice(HD * (g % 2), HD * (g % 2) + HD)
                nc.tensor.matmul(ps[rows, 0, 32 * (g // 2):32 * (g // 2) + 32], W2[:, 0, :], hp[:, 0, g, :],
                                 start=True, stop=True)
                nc.tensor.matmul(ps[rows, 1, P * (g // 2):P * (g // 2) + P], W2[:, 0, :], hs[:, 0, g],
                                 start=True, stop=True)
                nc.tensor.matmul(ps[32 * (g % 2):32 * (g % 2) + 32, 4, HD * (g // 2):HD * (g // 2) + HD],
                                 hp[:, 1, g, :], W2[:, 1, :], start=True, stop=True)
                mm = nc.tensor.matmul(ps[:, 5, HD * g:HD * g + HD], hs[:, 1, g], W2[:, 1, :],
                                      start=True, stop=True)
            mm.then_inc(comp_done, 1)
            for i in range(2, FT_Q):
                q_or_z(FT_KV + i)
            pe.wait_ge(q_kept, FT_Q)
            pe.wait_ge(comp_kept, 4)
            for t in range(4):
                if t >= 1:
                    pe.wait_ge(cs_step, 9 * t - 8)
                for h in range(HEADS):
                    g, j = divmod(h, HPG)
                    rows = slice(HD * (g % 2), HD * (g % 2) + HD)
                    col = P * (g // 2) + 32 * j
                    mm = nc.tensor.matmul(ps[:, 4 + g % 2, col:col + 32], QT[rows, HPG * (g // 2) + j, t * P:(t + 1) * P],
                                          kcp[rows, g // 2, :], start=True, stop=True)
                mm.then_inc(cs_done, 1)
                q_or_z(FT_KV + FT_Q + 2 * t)
                pe.wait_ge(cs_step, 9 * t + 9)
                if t >= 1:
                    pe.wait_ge(cs_kept, t)
                for i in range(8):
                    mm = nc.tensor.transpose(ps[0:HD, 6 + i // 4, P * (i % 4):P * (i % 4) + P],
                                             S[:, 0, HD * i:HD * i + HD], ident[:])
                mm.then_inc(cs_t, 1)
                q_or_z(FT_KV + FT_Q + 2 * t + 1)

            pe.wait_ge(zt_ready, FT_Z)
            pe.wait_ge(cs_kept, 4)

            def qk(i, u, gp):
                r, b, t = u // 8, u % 8 // 4, u % 4
                rows, n = slice(HD * r, HD * r + HD), (t + 1) * P
                if u % 8 == 0:
                    pe.wait_ge(qb_set, 2 * i + r + 1)
                if u >= 4 or reaches(i, 1):
                    pe.wait_ge(sc_ready, 16 * i + u - 3)
                nc.tensor.matmul(ps[:, u % 4, 0:n], qb[rows, t * P:(t + 1) * P], KTm[rows, b, gp, 0:n],
                                 start=True, stop=True).then_inc(qk_done, 1)

            def transpose(i, u):
                t = u % 4
                pe.wait_ge(p_ready, 16 * i + u + 1)
                if u >= 2 or reaches(i, 1):
                    pe.wait_ge(pt_kept, 16 * i + u - 1)
                for k in range(t + 1):
                    mm = nc.tensor.transpose(ps[:, 4 + u % 2, P * k:P * k + P], weights_at(u)[:, P * k:P * k + P], ident[:])
                mm.then_inc(t_done, 1)

            def pv(i, n, gp):
                r, b, k = n // 8, n % 8 // 4, n % 4
                out = ps[HD * r:HD * r + HD, 6 + r]
                if n % 8 == 0:
                    nc.tensor.matmul(out, vcd[:, gp, HD * r:HD * r + HD], PT[0:HD, 0, :], start=True, stop=False)
                if k == 0:
                    pe.wait_ge(pt_kept, 16 * i + n + 4)
                v = b * GROUPS * HD + (2 * gp + r) * HD
                mm = nc.tensor.matmul(out[:, P * k:NP_], V[:, k, v:v + HD], PTB[:, b, k, P * k:NP_],
                                      start=False, stop=(b == 1 and k == 3))
                if k == 3:
                    mm.then_inc(pv_done, 1)

            def attend(i, gp, last_gp):
                for u in range(16):
                    if u >= 4:
                        transpose(i, u - 4)
                    elif reaches(i, 1):
                        transpose(i - 1, u + 12)
                    if u == 8:
                        if reaches(i, 1):
                            pe.wait_ge(og, 2 * i - 1)
                        pe.wait_ge(pc_set, i + 1)
                    elif u == 0 and reaches(i, 2):
                        pe.wait_ge(og, 2 * i - 2)
                    qk(i, u, gp)
                    if u >= 8:
                        pv(i, u - 8, gp)
                    elif reaches(i, 1):
                        pv(i - 1, u + 8, last_gp)

            attend(0, 0, 0)
            attend(1, 0, 0)
            with pe.Fori(2, 4) as i:
                attend(i, 0, 0)
            attend(4, 1, 0)
            with pe.Fori(5, 8) as i:
                attend(i, 1, 1)
            for u in range(8):
                if u < 4:
                    transpose(7, u + 12)
                if u == 0:
                    pe.wait_ge(og, 14)
                pv(7, u + 8, 1)

            pe.wait_ge(qblk_ready, 1)
            pe.wait_ge(sel_in, 16 * SEQS * NPG)

            def sample_scores(v):
                gp, sg, br = sample_unit(v)
                if v < 2:
                    pe.wait_ge(sc_ready, 16 * 8)
                else:
                    pe.wait_ge(ss_ready, v - 1)
                if v == SAMPLE_WIN:
                    pe.wait_ge(win_in, 16)
                for q in range(4):
                    s_ = 4 * sg + q
                    rows = slice(32 * q, 32 * q + 32)
                    if br == 0:
                        mm = nc.tensor.matmul(ps[rows, v % 2, 0:P], qblk[:, s_, gp, :], kcs[:, gp, :], start=True, stop=True)
                        continue
                    keys = (cache_sel[:, s_, :, gp * P:gp * P + P] if br == 1
                            else cache_win[:, s_, gp * PAST:(gp + 1) * PAST])
                    nc.tensor.matmul(ps[rows, v % 2, 0:PAST], qblk[:, s_, gp, :], keys, start=True, stop=True)
                    mm = nc.tensor.matmul(ps[rows, v % 2, PAST:NKEY], qblk[:, s_, gp, :], KTm[:, br - 1, gp, NP_:T],
                                          start=True, stop=True)
                mm.then_inc(ss_done, 1)

            def sample_transpose(v):
                br = sample_unit(v)[2]
                pe.wait_ge(ss_step, 3 * v + 3)
                if v >= 2:
                    pe.wait_ge(ss_pt, v - 1)
                for k in range(1 if br == 0 else 2):
                    mm = nc.tensor.transpose(ps[:, 2 + v % 2, P * k:P * k + P], S[:, v % 4, P * k:P * k + P], ident[:])
                if br:
                    mm = nc.tensor.transpose(ps[0:NS_, 2 + v % 2, PAST:PAST + P], S[:, v % 4, PAST:NKEY], ident[:])
                mm.then_inc(ss_t, 1)

            def sample_pv(v):
                gp, sg, br = sample_unit(v)
                bank = 4 + 2 * gp + sg
                pe.wait_ge(ss_pt, v + 1)
                if v == 0:
                    pe.wait_ge(og, 16)
                    pe.wait_ge(pt_kept, 128)
                if br == 0:
                    mm = nc.tensor.matmul(ps[:, bank, 0:P], vcs[:, gp * P:(gp + 1) * P], PT[:, v % 2, 0:P],
                                          start=True, stop=False)
                else:
                    for q in range(4):
                        s_ = 4 * sg + q
                        for c in range(2):
                            vals = (cache_sel[:, s_, c, PAST + gp * P:PAST + gp * P + P] if br == 1
                                    else cache_win[:, s_, (2 + c) * PAST + gp * P:(2 + c) * PAST + gp * P + P])
                            nc.tensor.matmul(ps[:, bank, 32 * q:32 * q + 32], vals,
                                             PT[:, v % 2, P * c + 32 * q:P * c + 32 * q + 32], start=False, stop=False)
                    vnew = (br - 1) * GROUPS * HD + gp * P
                    mm = nc.tensor.matmul(ps[:, bank, 0:P], V[0:NS_, 4, vnew:vnew + P], PT[0:NS_, v % 2, PAST:PAST + P],
                                          start=False, stop=(br == 2))
                mm.then_inc(ss_pv, 1)

            for v in range(12 + 3):
                if v < 12:
                    sample_scores(v)
                if 2 <= v < 14:
                    sample_transpose(v - 2)
                if v >= 3:
                    sample_pv(v - 3)

            for n in range(KT):
                pair = 2 + n % 2
                pe.wait_ge(wO_in[n % 2], 16 * (n // 2 + 1))
                if n == 0:
                    pe.wait_ge(og, 16)
                    pe.wait_ge(og_sample, 4)
                if n >= 2:
                    pe.wait_ge(x2_added, n - 1)
                for k in range(KT):
                    for dst, cols in halves(pair):
                        mm = nc.tensor.matmul(dst, ringE[:, n % 2, k, :], ZT[:, k, cols],
                                              start=(k == 0), stop=(k == KT - 1))
                mm.then_inc(out2_done, 1)
            for k in range(KT):
                pe.wait_ge(squared, 2 * KT + CT + k + 1)
                for dst, cols in halves(0):
                    mm = nc.tensor.matmul(dst, ones[:], sq[:, k % 2, cols], start=(k == 0), stop=(k == KT - 1))
                mm.then_inc(sq_summed, 1)

        @block.scalar
        def _(act):
            act.wait_ge(x_in, 16)
            for k in range(KT):
                if k >= 2:
                    act.wait_ge(sq_summed, k - 1)
                nc.scalar.activation(sq[:, k % 2, :], X[:, k, :], ACT.Square).then_inc(squared, 1)
            act.wait_ge(inv_var, 1)
            nc.scalar.activation(rstd[:], rstd[:], ACT.Sqrt).then_inc(rstd_ready, 1)

            def tile(c, par):
                act.wait_ge(gate_done, c + 1)
                if reaches(c, 2):
                    act.wait_ge(v_ready, 2 * c - 2)
                nc.scalar.activation(sig[:, par, 0:NP_].rearrange("p (b t) -> p b t", b=2), prompt_of(0), ACT.Sigmoid)
                nc.scalar.activation(sig[:, par, NP_:T], sample_of(0), ACT.Sigmoid).then_inc(sig_ready, 1)
                act.wait_ge(v_ready, 2 * c + 2)
                nc.scalar.activation(ctail[:, c, :], VP[:, par, NP_:NP_ + STATE], ACT.Copy).then_inc(tail_kept, 1)
                act.wait_ge(z_done, c + 1)
                nc.scalar.activation(Z1[:, c, 0:NP_].rearrange("p (b t) -> p b t", b=2), prompt_of(2), ACT.Silu)
                nc.scalar.activation(Z1[:, c, NP_:T], sample_of(2), ACT.Silu).then_inc(z_kept, 1)

            tile(0, 0)
            tile(1, 1)
            with act.Fori(1, CT // 2) as j:
                tile(2 * j, 0)
                tile(2 * j + 1, 1)

            act.wait_ge(z_kept, CT)
            for c in range(CT):
                act.wait_ge(centered, c + 1)
                if c >= 2:
                    act.wait_ge(sq_summed, KT + c - 1)
                nc.scalar.activation(sq[:, c % 2, :], C[:, c, :], ACT.Square).then_inc(squared, 1)
            for n in range(2):
                act.wait_ge(wC_in[n], 16)
                nc.scalar.activation(ringCh[:, n], ringC[:, n], ACT.Copy).then_inc(wCh_ready, 1)
            act.wait_ge(inv_var, 2)
            nc.scalar.activation(rstd[:], rstd[:], ACT.Sqrt).then_inc(rstd_ready, 1)
            act.wait_ge(consts_in, 48)

            def high_wC(n):
                if n >= 2:
                    act.wait_ge(out1_done, n - 1)
                act.wait_ge(wC_in[n % 2], 16 * (n // 2 + 1))
                nc.scalar.activation(ringCh[:, n % 2], ringC[:, n % 2], ACT.Copy).then_inc(wCh_ready, 1)

            for c in range(CT + 1):
                if c < CT:
                    act.wait_ge(scaled, c + 1)
                    nc.scalar.activation(C[:, c, :], C[:, c, :], ACT.Silu, scale=lng[:, c:c + 1],
                                         bias=lnb[:, c:c + 1]).then_inc(activated, 1)
                if c >= 1:
                    act.wait_ge(c_gated, c)
                    nc.scalar.activation(Ch[:, c - 1, :], C[:, c - 1, :], ACT.Copy).then_inc(ch_ready, 1)
            for n in range(2, KT):
                high_wC(n)

            def square_x(added, done):
                for k in range(KT):
                    act.wait_ge(added, k + 1)
                    act.wait_ge(sq_summed, done + k - 1)
                    nc.scalar.activation(sq[:, k % 2, :], X[:, k, :], ACT.Square).then_inc(squared, 1)

            square_x(x_added, KT + CT)
            act.wait_ge(inv_var, 3)
            nc.scalar.activation(rstd[:], rstd[:], ACT.Sqrt).then_inc(rstd_ready, 1)
            for i in range(5):
                rows = min(P, T - i * P)
                act.wait_ge(tok_done, i + 1)
                nc.scalar.activation(V[0:rows, i, :].rearrange("p (b n) -> p b n", b=2),
                                     ps[0:rows, 2 * (i % 4):2 * (i % 4) + 2, 0:VH], ACT.Copy).then_inc(v_kept, 1)
            act.wait_ge(v_kept, 5)
            logits = V[:, 0:4, 2 * GROUPS * HD:VTOK].rearrange("p t (h b) -> p t h b", b=3)
            nc.scalar.activation(gates_c[:], logits[:, :, :, 0], ACT.Sigmoid)
            nc.scalar.activation(gates_sw[:].rearrange("p t (h b) -> p t h b", b=2), logits[:, :, :, 1:3],
                                 ACT.Sigmoid).then_inc(gates_ready, 1)
            act.wait_ge(grow_kept, 3)
            nc.scalar.activation(grow[:], grow[:], ACT.Sigmoid).then_inc(grow_ready, 1)
            act.wait_ge(hid_done, 2)
            act.wait_ge(pe_kept, 1)
            for kv in range(2):
                nc.scalar.activation(hp[:, kv, :, 0:NCP],
                                     ps[:, kv, 0:GROUPS * NCP].rearrange("p (g c) -> p g c", g=GROUPS),
                                     ACT.Silu, bias=pe_hid[:, kv:kv + 1]).then_inc(hid_ready, 1)
                nc.scalar.activation(hs[:, kv].rearrange("p g (s c) -> p (g s) c", c=16)[:, :, 0:NCS],
                                     ps[:, 4 + kv, 0:SEQS * GROUPS * NCS].rearrange("p (g c) -> p g c", c=NCS),
                                     ACT.Silu, bias=pe_hid[:, kv:kv + 1]).then_inc(hid_ready, 1)
            for i in range(FT_Q):
                pair = 3 if i % 2 else 1
                act.wait_ge(f_done, FT_KV + i + 1)
                nc.scalar.activation(split(QT[:, i, 0:NP_]), prompt_of(pair), ACT.Copy, scale=HD ** -0.5)
                nc.scalar.activation(QT[:, i, NP_:T], sample_of(pair), ACT.Copy, scale=HD ** -0.5).then_inc(q_kept, 1)

            def z_tile(i):
                act.wait_ge(f_done, FT_KV + FT_Q + i + 1)
                nc.scalar.activation(split(ZT[:, i, 0:NP_]), prompt_of(i % 2), ACT.Silu)
                nc.scalar.activation(ZT[:, i, NP_:T], sample_of(i % 2), ACT.Silu).then_inc(zt_ready, 1)

            for t in range(4):
                act.wait_ge(cs_step, 9 * t + 4)
                nc.scalar.activation(S[:, 0, :], S[:, 0, :], ACT.Exp).then_inc(cs_exp, 1)
                z_tile(2 * t)
                z_tile(2 * t + 1)
                act.wait_ge(cs_t, t + 1)
                nc.scalar.activation(PCT[:, :, P * t:P * t + P].rearrange("p (a j) q -> p a j q", a=2),
                                     ps[0:HD, 6:8, :].rearrange("p a (j q) -> p a j q", j=4), ACT.Copy).then_inc(cs_kept, 1)

            def exp(i, u):
                n = (u % 4 + 1) * P
                act.wait_ge(sc_ready, 16 * i + u + 1)
                w = weights_at(u)[:, 0:n]
                nc.scalar.activation(w, w, ACT.Exp, scale=-1.0, bias=nmax[:, u:u + 1],
                                     accum_out=rsum[:, u:u + 1]).then_inc(exp_ready, 1)

            def copy_weights(i, u):
                turn, t = u // 4 % 2, u % 4
                act.wait_ge(t_done, 16 * i + u + 1)
                if t == 0 and (u >= 8 or reaches(i, 1)):
                    act.wait_ge(pv_done, 4 * i + u // 4 - 1)
                nc.scalar.activation(PTB[:, turn, 0:t + 1, P * t:P * t + P],
                                     ps[:, 4 + u % 2, 0:(t + 1) * P].rearrange("p (k q) -> p k q", q=P),
                                     ACT.Copy).then_inc(pt_kept, 1)

            def attend(i):
                for u in range(16):
                    if u >= 4:
                        copy_weights(i, u - 4)
                    elif reaches(i, 1):
                        copy_weights(i - 1, u + 12)
                    exp(i, u)

            attend(0)
            with act.Fori(1, 8) as i:
                attend(i)
            for u in range(12, 16):
                copy_weights(7, u)

            for v in range(12):
                n = NKEY if sample_unit(v)[2] else P
                act.wait_ge(ss_ready, v + 1)
                nc.scalar.activation(S[:, v % 4, 0:n], S[:, v % 4, 0:n], ACT.Exp, scale=-1.0, bias=nmax[:, v:v + 1],
                                     accum_out=rsum[:, v:v + 1]).then_inc(ss_exp, 1)
            square_x(x2_added, 2 * KT + CT)
            act.wait_ge(inv_var, 4)
            nc.scalar.activation(rstd[:], rstd[:], ACT.Sqrt).then_inc(rstd_ready, 1)

        @block.vector
        def _(dve):
            nc.vector.memset(ones[:], 1.0).then_inc(ones_set, 1)
            nc.vector.memset(VP[:, :, 0:STATE], 0.0).then_inc(pads_set, 1)

            def inverse_variance(pair, count, n):
                nc.vector.tensor_scalar(rstd[:, 0:NP_].rearrange("p (b t) -> p b t", b=2), prompt_of(pair),
                                        1.0 / count, EPS, ALU.mult, ALU.add)
                nc.vector.tensor_scalar(rstd[:, NP_:T], sample_of(pair), 1.0 / count, EPS,
                                        ALU.mult, ALU.add).then_inc(mean_sq, 1)
                dve.wait_ge(mean_sq, n)
                nc.vector.reciprocal(rstd[:], rstd[:]).then_inc(inv_var, 1)

            dve.wait_ge(sq_summed, KT)
            inverse_variance(3, D, 1)
            dve.wait_ge(rstd_ready, 1)
            dve.wait_ge(gains_in, 16)
            for k in range(KT):
                nc.vector.scalar_tensor_tensor(H[:, k, :], X[:, k, :], gains[:, 0, k:k + 1], rstd[:],
                                               ALU.mult, ALU.mult).then_inc(h_ready, 1)
            dve.wait_ge(taps_in, 16)
            dve.wait_ge(state_in, 16)
            dve.wait_ge(pads_set, 1)

            def tile(c, par):
                if reaches(c, 2):
                    dve.wait_ge(pool_step, 7 * c - 7)
                nc.vector.tensor_copy(tapc[:, par, :], taps[:, c, :]).then_inc(tap_set, 1)
                dve.wait_ge(sig_ready, c + 1)
                dve.wait_ge(lin_done, c + 1)
                if reaches(c, 2):
                    dve.wait_ge(tail_kept, c - 1)
                nc.vector.tensor_tensor(VP[:, par, STATE:].rearrange("p (b t) -> p b t", b=2), prompt_of(1),
                                        sig[:, par, 0:NP_].rearrange("p (b t) -> p b t", b=2),
                                        ALU.mult).then_inc(v_ready, 1)
                nc.vector.tensor_tensor(VS[:, c, :, STATE:], sample_of(1).rearrange("p (s t) -> p s t", s=SEQS),
                                        sig[:, par, NP_:T].rearrange("p (s t) -> p s t", s=SEQS),
                                        ALU.mult).then_inc(v_ready, 1)
                dve.wait_ge(tap_set, c + 1)
                dve.wait_ge(v_ready, 2 * c + 1)
                for k in range(TAPS):
                    src, w = VP[:, par, k:k + NP_], tapc[:, par, k:k + 1]
                    if k == 0:
                        op = nc.vector.tensor_scalar(acc[:, 0, :], src, w, tapc[:, par, TAPS:TAPS + 1], ALU.mult, ALU.add)
                    elif k == 1:
                        op = nc.vector.tensor_scalar(acc[:, 1, :], src, w, None, ALU.mult)
                    else:
                        dve.wait_ge(conv_step, 32 * c + k - 1)
                        op = nc.vector.scalar_tensor_tensor(acc[:, k % 2, :], src, w, acc[:, k % 2, :], ALU.mult, ALU.add)
                    op.then_inc(conv_step, 1)
                dve.wait_ge(conv_step, 32 * c + TAPS)
                nc.vector.tensor_tensor(C[:, c, 0:NP_], acc[:, 0, :], acc[:, 1, :], ALU.add).then_inc(conv_step, 1)
                dve.wait_ge(conv_step, 32 * c + 32)

            tile(0, 0)
            tile(1, 1)
            with dve.Fori(1, CT // 2) as j:
                tile(2 * j, 0)
                tile(2 * j + 1, 1)

            dve.wait_ge(c_summed, CT)
            nc.vector.tensor_scalar(mean[:, 0:NP_].rearrange("p (b t) -> p b t", b=2), prompt_of(3),
                                    1.0 / DC, None, ALU.mult)
            nc.vector.tensor_scalar(mean[:, NP_:T], sample_of(3), 1.0 / DC, None, ALU.mult).then_inc(mean_ready, 1)
            dve.wait_ge(mean_ready, 1)
            dve.wait_ge(pool_step, 7 * CT)
            for c in range(CT):
                nc.vector.tensor_tensor(C[:, c, :], C[:, c, :], mean[:], ALU.subtract).then_inc(centered, 1)
            for n in range(2):
                dve.wait_ge(wCh_ready, n + 1)
                nc.vector.tensor_tensor(ringCl[:, n], ringC[:, n], ringCh[:, n].bitcast(F32),
                                        ALU.subtract).then_inc(wCl_ready, 1)
            dve.wait_ge(sq_summed, KT + CT)
            inverse_variance(0, DC, 2)
            dve.wait_ge(rstd_ready, 2)
            dve.wait_ge(squared, KT + CT)

            def scale(c):
                nc.vector.tensor_tensor(C[:, c, :], C[:, c, :], rstd[:], ALU.mult).then_inc(scaled, 1)

            scale(0)
            scale(1)
            for c in range(CT + 1):
                if c + 2 < CT:
                    scale(c + 2)
                if c < CT:
                    dve.wait_ge(activated, c + 1)
                    nc.vector.tensor_tensor(C[:, c, :], C[:, c, :], Z1[:, c, :], ALU.mult).then_inc(c_gated, 1)
                if c >= 1:
                    dve.wait_ge(ch_ready, c)
                    nc.vector.tensor_tensor(Cl[:, c - 1, :], C[:, c - 1, :], Ch[:, c - 1, :].bitcast(F32),
                                            ALU.subtract).then_inc(cl_ready, 1)

            def low_wC(n):
                dve.wait_ge(wCh_ready, n + 1)
                nc.vector.tensor_tensor(ringCl[:, n % 2], ringC[:, n % 2], ringCh[:, n % 2].bitcast(F32),
                                        ALU.subtract).then_inc(wCl_ready, 1)

            for n in range(KT):
                if n + 2 < KT:
                    low_wC(n + 2)
                dve.wait_ge(out1_done, n + 1)
                nc.vector.tensor_tensor(X[:, n, 0:NP_].rearrange("p (b t) -> p b t", b=2), prompt_of(1 + n % 3),
                                        X[:, n, 0:NP_].rearrange("p (b t) -> p b t", b=2), ALU.add)
                nc.vector.tensor_tensor(X[:, n, NP_:T], sample_of(1 + n % 3), X[:, n, NP_:T],
                                        ALU.add).then_inc(x_added, 1)

            dve.wait_ge(sq_summed, 2 * KT + CT)
            inverse_variance(3, D, 3)
            dve.wait_ge(rstd_ready, 3)
            dve.wait_ge(x_added, KT)
            for k in range(KT):
                nc.vector.scalar_tensor_tensor(H[:, k, :], X[:, k, :], gains[:, 1, k:k + 1], rstd[:],
                                               ALU.mult, ALU.mult).then_inc(h2_ready, 1)
            for n in range(FT_KV):
                dve.wait_ge(f_done, n + 1)
                if n < 4:
                    kv, gp = divmod(n, 2)
                    for r in range(2):
                        for par in range(2):
                            nc.vector.tensor_copy(split(KK[HD * par:HD * par + HD, kv, 2 * gp + r, :]),
                                                  ps[HD * r:HD * r + HD, 2 * n:2 * n + 2, par:TA:2])
                    nc.vector.tensor_copy(KN[:, n, :], sample_of(n)).then_inc(kv_kept, 1)
                else:
                    b, gp = divmod(n - 4, 2)
                    nc.vector.tensor_copy(split(KTm[:, b, gp, 0:NP_]), prompt_of(n % 4))
                    nc.vector.tensor_copy(KTm[:, b, gp, NP_:T], sample_of(n % 4)).then_inc(kv_kept, 1)
            dve.wait_ge(small_in, 96)
            dve.wait_ge(grow_done, 1)
            for sg in range(2):
                nc.vector.tensor_tensor(gtmp[:, sg], ps[:, 2 + sg:3 + sg, 0:GL].to_broadcast([P, 2, GL]), headsel[:],
                                        ALU.mult).then_inc(grow_kept, 1)
            dve.wait_ge(grow_kept, 2)
            nc.vector.tensor_reduce(grow[:].rearrange("p a g b -> p (a g) b"),
                                    gtmp[:].rearrange("p a g (h b) -> p (a g) b h", b=3), AX.X, ALU.add).then_inc(grow_kept, 1)
            dve.wait_ge(hid_done, 2)
            nc.vector.tensor_copy(pe_hid[:], ps[:, 6:8, 0]).then_inc(pe_kept, 1)
            dve.wait_ge(comp_done, 1)
            dve.wait_ge(zeros_set, 1)
            nc.vector.tensor_copy(kcp[:], ps[:, 0, 0:64].rearrange("p (g c) -> p g c", g=2)).then_inc(comp_kept, 1)
            nc.vector.tensor_copy(kcs[:], ps[:, 1, 0:2 * P].rearrange("p (g c) -> p g c", g=2)).then_inc(comp_kept, 1)
            for r in range(2):
                rows = slice(32 * r, 32 * r + 32)
                op = nc.vector.tensor_copy(vcd[rows, :, HD * r:HD * r + HD],
                                           ps[rows, 4, 0:2 * HD].rearrange("p (g d) -> p g d", g=2))
            op.then_inc(comp_kept, 1)
            nc.vector.tensor_copy(vcs[:], ps[:, 5, 0:GROUPS * HD]).then_inc(comp_kept, 1)
            dve.wait_ge(q_kept, FT_Q)
            for gp in range(2):
                for r in range(2):
                    rows = slice(HD * r, HD * r + HD)
                    for j in range(HPG):
                        op = nc.vector.tensor_copy(qblk[rows, :, gp, 16 * r + 4 * j:16 * r + 4 * j + 4],
                                                   QT[rows, HPG * gp + j, NP_:T].rearrange("p (s t) -> p s t", s=SEQS))
            op.then_inc(qblk_ready, 1)

            dve.wait_ge(kk_stored, 16)
            dve.wait_ge(cbias_in, 16)
            dve.wait_ge(gates_ready, 1)
            Sh = S[:, 0, :].rearrange("p (h c) -> p h c", h=HEADS)
            for t in range(4):
                dve.wait_ge(cs_done, t + 1)
                if t >= 1:
                    dve.wait_ge(cs_t, t)
                nc.vector.tensor_tensor(S[:, 0, :].rearrange("p (i r c) -> p r i c", r=2, c=32),
                                        ps[:, 4:6, 0:2 * P].rearrange("p r (i c) -> p r i c", c=32),
                                        cbias[:, t, :].rearrange("p (i r c) -> p r i c", r=2, c=32), ALU.add).then_inc(cs_step, 1)
                dve.wait_ge(cs_step, 9 * t + 1)
                nc.vector.tensor_reduce(m16[:], Sh, AX.X, ALU.max).then_inc(cs_step, 1)
                dve.wait_ge(cs_step, 9 * t + 2)
                nc.vector.tensor_scalar(m16[:], m16[:], FLOOR, None, ALU.max).then_inc(cs_step, 1)
                dve.wait_ge(cs_step, 9 * t + 3)
                nc.vector.tensor_tensor(Sh, Sh, m16[:].unsqueeze(2).to_broadcast([P, HEADS, 32]),
                                        ALU.subtract).then_inc(cs_step, 1)
                dve.wait_ge(cs_exp, t + 1)
                nc.vector.tensor_reduce(s16[:], Sh, AX.X, ALU.add).then_inc(cs_step, 1)
                dve.wait_ge(cs_step, 9 * t + 5)
                nc.vector.tensor_scalar(s16[:], s16[:], 1e-30, None, ALU.max).then_inc(cs_step, 1)
                dve.wait_ge(cs_step, 9 * t + 6)
                nc.vector.reciprocal(s16[:], s16[:]).then_inc(cs_step, 1)
                dve.wait_ge(cs_step, 9 * t + 7)
                nc.vector.tensor_tensor(s16[:], s16[:], gates_c[:, t, :], ALU.mult).then_inc(cs_step, 1)
                dve.wait_ge(cs_step, 9 * t + 8)
                nc.vector.tensor_tensor(Sh, Sh, s16[:].unsqueeze(2).to_broadcast([P, HEADS, 32]),
                                        ALU.mult).then_inc(cs_step, 1)

            dve.wait_ge(cs_t, 4)

            def score(i, u):
                r, n = u // 8, (u % 4 + 1) * P
                if u % 8 == 0:
                    dve.wait_ge(bias_set, 2 * i + r + 1)
                dve.wait_ge(qk_done, 16 * i + u + 1)
                if u >= 8 or reaches(i, 1):
                    dve.wait_ge(t_done, 16 * i + u - 7)
                nc.vector.memset(tick[:, u:u + 1], 0.0)
                nc.vector.tensor_tensor_reduce(weights_at(u)[:, 0:n], ps[:, u % 4, 0:n], bias[:, r, NP_ - n:NP_], -1.0, 3e38,
                                               ALU.add, ALU.min, nmax[:, u:u + 1]).then_inc(sc_ready, 1)

            def invert(i, u):
                dve.wait_ge(exp_ready, 16 * i + u + 1)
                nc.vector.reciprocal(gsc[:, u:u + 1], rsum[:, u:u + 1]).then_inc(inv_ready, 1)

            def normalize(i, u):
                r, b, t = u // 8, u % 8 // 4, u % 4
                if u == 0:
                    dve.wait_ge(gate_set, i + 1)
                dve.wait_ge(inv_ready, 16 * i + u + 1)
                w = weights_at(u)[:, 0:(t + 1) * P]
                nc.vector.tensor_scalar(w, w, gsc[:, u:u + 1], gpair[:, t, r, b:b + 1],
                                        ALU.mult, ALU.mult).then_inc(p_ready, 1)

            def set_gates(i):
                if reaches(i, 1):
                    dve.wait_ge(p_ready, 16 * i)
                nc.vector.tensor_copy(gpair[:].rearrange("p t r b -> p t (r b)"), gates_sw[:, :, bass.ds(4 * i, 4)]).then_inc(gate_set, 1)

            def gate_head(i, r):
                rows = slice(HD * r, HD * r + HD)
                dve.wait_ge(pv_done, 4 * i + 2 * r + 2)
                nc.vector.tensor_tensor(ZT[rows, i, 0:NP_], ps[rows, 6 + r, :], ZT[rows, i, 0:NP_], ALU.mult).then_inc(og, 1)

            def attend(i):
                for u in range(16):
                    score(i, u)
                    if u >= 2:
                        normalize(i, u - 2)
                    elif reaches(i, 1):
                        normalize(i - 1, u + 14)
                    if u >= 1:
                        invert(i, u - 1)
                    elif reaches(i, 1):
                        invert(i - 1, 15)
                    if u == 1:
                        set_gates(i)
                        if reaches(i, 1):
                            gate_head(i - 1, 0)
                    if u == 9 and reaches(i, 1):
                        gate_head(i - 1, 1)

            attend(0)
            with dve.Fori(1, 8) as i:
                attend(i)
            normalize(7, 14)
            invert(7, 15)
            normalize(7, 15)
            gate_head(7, 0)
            gate_head(7, 1)

            dve.wait_ge(sbias_in, 16)
            dve.wait_ge(grow_ready, 1)
            dve.wait_ge(t_done, 128)

            def sample_softmax_in(v):
                gp, sg, br = sample_unit(v)
                n, at_ = (P, NKEY) if br == 0 else (NKEY, 0)
                dve.wait_ge(ss_done, v + 1)
                if v >= 4:
                    dve.wait_ge(ss_t, v - 3)
                nc.vector.tensor_tensor_reduce(S[:, v % 4, 0:n], ps[:, v % 2, 0:n], sbias[:, gp, sg, at_:at_ + n], -1.0, 3e38,
                                               ALU.add, ALU.min, nmax[:, v:v + 1]).then_inc(ss_ready, 1)

            def sample_softmax_out(v):
                gp, sg, br = sample_unit(v)
                n = P if br == 0 else NKEY
                dve.wait_ge(ss_exp, v + 1)
                nc.vector.reciprocal(s16[:, v:v + 1], rsum[:, v:v + 1]).then_inc(ss_step, 1)
                dve.wait_ge(ss_step, 3 * v + 1)
                nc.vector.tensor_tensor(m16[:, v:v + 1], s16[:, v:v + 1], grow[:, sg, gp, br:br + 1], ALU.mult).then_inc(ss_step, 1)
                dve.wait_ge(ss_step, 3 * v + 2)
                nc.vector.tensor_scalar(S[:, v % 4, 0:n], S[:, v % 4, 0:n], m16[:, v:v + 1], None, ALU.mult).then_inc(ss_step, 1)

            def sample_copy(v):
                dve.wait_ge(ss_t, v + 1)
                if v >= 2:
                    dve.wait_ge(ss_pv, v - 1)
                if sample_unit(v)[2] == 0:
                    nc.vector.tensor_copy(PT[:, v % 2, 0:P], ps[:, 2 + v % 2, 0:P]).then_inc(ss_pt, 1)
                else:
                    nc.vector.tensor_copy(PT[:, v % 2, 0:PAST], ps[:, 2 + v % 2, 0:PAST])
                    nc.vector.tensor_copy(PT[0:NS_, v % 2, PAST:PAST + P], ps[0:NS_, 2 + v % 2, PAST:PAST + P]).then_inc(ss_pt, 1)

            def sample_gate(w):
                gp, sg = divmod(w, 2)
                dve.wait_ge(ss_pv, SAMPLE_WIN + w + 1)
                for r in range(2):
                    rows = slice(HD * r, HD * r + HD)
                    o4 = ps[rows, 4 + w, 0:P].rearrange("p (s r j t) -> p r j s t", s=4, r=2, j=HPG)
                    zt = ZT[rows, HPG * gp:HPG * gp + HPG, NP_ + 16 * sg:NP_ + 16 * sg + 16]
                    zt = zt.rearrange("p j (s t) -> p j s t", s=4)
                    op = nc.vector.tensor_tensor(zt, o4[:, r], zt, ALU.mult)
                op.then_inc(og_sample, 1)

            for v in range(12 + 3):
                if v < 12:
                    sample_softmax_in(v)
                if 1 <= v < 13:
                    sample_softmax_out(v - 1)
                if 2 <= v < 14:
                    sample_copy(v - 2)
                if v - 3 >= SAMPLE_WIN:
                    sample_gate(v - 3 - SAMPLE_WIN)

            for n in range(KT):
                dve.wait_ge(out2_done, n + 1)
                nc.vector.tensor_tensor(split(X[:, n, 0:NP_]), prompt_of(2 + n % 2), split(X[:, n, 0:NP_]), ALU.add)
                nc.vector.tensor_tensor(X[:, n, NP_:T], sample_of(2 + n % 2), X[:, n, NP_:T], ALU.add).then_inc(x2_added, 1)
            dve.wait_ge(sq_summed, 3 * KT + CT)
            inverse_variance(0, D, 4)
            dve.wait_ge(rstd_ready, 4)
            dve.wait_ge(x2_added, KT)
            for k in range(KT):
                nc.vector.scalar_tensor_tensor(Y[:, k, :], X[:, k, :], gains[:, 2, k:k + 1], rstd[:],
                                               ALU.mult, ALU.mult).then_inc(y_ready, 1)

        @block.gpsimd
        def _(pool):
            def tile(c, par):
                pool.wait_ge(v_ready, 2 * c + 2)
                pool.wait_ge(tap_set, c + 1)
                if reaches(c, 1):
                    pool.wait_ge(pool_step, 7 * c)
                for s0 in range(STEPS):
                    win = VS[:, c, :, s0:s0 + TAPS].rearrange("p s k -> p k s")
                    dst = prod[:, 0:TAPS, s0:NS_:STEPS]
                    w = tapc[:, par, 0:TAPS].unsqueeze(2).to_broadcast([P, TAPS, SEQS])
                    op = nc.gpsimd.tensor_tensor(dst, win, w, ALU.mult)
                op.then_inc(pool_step, 1)
                nc.gpsimd.tensor_tensor(prod[:, TAPS, :], ones[:, 0:NS_],
                                        tapc[:, par, TAPS:TAPS + 1].to_broadcast([P, NS_]), ALU.mult).then_inc(pool_step, 1)
                for i, n in enumerate((16, 8, 4, 2)):
                    pool.wait_ge(pool_step, 7 * c + 2 + i)
                    nc.gpsimd.tensor_tensor(prod[:, 0:n, :], prod[:, 0:n, :], prod[:, n:2 * n, :],
                                            ALU.add).then_inc(pool_step, 1)
                pool.wait_ge(pool_step, 7 * c + 6)
                nc.gpsimd.tensor_tensor(C[:, c, NP_:T], prod[:, 0, :], prod[:, 1, :], ALU.add).then_inc(pool_step, 1)

            pool.wait_ge(ones_set, 1)
            pool.wait_ge(state_in, 16)
            tile(0, 0)
            tile(1, 1)
            with pool.Fori(1, CT // 2) as j:
                tile(2 * j, 0)
                tile(2 * j + 1, 1)

            pool.wait_ge(h2_ready, KT)
            nc.gpsimd.memset(hp[:, :, :, NCP:32], 0.0)
            nc.gpsimd.memset(hs[:].rearrange("p v g (s c) -> p (v g s) c", c=16)[:, :, NCS:16], 0.0).then_inc(pads2_set, 1)
            pool.wait_ge(store_p, 16)
            pool.wait_ge(conv_step, 32 * CT)
            nc.gpsimd.memset(vcd[:], 0.0)
            nc.gpsimd.memset(qblk[:], 0.0).then_inc(zeros_set, 1)
            pool.wait_ge(small_in, 96)
            pool.wait_ge(q_kept, FT_Q)
            pool.wait_ge(grow_kept, 3)
            pool.wait_ge(cs_kept, 4)

            def head(i, r):
                rows = slice(HD * r, HD * r + HD)
                if reaches(i, 1):
                    pool.wait_ge(qk_done, 16 * i + 8 * r - 8)
                if r or reaches(i, 1):
                    pool.wait_ge(bias_set, 2 * i + r)
                nc.gpsimd.tensor_copy(qb[rows, :], QT[rows, i, 0:NP_]).then_inc(qb_set, 1)
                if reaches(i, 1):
                    pool.wait_ge(sc_ready, 16 * i + 8 * r - 8)
                pool.wait_ge(qb_set, 2 * i + r + 1)
                nc.gpsimd.tensor_tensor(bias[:, r, :], dist[:], slopes[:, i, r:r + 1].to_broadcast([P, NP_]),
                                        ALU.mult).then_inc(bias_set, 1)

            def compressed(i):
                if reaches(i, 1):
                    pool.wait_ge(pv_done, 4 * i - 1)
                pool.wait_ge(bias_set, 2 * i + 2)
                nc.gpsimd.tensor_copy(PT[0:HD, 0, :], PCT[:, i, :]).then_inc(pc_set, 1)

            def step(i):
                head(i, 0)
                head(i, 1)
                compressed(i)

            step(0)
            with pool.Fori(1, 8) as i:
                step(i)


def feature_major(xp, xs):
    x = np.concatenate([xp.reshape(NP_, D), xs.reshape(NS_, D)], axis=0)
    return np.ascontiguousarray(x.T.reshape(KT, P, T).transpose(1, 0, 2))


def by_partition(v, n):
    return np.ascontiguousarray(v.reshape(n, P).T)


def shape_constants():
    out = {}
    slope = np.exp2(-8.0 * np.arange(1, HEADS + 1) / HEADS).astype(np.float32)
    by_step = np.array([[slope[8 * (i // 4) + 4 * r + i % 4] for r in range(2)] for i in range(8)], np.float32)
    out["slopes"] = np.ascontiguousarray(np.broadcast_to(by_step, (P, 8, 2)))
    q, k = np.arange(P)[:, None], np.arange(NP_)[None, :] - (NP_ - P)
    out["dist"] = np.where(k <= q, k - q, NEG).astype(np.float32)
    q = (np.arange(4) * P)[None, :, None, None] + np.arange(P)[:, None, None, None]
    blk = np.arange(32)[None, None, None, :]
    d = q - (blk * CSTRIDE + CBLK - 1)
    cb = np.where((d >= 0) & (blk < NCP), -by_step.reshape(1, 1, HEADS, 1) * d, NEG)
    out["cbias"] = np.ascontiguousarray(cb.reshape(P, 4, HEADS * 32).astype(np.float32))
    q_, r, j, t = np.unravel_index(np.arange(P), (4, 2, HPG, STEPS))
    sb = np.full((P, 2, 2, NKEY + P), NEG, np.float32)
    sel = np.zeros((P, 2, HEADS, 3), np.float32)
    for gp in range(2):
        head = HPG * (2 * gp + r) + j
        sel[np.arange(P), gp, 2 * (HPG * gp + j) + r] = 1.0
        m = slope[head][:, None]
        for sg in range(2):
            seq = (4 * sg + q_)[:, None]
            sb[:, gp, sg, :PAST] = m * (np.arange(PAST)[None] - PAST - t[:, None])
            s_new, t_new = np.divmod(np.arange(NS_)[None], STEPS)
            sb[:, gp, sg, PAST:NKEY] = np.where((s_new == seq) & (t_new <= t[:, None]), m * (t_new - t[:, None]), NEG)
            s_c, c = np.divmod(np.arange(P)[None], 16)
            sb[:, gp, sg, NKEY:] = np.where((s_c == seq) & (c < NCS), m * (c * CSTRIDE + CBLK - 1 - PAST - t[:, None]), NEG)
    row = np.zeros((NS_, 2, P), np.float32)
    for sg in range(2):
        row[STEPS * (4 * sg + q_) + t, sg, np.arange(P)] = 1.0
    out["rowsel"] = row
    out["sbias"], out["headsel"] = sb, sel.reshape(P, 2, GL)
    return out


def kernel(x_prompt, x_sample, cache_kv, state_kv_win, state_conv, page_table, norm_g, final_norm_g,
           conv_w_in, conv_dw_w, conv_dw_b, conv_ln_g, conv_ln_b, conv_w_out,
           nsa_w_in, nsa_w_out, nsa_cmp_pe, nsa_cmp_w1, nsa_cmp_w2):
    import concourse.bacc as bacc
    from concourse.bass_utils import run_bass_kernel_spmd

    A = np.asarray
    arrays = {}
    arrays["x"] = feature_major(A(x_prompt), A(x_sample))
    g = np.concatenate([A(norm_g), A(final_norm_g)[None]], axis=0)
    arrays["gains"] = np.ascontiguousarray(g.reshape(3, KT, P).transpose(2, 0, 1))
    w = A(conv_w_in)[0].reshape(KT, P, 3, CT, P)[:, :, [1, 0, 2]]
    arrays["w_a"] = np.ascontiguousarray(w.transpose(3, 1, 2, 0, 4))
    taps = np.concatenate([A(conv_dw_w)[0], A(conv_dw_b)], axis=0)
    arrays["taps"] = np.ascontiguousarray(taps.reshape(32, CT, P).transpose(2, 1, 0))
    state = A(state_conv)[0].reshape(SEQS, STATE, CT, P).transpose(3, 2, 0, 1)
    arrays["state"] = np.ascontiguousarray(np.pad(state, ((0, 0), (0, 0), (0, 0), (0, STEPS))))
    arrays["ident"] = np.eye(P, dtype=np.float32)
    arrays["lng"] = by_partition(A(conv_ln_g)[0], CT)
    arrays["lnb"] = by_partition(A(conv_ln_b)[0], CT)
    arrays["w_c"] = np.ascontiguousarray(A(conv_w_out)[0].reshape(CT, P, KT, P).transpose(2, 1, 0, 3))
    w = A(nsa_w_in)[0]
    wq, wz, wkv, wgl = np.split(w, [D, 2 * D, 2 * D + 6 * GROUPS * HD], axis=1)
    def by_pairs(w, width):
        return w.reshape(-1, 2, 2, HPG, width).transpose(0, 1, 3, 2, 4).reshape(-1, HEADS * width)

    wq, wz, wgl = by_pairs(wq, HD), by_pairs(wz, HD), by_pairs(wgl, 3)
    wkv = wkv.reshape(D, 6, GROUPS * HD)
    w_f = np.concatenate([wkv[:, 0], wkv[:, 1], wkv[:, 2], wkv[:, 4], wq, wz], axis=1)
    arrays["w_f"] = np.ascontiguousarray(w_f.reshape(KT, P, FT, P).transpose(2, 1, 0, 3))
    w_t = np.concatenate([wkv[:, 3], wkv[:, 5], wgl], axis=1)
    arrays["w_t"] = np.ascontiguousarray(w_t.reshape(KT, P, VTOK).transpose(1, 0, 2))
    w_o = by_pairs(A(nsa_w_out)[0].T, HD).T
    arrays["w_o"] = np.ascontiguousarray(w_o.reshape(KT, P, KT, P).transpose(2, 1, 0, 3))
    arrays["w1"] = np.ascontiguousarray(A(nsa_cmp_w1)[0].reshape(2, CBLK // 2, P, P).transpose(2, 0, 1, 3))
    arrays["w2"] = np.ascontiguousarray(A(nsa_cmp_w2)[0].transpose(1, 0, 2))
    arrays["pe"] = np.ascontiguousarray(A(nsa_cmp_pe)[0].reshape(2, CBLK // 2, P).transpose(2, 0, 1))
    cache = A(cache_kv)[0]
    pool = cache.shape[0]
    c01 = cache[:, :, 0:2].reshape(pool, SEL, 2, 2, GROUPS, HD)
    arrays["cache_cmp"] = np.ascontiguousarray(c01.transpose(0, 2, 5, 3, 4, 1).reshape(pool, P, 2, GROUPS, SEL))
    k2 = cache[:, :, 2].reshape(pool, PAGE, 2, 2, HD).transpose(0, 3, 4, 2, 1).reshape(pool, P, 2 * P)
    arrays["cache_sel"] = np.ascontiguousarray(np.concatenate([k2, cache[:, :, 3].reshape(pool, P, 2 * P)], axis=2))
    win = A(state_kv_win)[0]
    kw = win[:, :, 0].reshape(SEQS, PAST, 2, 2, HD).transpose(3, 4, 0, 2, 1).reshape(P, SEQS, 2 * PAST)
    vw = win[:, :, 1].reshape(SEQS, 2, P, GROUPS * HD).transpose(2, 0, 1, 3).reshape(P, SEQS, 2 * PAST)
    arrays["cache_win"] = np.ascontiguousarray(np.concatenate([kw, vw], axis=2))
    arrays["win_state"] = np.ascontiguousarray(win[:, STEPS:].reshape(SEQS, -1))
    arrays["pages"] = np.ascontiguousarray(A(page_table).reshape(1, SEQS * NPG).astype(np.int32))
    arrays.update(shape_constants())
    outs = {"y": (P, KT, T), "conv_p": (P, CT, STATE), "conv_s": (P, CT, SEQS, STATE + STEPS),
            "kv_cmp": (P, 2, GROUPS, NP_ // 2), "kv_cmp_s": (P, 4, NS_), "k_new": (P, 2, 2, T),
            "v_new": (P, 5, 2 * GROUPS * HD), "win_s": (SEQS, (PAST - STEPS) * 2 * GROUPS * HD)}

    nc = bacc.Bacc("TRN2", target_bir_lowering=False, num_devices=1)
    io = {}
    for n, a in arrays.items():
        io[n] = nc.dram_tensor(f"in_{n}", a.shape, mybir.dt.from_np(a.dtype), kind="ExternalInput").ap()
    for n, shape in outs.items():
        io[n] = nc.dram_tensor(f"out_{n}", shape, F32, kind="ExternalOutput").ap()
    build(nc, io)
    r = run_bass_kernel_spmd(nc, [{f"in_{n}": a for n, a in arrays.items()}], core_ids=[0])
    r = r.results[0]
    y = r["out_y"].transpose(2, 1, 0).reshape(T, D)
    conv_p = r["out_conv_p"].transpose(2, 1, 0).reshape(1, 1, STATE, DC)
    conv_s = r["out_conv_s"][:, :, :, STEPS:].transpose(2, 3, 1, 0).reshape(1, SEQS, STATE, DC)
    kv = np.empty((T, 6, GROUPS, HD), np.float32)
    kv[:NP_, 0:2] = r["out_kv_cmp"].reshape(2, HD, 2, GROUPS, NP_ // 2).transpose(4, 0, 2, 3, 1).reshape(NP_, 2, GROUPS, HD)
    kv[NP_:, 0:2] = r["out_kv_cmp_s"].reshape(2, HD, 2, 2, NS_).transpose(4, 2, 3, 0, 1).reshape(NS_, 2, GROUPS, HD)
    k = r["out_k_new"].reshape(2, HD, 2, 2, T).transpose(4, 2, 3, 0, 1).reshape(T, 2, GROUPS, HD)
    v = r["out_v_new"].reshape(P, 5, 2, GROUPS, HD)
    v = np.concatenate([v[:, 0:4].transpose(1, 0, 2, 3, 4).reshape(NP_, 2, GROUPS, HD), v[:NS_, 4]], axis=0)
    kv[:, 2::2], kv[:, 3::2] = k, v
    kv_prompt = kv[:NP_, :4].reshape(1, 1, NP_, 4, GROUPS, HD)
    kv_sample = kv[NP_:, :4].reshape(1, SEQS, STEPS, 4, GROUPS, HD)
    win_prompt = kv[:NP_, 4:].reshape(1, 1, NP_, 2, GROUPS, HD)
    win_sample = np.concatenate([r["out_win_s"].reshape(SEQS, PAST - STEPS, 2, GROUPS, HD),
                                 kv[NP_:, 4:].reshape(SEQS, STEPS, 2, GROUPS, HD)], axis=1)[None]
    return (y[:NP_].reshape(1, NP_, D), y[NP_:].reshape(SEQS, STEPS, D), kv_prompt, kv_sample,
            win_prompt, win_sample, conv_p, conv_s)
```

```python
import numpy as np
import concourse.bass as bass
from concourse import mybir
from contextlib import ExitStack

F32 = mybir.dt.float32
F32R = mybir.dt.float32r
I32 = mybir.dt.int32
ACT = mybir.ActivationFunctionType
ALU = mybir.AluOpType
AX = mybir.AxisListType

P = 128
D = 1024
KT = D // P
NP_, NS_ = 512, 32
T = NP_ + NS_
TA = 256
TB = T - TA
Q = T // 4
SEQS, STEPS = 8, 4
DC = 2048
CT = DC // P
TAPS = 31
STATE = TAPS - 1
PTAPS = 4
PTAPS_LAST = 10
CSTEPS = TAPS - PTAPS + 2
EPS = 1e-6
HEADS, HD, GROUPS = 16, 64, 4
HPG = HEADS // GROUPS
PAST, PAGE = 256, 128
NPG = PAST // PAGE
SEL = 64
CSTRIDE, CBLK = 16, 32
NCP = (NP_ - CBLK) // CSTRIDE + 1
NCS = (PAST + STEPS - CBLK) // CSTRIDE + 1
NEG = -1e30
FLOOR = -1e28
GL = HEADS * 3
VTOK = 2 * GROUPS * HD + GL
VH = VTOK // 2
FT_KV, FT_Q, FT_Z = 8, 8, 8
FT = FT_KV + FT_Q + FT_Z
NKEY = PAST + NS_

BASE = 16512


def conv_steps_to(c):
    return CSTEPS * (c + 1) - (PTAPS_LAST - PTAPS if c == CT - 1 else 0)


def reaches(i, n):
    return not isinstance(i, int) or i >= n


SAMPLE_WIN = 8


def sample_unit(v):
    w, br = divmod(v, 2) if v < SAMPLE_WIN else (v - SAMPLE_WIN, 2)
    return w // 2, w % 2, br


def build(nc, io):
    ctx = ExitStack()
    with ctx:
        def at(name, shape, offset, dt=F32):
            return nc.alloc_sbuf_tensor_at(name, shape, dt, offset=offset)

        def sem(name):
            return ctx.enter_context(nc.semaphore(name))

        ROW = T * 4
        o = BASE
        X = at("X", [P, KT, T], o); o += KT * ROW
        SM = o; o += 12288
        HR = o; o += KT * ROW
        W1R = o; o += 16384
        G0 = o; o += 2 * KT * ROW
        G1 = o
        NR = 229344 - 4 * ROW
        s = SM
        ones = at("ones", [P, P], s); s += P * 4
        ident = at("ident", [P, P], s); s += P * 4
        gains = at("gains", [P, 3, KT], s); s += 96
        lng = at("lng", [P, CT], s); s += 64
        lnb = at("lnb", [P, CT], s); s += 64
        SMT = s
        taps = at("taps", [P, CT, 32], s); s += CT * 128
        tapc = at("tapc", [P, 2, 32], s); s += 256
        ctail = at("ctail", [P, CT, STATE], s); s += CT * STATE * 4
        SMX = s
        mean4 = at("mean4", [P, Q], NR)
        rstd4 = at("rstd4", [P, Q], NR + ROW)
        sq = at("sq", [P, 2, T], NR + 2 * ROW)
        Hh = at("Hh", [P, KT, T], HR, F32R)
        Xl = at("Xl", [P, KT, T], BASE, F32R)
        ringAh = at("ringAh", [P, 3, KT, P], W1R, F32R)
        diag = at("diag", [P, 2, PTAPS, P], W1R + 3 * KT * P * 4)
        diag_last = at("diag_last", [P, PTAPS_LAST, P], W1R)
        C = at("C", [P, CT, T], G0)
        s = G1
        Z1 = at("Z1", [P, CT, T], s); s += CT * ROW
        ringA = at("ringA", [P, 2, 3, KT, P], s); RINGA = s
        ringAl = at("ringAl", [P, 2, 3, KT, P], s, F32R)
        s += 2 * 3 * KT * P * 4
        VS = at("VS", [P, CT, SEQS, STATE + STEPS], s); s += CT * SEQS * (STATE + STEPS) * 4
        VP = at("VP", [P, 2, STATE + NP_], s); s += 2 * 2176
        sig = at("sig", [P, 2, T], s); s += 2 * ROW
        acc = at("acc", [P, 2, NP_], s); s += 2 * NP_ * 4
        prod = at("prod", [P, 32, NS_], s); s += 32 * NS_ * 4
        assert s <= NR
        Ch = at("Ch", [P, CT, T], G1, F32R)
        Cl = at("Cl", [P, CT, T], G0, F32R)
        ringC = at("ringC", [P, 3, CT, P], RINGA)
        ringCl = at("ringCl", [P, 3, CT, P], RINGA, F32R)
        ringCh = [at(f"ringCh{i}", [P, CT, P], o, F32R) for i, o in enumerate((HR, W1R, W1R + CT * P * 4))]
        s = VSR = RINGA + 2 * 3 * KT * P * 4
        ringE = at("ringE", [P, 3, KT, P], s); s += 3 * KT * P * 4
        BIAS = s
        bias = at("bias", [P, 2, NP_], s); s += 2 * NP_ * 4
        rowsel = at("rowsel", [NS_, 2, P], s)
        vcs = at("vcs", [P, GROUPS * HD], s); s += GROUPS * HD * 4
        assert s <= VSR + 17408
        s = VSR + 17408
        WTOK = s
        wtok = at("wtok", [P, KT, VTOK], s)
        WOp = at("WOp", [P, KT, P], s)
        sq2 = at("sq2", [P, 6, T], s + KT * P * 4)
        PCT = at("PCT", [HD, 8, NP_], s); s += KT * VTOK * 4
        KK = at("KK", [P, 2, GROUPS, NP_ // 2], s)
        S = at("S", [P, 4, NP_], s); s += 4 * NP_ * 4
        assert s <= NR - 2048
        cache_cmp = at("cache_cmp", [P, 2, SEQS * GROUPS, P], G1)
        cache_sel = at("cache_sel", [P, SEQS, NPG, 4 * P], G1)
        s = RINGA - 2048
        KTm = at("KTm", [P, 2, 2, T], s); s += 4 * ROW
        V = at("V", [P, 5, VTOK], s); s += 5 * VTOK * 4
        PTR = s
        PT = at("PT", [P, 2, NP_], s); s += 2 * NP_ * 4
        kcs = at("kcs", [P, 2, P], s); s += 2 * P * 4
        kcp = at("kcp", [P, 2, 32], s); s += 2 * 32 * 4
        KN = at("KN", [P, 4, NS_], s); s += 4 * NS_ * 4
        assert s <= VSR
        H2 = at("H2", [P, KT, T], G0 + KT * ROW)
        Hl = at("Hl", [P, KT, T], G0 + KT * ROW, F32R)
        Hlz = at("Hlz", [P, KT, T], G1, F32R)
        ringEl = at("ringEl", [P, 3, KT, P], VSR, F32R)
        ringEh = [at("ringEh0", [P, KT, P], BIAS, F32R), at("ringEh1", [P, KT, P], PTR, F32R)]
        wtokl = at("wtokl", [P, KT, VTOK], WTOK, F32R)
        wtokh = at("wtokh", [P, KT - 1, VTOK], G0, F32R)
        wtokh_last = at("wtokh_last", [P, VTOK], SMT, F32R)
        QT = at("QT", [P, 8, T], G0)
        ZT = at("ZT", [P, 8, T], G0 + KT * ROW)
        WOq = at("WOq", [P, 4, KT, P], G0)
        W1 = at("W1", [P, 2, CBLK // 2, P], W1R)
        cbias = at("cbias", [P, 4, NP_], W1R)
        SX = at("SX", [P, 4, NP_], W1R + 4 * NP_ * 4)
        KS = [at("KS0", [P, GROUPS, NP_], W1R, F32R), at("KS1", [P, GROUPS, NP_], VSR, F32R)]
        KTl = at("KTl", [P, 2, 2, T], RINGA - 2048, F32R)
        QS = [at("QS0", [P, NP_], NR - 2048, F32R), at("QS1", [P, NP_], PTR + NP_ * 4, F32R)]
        PTB = at("PTB", [P, 2, 4, NP_], HR)
        cache_win = at("cache_win", [P, SEQS, 8 * P], HR)
        s = NR
        hp = at("hp", [P, 2, GROUPS, 32], s); s += 2 * GROUPS * 32 * 4
        hs = at("hs", [P, 2, GROUPS, SEQS * 16], s); s += 2 * SEQS * GROUPS * 16 * 4
        sbias = at("sbias", [P, 2, 2, NKEY + P], NR)
        s = SMT
        vcd = at("vcd", [HD, 2, P], s)
        s = SMX
        dist = at("dist", [P, NP_], s); s += NP_ * 4
        qblk = at("qblk", [P, SEQS, 2, 32], s); s += SEQS * 2 * 32 * 4
        slopes = at("slopes", [P, 8, 2], s); s += 64
        pe_in = at("pe_in", [P, 2, CBLK // 2], s); s += 128
        pe_hid = at("pe_hid", [P, 2], s); s += 32
        W2 = at("W2", [P, 2, HD], s); s += 512
        headsel = at("headsel", [P, 2, GL], s); s += 2 * GL * 4
        gates_c = at("gates_c", [P, 4, HEADS], s); s += 4 * HEADS * 4
        gates_sw = at("gates_sw", [P, 4, HEADS * 2], s); s += 4 * HEADS * 8
        gpair = at("gpair", [P, 4, 2, 2], s); s += 64
        nmax = at("nmax", [P, 16], s); s += 64
        rsum = at("rsum", [P, 16], s); s += 64
        gsc = at("gsc", [P, 16], s); s += 64
        m16 = at("m16", [P, HEADS], s); s += 64
        s16 = at("s16", [P, HEADS], s); s += 64
        grow = at("grow", [P, 2, 2, 3], s); s += 64
        tick = at("tick", [1, 16], s); s += 64
        ptick = at("ptick", [P, 2], s); s += 32
        one = at("one", [P, 1], s)
        scrap = at("scrap", [P, 2], s + 32); s += 64
        pages = at("pages", [1, SEQS * NPG], s, I32); s += 64
        assert s <= HR, (s, HR)
        OS = at("OS", [P, 4, P], NR - 2048)
        gtmp = at("gtmp", [P, 2, 2, GL], NR - 2048)

        ps = ctx.enter_context(nc.psum_tensor("ps", [P, 8, 512], F32))

        def halves(i):
            return ((ps[:, 2 * i, 0:TA], slice(0, TA)), (ps[:, 2 * i + 1, 0:TB], slice(TA, T)))

        def prompt_of(i):
            return ps[:, 2 * i:2 * i + 2, 0:TA]

        def sample_of(i):
            return ps[:, 2 * i + 1, TA:TB]

        def quarters(ap):
            return ap.rearrange("p (j q) -> p j q", j=4)

        x_in = [sem(f"x_in{i}") for i in range(4)]
        consts_in = sem("consts_in")
        gains_in = sem("gains_in")
        taps_in = sem("taps_in")
        state_in = sem("state_in")
        wA_in = [sem(f"wA_in{i}") for i in range(2)]
        wC_in = [sem(f"wC_in{i}") for i in range(3)]
        store_p = sem("store_p")
        store_s = sem("store_s")
        stored = sem("stored")
        squared = sem("squared")
        sq_summed = sem("sq_summed")
        mean_sq = sem("mean_sq")
        inv_var = sem("inv_var")
        rstd_kept = sem("rstd_kept")
        rstd_ready = sem("rstd_ready")
        one_set = sem("one_set")
        h_ready = sem("h_ready")
        h1h_ready = sem("h1h_ready")
        h1l_ready = sem("h1l_ready")
        x_again = sem("x_again")
        wAh_ready = sem("wAh_ready")
        wAl_ready = sem("wAl_ready")
        diag_ready = sem("diag_ready")
        taps_done = sem("taps_done")
        ones_set = sem("ones_set")
        pads_set = sem("pads_set")
        gate_done = sem("gate_done")
        lin_done = sem("lin_done")
        z_done = sem("z_done")
        sig_ready = sem("sig_ready")
        z_kept = sem("z_kept")
        tail_kept = sem("tail_kept")
        tap_set = sem("tap_set")
        v_ready = sem("v_ready")
        conv_step = sem("conv_step")
        pool_step = sem("pool_step")
        c_summed = sem("c_summed")
        mean_ready = sem("mean_ready")
        centered = sem("centered")
        scaled = sem("scaled")
        activated = sem("activated")
        c_gated = sem("c_gated")
        ch_ready = sem("ch_ready")
        cl_ready = sem("cl_ready")
        wCh_ready = sem("wCh_ready")
        wCl_first = sem("wCl_first")
        wCl_ready = sem("wCl_ready")
        out1_done = sem("out1_done")
        x_added = sem("x_added")

        wtok_in = sem("wtok_in")
        w1_in = sem("w1_in")
        small_in = sem("small_in")
        pages_in = sem("pages_in")
        cmp_in = sem("cmp_in")
        sel_in = sem("sel_in")
        win_in = sem("win_in")
        cbias_in = sem("cbias_in")
        sbias_in = sem("sbias_in")
        wE_in = [sem(f"wE_in{i}") for i in range(3)]
        wO_in = [sem(f"wO_in{i}") for i in range(KT)]
        h2_ready = sem("h2_ready")
        hh_ready = sem("hh_ready")
        hl_ready = sem("hl_ready")
        hl_moved = sem("hl_moved")
        wEh_ready = sem("wEh_ready")
        wEl_first = sem("wEl_first")
        wEl_ready = sem("wEl_ready")
        wTh_ready = sem("wTh_ready")
        wTl_ready = sem("wTl_ready")
        f_done = sem("f_done")
        kv_kept = sem("kv_kept")
        tok_done = sem("tok_done")
        v_kept = sem("v_kept")
        grow_done = sem("grow_done")
        grow_kept = sem("grow_kept")
        zeros_set = sem("zeros_set")
        kk_stored = sem("kk_stored")
        k_stored = sem("k_stored")
        grow_ready = sem("grow_ready")
        gates_ready = sem("gates_ready")
        hid_done = sem("hid_done")
        pe_kept = sem("pe_kept")
        hid_ready = sem("hid_ready")
        pads2_set = sem("pads2_set")
        comp_done = sem("comp_done")
        comp_kept = sem("comp_kept")
        q_kept = sem("q_kept")
        qblk_ready = sem("qblk_ready")
        zt_ready = sem("zt_ready")
        cs_done = sem("cs_done")
        cs_step = sem("cs_step")
        cs_exp = sem("cs_exp")
        cs_t = sem("cs_t")
        cs_kept = sem("cs_kept")
        kh_ready = sem("kh_ready")
        kh1_ready = sem("kh1_ready")
        kl_ready = sem("kl_ready")
        qh_set = sem("qh_set")
        ql_set = sem("ql_set")
        pc_set = sem("pc_set")
        bias_set = sem("bias_set")
        qk_done = sem("qk_done")
        sc_ready = sem("sc_ready")
        exp_ready = sem("exp_ready")
        gate_set = sem("gate_set")
        inv_ready = sem("inv_ready")
        p_ready = sem("p_ready")
        t_done = sem("t_done")
        pt_kept = sem("pt_kept")
        pv_done = sem("pv_done")
        ss_done = sem("ss_done")
        ss_ready = sem("ss_ready")
        ss_exp = sem("ss_exp")
        ss_step = sem("ss_step")
        ss_t = sem("ss_t")
        ss_pt = sem("ss_pt")
        ss_pv = sem("ss_pv")
        os_kept = sem("os_kept")
        og_sample = sem("og_sample")
        og = sem("og")
        out2_done = sem("out2_done")
        x2_added = sem("x2_added")
        out2s_done = sem("out2s_done")
        x2s_added = sem("x2s_added")
        y_ready = sem("y_ready")

        def tok_bank(i):
            return 2 * i if i < 4 else 2

        def weights_at(u):
            return S[:, u % 8] if u % 8 < 4 else SX[:, u % 8 - 4]

        def w_o(n):
            return WOq[:, n] if n < 4 else WOp[:] if n == 5 else ringE[:, 2 if n == 4 else n - 6]

        def split(ap):
            return ap.rearrange("p (b t) -> p b t", b=2)

        block = ctx.enter_context(nc.Block())

        @block.sync
        def _(sp):
            for i in range(4):
                sp.dma_start(X[:, 2 * i:2 * i + 2], io["x"][:, 2 * i:2 * i + 2]).then_inc(x_in[i], 16)
            sp.dma_start(gains[:], io["gains"]).then_inc(gains_in, 16)

            def load_wA(c, par, turn):
                if turn is not None:
                    sp.wait_ge(z_done, c - 1)
                sp.dma_start(ringA[:, par], io["w_a"][c]).then_inc(wA_in[par], 16)

            load_wA(0, 0, None)
            sp.dma_start(pages[:], io["pages"]).then_inc(pages_in, 16)
            sp.dma_start(taps[:], io["taps"]).then_inc(taps_in, 16)
            load_wA(1, 1, None)
            sp.dma_start(VS[:], io["state"]).then_inc(state_in, 16)
            sp.dma_start(ident[:], io["ident"]).then_inc(consts_in, 16)
            sp.dma_start(lng[:], io["lng"]).then_inc(consts_in, 16)
            sp.dma_start(lnb[:], io["lnb"]).then_inc(consts_in, 16)
            with sp.Fori(1, CT // 2) as j:
                load_wA(2 * j, 0, j)
                load_wA(2 * j + 1, 1, j)
            for n in range(KT):
                if n < 3:
                    sp.wait_ge(z_done, CT)
                else:
                    sp.wait_ge(out1_done, n - 2)
                sp.dma_start(ringC[:, n % 3], io["w_c"][n]).then_inc(wC_in[n % 3], 16)
                if n == 2:
                    sp.dma_start(X[:], io["x"]).then_inc(x_again, 16)
                    sp.wait_ge(tail_kept, CT)
                    sp.dma_start(io["conv_p"], ctail[:]).then_inc(store_p, 16)
                    sp.wait_ge(v_ready, 2 * CT)
                    sp.dma_start(io["conv_s"], VS[:]).then_inc(store_s, 16)
            for name, tile in (("slopes", slopes), ("dist", dist), ("pe", pe_in), ("w2", W2), ("headsel", headsel), ("rowsel", rowsel)):
                sp.dma_start(tile[:], io[name]).then_inc(small_in, 16)
            sp.wait_ge(store_s, 16)
            sp.wait_ge(pool_step, 7 * CT)
            for n in range(3):
                sp.dma_start(ringE[:, n], io["w_f"][n]).then_inc(wE_in[n], 16)
            sp.dma_start(wtok[:], io["w_t"]).then_inc(wtok_in, 16)
            sp.wait_ge(out1_done, KT)
            sp.wait_ge(pages_in, 16)

            def load_cache_cmp(i):
                page = sp.value_load(pages[0:1, i:i + 1], min_val=0, max_val=io["cache_cmp"].shape[0] - 1)
                q, pg = divmod(i, NPG)
                for kv in range(2):
                    sp.dma_start(cache_cmp[:, kv, q::SEQS, pg * SEL:(pg + 1) * SEL],
                                 io["cache_cmp"][bass.ds(page, 1), :, kv].rearrange("o p g t -> (o p) g t")).then_inc(cmp_in, 16)

            for n in range(3, FT):
                sp.wait_ge(f_done, n - 2)
                sp.dma_start(ringE[:, n % 3], io["w_f"][n]).then_inc(wE_in[n % 3], 16)
                if n < 5:
                    sp.dma_start(W1[:, n - 3], io["w1"][:, n - 3]).then_inc(w1_in, 16)
                if 7 <= n < 11:
                    for i in range(4 * (n - 7), 4 * (n - 7) + 4):
                        load_cache_cmp(i)
                if n == FT_KV + 3:
                    sp.wait_ge(kv_kept, FT_KV)
                    sp.wait_ge(v_kept, 5)
                    sp.dma_start(io["kv_cmp"], KK[:]).then_inc(kk_stored, 16)
                    sp.dma_start(io["kv_cmp_s"], KN[:]).then_inc(stored, 16)
                    sp.dma_start(io["k_new"], KTm[:]).then_inc(k_stored, 16)
                    sp.dma_start(io["v_new"][:, 0:4], V[:, 0:4, 0:2 * GROUPS * HD]).then_inc(stored, 16)
                    sp.dma_start(io["v_new"][0:NS_, 4], V[0:NS_, 4, 0:2 * GROUPS * HD]).then_inc(stored, 16)
                    sp.wait_ge(hid_done, 2)
                    sp.dma_start(cbias[:], io["cbias"]).then_inc(cbias_in, 16)
            sp.wait_ge(f_done, FT)
            sp.dma_start(w_o(4), io["w_o"][4]).then_inc(wO_in[4], 16)
            for i in range(SEQS * NPG):
                page = sp.value_load(pages[0:1, i:i + 1], min_val=0, max_val=io["cache_sel"].shape[0] - 1)
                sp.dma_start(cache_sel[:, i // NPG, i % NPG, :],
                             io["cache_sel"][bass.ds(page, 1)].rearrange("o p n -> (o p) n")).then_inc(sel_in, 16)
            sp.dma_start(sbias[:], io["sbias"]).then_inc(sbias_in, 16)
            sp.dma_start(io["win_s"], io["win_state"]).then_inc(stored, 16)
            sp.wait_ge(ql_set, 16)
            for n in range(4):
                sp.dma_start(w_o(n), io["w_o"][n]).then_inc(wO_in[n], 16)
            sp.wait_ge(pc_set, 8)
            sp.dma_start(w_o(5), io["w_o"][5]).then_inc(wO_in[5], 16)
            sp.wait_ge(qk_done, 128)
            for n in range(6, KT):
                sp.dma_start(w_o(n), io["w_o"][n]).then_inc(wO_in[n], 16)
            sp.wait_ge(pv_done, 32)
            sp.dma_start(cache_win[:], io["cache_win"]).then_inc(win_in, 16)
            for k in range(KT):
                sp.wait_ge(y_ready, k + 1)
                sp.dma_start(io["y"][:, k], X[:, k]).then_inc(stored, 16)
            sp.wait_ge(stored, 16 * (4 + KT))
            sp.wait_ge(store_p, 16)

        @block.tensor
        def _(pe):
            def add_up(bank, row, first, last, n=Q):
                for j in range(4):
                    mm = nc.tensor.matmul(ps[32 * j:32 * j + 32, bank, 0:n], ones[:, 0:32], row[:, n * j:n * j + n],
                                          start=first, stop=last)
                return mm

            def spread(bank, row4, n=Q):
                for j in range(4):
                    mm = nc.tensor.matmul(ps[:, bank + j, 0:n], ones[32 * j:32 * j + 1, :], row4[32 * j:32 * j + 1, 0:n],
                                          start=True, stop=True)
                return mm

            pe.wait_ge(ones_set, 1)
            for k in range(KT):
                pe.wait_ge(squared, k + 1)
                add_up(7, sq[:, k % 2], k == 0, k == KT - 1).then_inc(sq_summed, 1)
            pe.wait_ge(rstd_kept, 1)
            spread(0, rstd4).then_inc(rstd_ready, 1)

            def split_product(dst_of, wh, wl, xh, xl, first, last):
                for w, x, begins, ends in ((wh, xh, first, False), (wh, xl, False, False), (wl, xh, False, last)):
                    for dst, cols in dst_of:
                        mm = nc.tensor.matmul(dst, w, x[:, cols], start=begins, stop=ends)
                return mm

            def project(c, par, j, pair, done):
                pe.wait_ge(wAl_ready, 3 * c + j + 1)
                for k in range(KT):
                    if j == 0 and not reaches(c, 1):
                        pe.wait_ge(h1h_ready, k + 1)
                        pe.wait_ge(h1l_ready, k + 1)
                    mm = split_product(halves(pair), ringAh[:, j, k, :], ringAl[:, par, j, k, :],
                                       Hh[:, k, :], Xl[:, k, :], k == 0, k == KT - 1)
                mm.then_inc(done, 1)

            def add_to_mean(c):
                pe.wait_ge(conv_step, conv_steps_to(c))
                pe.wait_ge(pool_step, 7 * c + 7)
                add_up(7, C[:, c, :], c == 0, c == CT - 1).then_inc(c_summed, 1)

            def tile(c, par, diags=None):
                if reaches(c, 1):
                    pe.wait_ge(sig_ready, c)
                project(c, par, 0, 0, gate_done)
                if reaches(c, 1):
                    pe.wait_ge(v_ready, 2 * c)
                project(c, par, 1, 1, lin_done)
                if reaches(c, 1):
                    pe.wait_ge(z_kept, c)
                project(c, par, 2, 2, z_done)
                pe.wait_ge(diag_ready, c + 1)
                pe.wait_ge(v_ready, 2 * c + 1)
                if reaches(c, 1):
                    pe.wait_ge(conv_step, CSTEPS * c)
                if diags is None:
                    diags = [diag[:, par, i] for i in range(PTAPS)]
                for i, d in enumerate(diags):
                    k = TAPS - len(diags) + i
                    mm = nc.tensor.matmul(ps[:, 6], d, VP[:, par, k:k + NP_], start=(i == 0), stop=(k == TAPS - 1))
                mm.then_inc(taps_done, 1)

            pe.wait_ge(h_ready, KT)
            tile(0, 0)
            tile(1, 1)
            with pe.Fori(1, CT // 2 - 1) as j:
                tile(2 * j, 0)
                tile(2 * j + 1, 1)
            tile(CT - 2, 0)
            tile(CT - 1, 1, [diag_last[:, i] for i in range(PTAPS_LAST)])
            for c in range(CT):
                add_to_mean(c)

            pe.wait_ge(z_kept, CT)
            pe.wait_ge(mean_ready, 1)
            spread(4, mean4).then_inc(mean_ready, 1)
            pe.wait_ge(sig_ready, CT)
            pe.wait_ge(v_ready, 2 * CT)
            for c in range(CT):
                pe.wait_ge(squared, KT + c + 1)
                add_up(0, sq[:, c % 2], c == 0, c == CT - 1).then_inc(sq_summed, 1)
            pe.wait_ge(rstd_kept, 2)
            spread(0, rstd4).then_inc(rstd_ready, 1)

            def out1(n, k):
                return split_product(halves(1 + (n + 1) % 3), ringCh[n % 3][:, k, :], ringCl[:, n % 3, k, :],
                                     Ch[:, k, :], Cl[:, k, :], k == 0, k == CT - 1)

            def sum_x(k):
                pe.wait_ge(squared, KT + CT + k + 1)
                add_up(0, sq[:, k % 2], k == 0, k == KT - 1).then_inc(sq_summed, 1)

            pe.wait_ge(wCh_ready, 2)
            pe.wait_ge(wCl_first, 2)
            for k in range(CT):
                pe.wait_ge(ch_ready, k + 1)
                pe.wait_ge(cl_ready, k + 1)
                for n in range(2):
                    mm = out1(n, k)
                    if k == CT - 1:
                        mm.then_inc(out1_done, 1)
            for n in range(2, KT):
                pe.wait_ge(wCh_ready, n + 1)
                pe.wait_ge(wCl_ready, n - 1)
                if n >= 3:
                    pe.wait_ge(x_added, n - 2)
                for k in range(CT):
                    mm = out1(n, k)
                mm.then_inc(out1_done, 1)
                sum_x(n - 2)

            sum_x(KT - 2)
            sum_x(KT - 1)
            pe.wait_ge(rstd_kept, 3)
            spread(4, rstd4).then_inc(rstd_ready, 1)

            def f_part(n, k, pair, low):
                return split_product(halves(pair), ringEh[n % 2][:, k, :], ringEl[:, n % 3, k, :],
                                     Hh[:, k, :], low[:, k, :], k == 0, k == KT - 1)

            def f_tile(n, pair, low=Hl):
                pe.wait_ge(wEh_ready, n + 1)
                pe.wait_ge(wEl_ready, n - 1)
                for k in range(KT):
                    mm = f_part(n, k, pair, low)
                mm.then_inc(f_done, 1)

            pe.wait_ge(wEh_ready, 2)
            pe.wait_ge(wEl_first, 2)
            for k in range(KT):
                pe.wait_ge(hh_ready, k + 1)
                pe.wait_ge(hl_ready, k + 1)
                for n in range(2):
                    mm = f_part(n, k, n, Hl)
                    if k == KT - 1:
                        mm.then_inc(f_done, 1)
            for n in range(2, FT_KV):
                if n >= 4:
                    pe.wait_ge(kv_kept, n - 3)
                f_tile(n, n % 4)
            pe.wait_ge(wTh_ready, KT)
            pe.wait_ge(wTl_ready, KT)
            for i in range(5):
                if i < 4:
                    pe.wait_ge(kv_kept, 5 + i)
                else:
                    pe.wait_ge(v_kept, 2)
                first = min(i * P, T - P)
                for k in range(KT):
                    wh = wtokh[:, k, :] if k < KT - 1 else wtokh_last[:]
                    dst_of = [(ps[:, tok_bank(i) + b, 0:VH], slice(b * VH, (b + 1) * VH)) for b in range(2)]
                    mm = split_product(dst_of, Hh[:, k, first:first + P], Hl[:, k, first:first + P],
                                       wh, wtokl[:, k, :], k == 0, k == KT - 1)
                mm.then_inc(tok_done, 1)
            def gate_rows():
                pe.wait_ge(v_kept, 5)
                pe.wait_ge(small_in, 96)
                for sg in range(2):
                    mm = nc.tensor.matmul(ps[:, 2 + sg, 0:GL], rowsel[:, sg, :], V[0:NS_, 4, 2 * GROUPS * HD:VTOK],
                                          start=True, stop=True)
                mm.then_inc(grow_done, 1)

            pe.wait_ge(w1_in, 32)
            pe.wait_ge(cmp_in, 32 * SEQS * NPG)
            pe.wait_ge(v_kept, 4)
            for kv in range(2):
                if kv == 1:
                    gate_rows()
                for m in range(CBLK // 2):
                    w, first, last = W1[:, kv, m, :], m == 0, m == CBLK // 2 - 1
                    nc.tensor.matmul(ps[:, kv, 0:GROUPS * NCP], w, KK[:, kv, :, m:m + 8 * (NCP - 1) + 1:8],
                                     start=first, stop=last)
                    nc.tensor.matmul(ps[:, 4 + kv, 0:SEQS * GROUPS * NCS], w,
                                     cache_cmp[:, kv, :, m:m + 8 * (NCS - 1) + 1:8], start=first, stop=last)
                    mm = nc.tensor.matmul(ps[:, 6 + kv, 0:1], w, pe_in[:, kv, m:m + 1], start=first, stop=last)
                mm.then_inc(hid_done, 1)

            def q_or_z(n):
                i = n - FT_KV
                if i < FT_Q:
                    if i == 0:
                        pe.wait_ge(grow_kept, 2)
                    if i == 1:
                        pe.wait_ge(pe_kept, 1)
                    if i >= 2:
                        pe.wait_ge(q_kept, i - 1)
                    f_tile(n, 3 if i % 2 else 1)
                else:
                    i -= FT_Q
                    if i == 0:
                        pe.wait_ge(comp_kept, 4)
                    elif i == 1:
                        pe.wait_ge(q_kept, FT_Q)
                    else:
                        pe.wait_ge(zt_ready, i - 1)
                    if i == 0:
                        pe.wait_ge(hl_moved, 1)
                    f_tile(n, i % 2, Hlz)

            q_or_z(FT_KV)
            q_or_z(FT_KV + 1)
            pe.wait_ge(hid_ready, 4)
            pe.wait_ge(pads2_set, 1)
            for g in range(GROUPS):
                rows = slice(HD * (g % 2), HD * (g % 2) + HD)
                nc.tensor.matmul(ps[rows, 0, 32 * (g // 2):32 * (g // 2) + 32], W2[:, 0, :], hp[:, 0, g, :],
                                 start=True, stop=True)
                nc.tensor.matmul(ps[rows, 1, P * (g // 2):P * (g // 2) + P], W2[:, 0, :], hs[:, 0, g],
                                 start=True, stop=True)
                nc.tensor.matmul(ps[32 * (g % 2):32 * (g % 2) + 32, 4, HD * (g // 2):HD * (g // 2) + HD],
                                 hp[:, 1, g, :], W2[:, 1, :], start=True, stop=True)
                mm = nc.tensor.matmul(ps[:, 5, HD * g:HD * g + HD], hs[:, 1, g], W2[:, 1, :],
                                      start=True, stop=True)
            mm.then_inc(comp_done, 1)
            for i in range(2, FT_Q):
                q_or_z(FT_KV + i)
            def compressed_transpose(t):
                pe.wait_ge(cs_step, 9 * t + 9)
                if t >= 1:
                    pe.wait_ge(cs_kept, t)
                for i in range(8):
                    mm = nc.tensor.transpose(ps[0:HD, 6 + i // 4, P * (i % 4):P * (i % 4) + P],
                                             S[:, t, HD * i:HD * i + HD], ident[:])
                mm.then_inc(cs_t, 1)

            q_or_z(FT_KV + FT_Q)
            pe.wait_ge(q_kept, FT_Q)
            for t in range(4):
                if t >= 1:
                    pe.wait_ge(cs_step, 9 * t - 8)
                for h in range(HEADS):
                    g, j = divmod(h, HPG)
                    rows = slice(HD * (g % 2), HD * (g % 2) + HD)
                    col = P * (g // 2) + 32 * j
                    mm = nc.tensor.matmul(ps[:, 4 + g % 2, col:col + 32], QT[rows, HPG * (g // 2) + j, t * P:(t + 1) * P],
                                          kcp[rows, g // 2, :], start=True, stop=True)
                mm.then_inc(cs_done, 1)
                if t >= 1:
                    q_or_z(FT_KV + FT_Q + 2 * t)
                if t >= 1:
                    compressed_transpose(t - 1)
                q_or_z(FT_KV + FT_Q + 2 * t + 1)
            compressed_transpose(3)

            pe.wait_ge(zt_ready, FT_Z)

            def qk(i, u, gp):
                r, b, t = u // 8, u % 8 // 4, u % 4
                rows, n = slice(HD * r, HD * r + HD), (t + 1) * P
                if u % 8 == 0:
                    pe.wait_ge(ql_set, 2 * i + r + 1)
                if u % 4 == 0 and not reaches(i, 1):
                    pe.wait_ge(kl_ready, 2 * b + 2)
                if u >= 4 or reaches(i, 1):
                    pe.wait_ge(sc_ready, 16 * i + u - 3)
                nc.tensor.matmul(ps[:, u % 4, 0:n], QS[r][:, t * P:(t + 1) * P], KS[b][:, 2 * gp + r, 0:n],
                                 start=True, stop=False)
                nc.tensor.matmul(ps[:, u % 4, 0:n], QS[r][rows, t * P:(t + 1) * P], KTl[rows, b, gp, 0:n],
                                 start=False, stop=True).then_inc(qk_done, 1)

            def transpose(i, u):
                t = u % 4
                pe.wait_ge(p_ready, 16 * i + u + 1)
                if u >= 2 or reaches(i, 1):
                    pe.wait_ge(pt_kept, 16 * i + u - 1)
                for k in range(t + 1):
                    mm = nc.tensor.transpose(ps[:, 4 + u % 2, P * k:P * k + P], weights_at(u)[:, P * k:P * k + P], ident[:])
                mm.then_inc(t_done, 1)

            def pv(i, n, gp):
                r, b, k = n // 8, n % 8 // 4, n % 4
                out = ps[HD * r:HD * r + HD, 6 + r]
                if n % 8 == 0:
                    nc.tensor.matmul(out, vcd[:, gp, HD * r:HD * r + HD], PT[0:HD, 0, :], start=True, stop=False)
                if k == 0:
                    pe.wait_ge(pt_kept, 16 * i + n + 4)
                v = b * GROUPS * HD + (2 * gp + r) * HD
                mm = nc.tensor.matmul(out[:, P * k:NP_], V[:, k, v:v + HD], PTB[:, b, k, P * k:NP_],
                                      start=False, stop=(b == 1 and k == 3))
                if k == 3:
                    mm.then_inc(pv_done, 1)

            def attend(i, gp, last_gp):
                for u in range(16):
                    if u >= 4:
                        transpose(i, u - 4)
                    elif reaches(i, 1):
                        transpose(i - 1, u + 12)
                    if u == 8:
                        if reaches(i, 1):
                            pe.wait_ge(og, 2 * i - 1)
                        else:
                            pe.wait_ge(cs_kept, 4)
                        pe.wait_ge(pc_set, i + 1)
                    elif u == 0 and reaches(i, 2):
                        pe.wait_ge(og, 2 * i - 2)
                    qk(i, u, gp)
                    if u >= 8:
                        pv(i, u - 8, gp)
                    elif reaches(i, 1):
                        pv(i - 1, u + 8, last_gp)

            attend(0, 0, 0)
            attend(1, 0, 0)
            with pe.Fori(2, 4) as i:
                attend(i, 0, 0)
            attend(4, 1, 0)
            with pe.Fori(5, 8) as i:
                attend(i, 1, 1)
            for u in range(8):
                if u < 4:
                    transpose(7, u + 12)
                if u == 0:
                    pe.wait_ge(og, 14)
                pv(7, u + 8, 1)

            pe.wait_ge(qblk_ready, 1)
            pe.wait_ge(sel_in, 16 * SEQS * NPG)

            def sample_scores(v):
                gp, sg, br = sample_unit(v)
                if v < 2:
                    pe.wait_ge(sc_ready, 16 * 8)
                else:
                    pe.wait_ge(ss_ready, v - 1)
                if v == SAMPLE_WIN:
                    pe.wait_ge(win_in, 16)
                for q in range(4):
                    s_ = 4 * sg + q
                    rows = slice(32 * q, 32 * q + 32)
                    if br == 0:
                        mm = nc.tensor.matmul(ps[rows, v % 2, 0:P], qblk[:, s_, gp, :], kcs[:, gp, :], start=True, stop=True)
                        continue
                    keys = (cache_sel[:, s_, :, gp * P:gp * P + P] if br == 1
                            else cache_win[:, s_, gp * PAST:(gp + 1) * PAST])
                    nc.tensor.matmul(ps[rows, v % 2, 0:PAST], qblk[:, s_, gp, :], keys, start=True, stop=True)
                    mm = nc.tensor.matmul(ps[rows, v % 2, PAST:NKEY], qblk[:, s_, gp, :], KTm[:, br - 1, gp, NP_:T],
                                          start=True, stop=True)
                mm.then_inc(ss_done, 1)

            def sample_transpose(v):
                br = sample_unit(v)[2]
                pe.wait_ge(ss_step, 3 * v + 3)
                if v >= 2:
                    pe.wait_ge(ss_pt, v - 1)
                for k in range(1 if br == 0 else 2):
                    mm = nc.tensor.transpose(ps[:, 2 + v % 2, P * k:P * k + P], S[:, v % 4, P * k:P * k + P], ident[:])
                if br:
                    mm = nc.tensor.transpose(ps[0:NS_, 2 + v % 2, PAST:PAST + P], S[:, v % 4, PAST:NKEY], ident[:])
                mm.then_inc(ss_t, 1)

            def sample_pv(v):
                gp, sg, br = sample_unit(v)
                m = v // 2 if v < SAMPLE_WIN else v - 4
                pe.wait_ge(ss_pt, v + 1)
                if m >= 2:
                    pe.wait_ge(os_kept, m - 1)
                elif br == 0:
                    pe.wait_ge(pt_kept, 128)
                out = ps[:, 4 + m % 2]
                if br == 0:
                    nc.tensor.matmul(out[:, 0:P], vcs[:, gp * P:(gp + 1) * P], PT[:, v % 2, 0:P],
                                     start=True, stop=False).then_inc(ss_pv, 1)
                    return
                vnew = (br - 1) * GROUPS * HD + gp * P
                for q in range(4):
                    s_, cols = 4 * sg + q, slice(32 * q, 32 * q + 32)
                    for c in range(2):
                        vals = (cache_sel[:, s_, c, PAST + gp * P:PAST + gp * P + P] if br == 1
                                else cache_win[:, s_, (2 + c) * PAST + gp * P:(2 + c) * PAST + gp * P + P])
                        nc.tensor.matmul(out[:, cols], vals, PT[:, v % 2, P * c + 32 * q:P * c + 32 * q + 32],
                                         start=(br == 2 and c == 0), stop=False)
                    if br == 2:
                        mm = nc.tensor.matmul(out[:, cols], V[0:NS_, 4, vnew:vnew + P],
                                              PT[0:NS_, v % 2, PAST + 32 * q:PAST + 32 * q + 32], start=False, stop=True)
                if br == 1:
                    mm = nc.tensor.matmul(out[:, 0:P], V[0:NS_, 4, vnew:vnew + P], PT[0:NS_, v % 2, PAST:PAST + P],
                                          start=False, stop=True)
                mm.then_inc(ss_pv, 1)

            def out2(n, ks, dst_of):
                for k in ks:
                    for dst, cols in dst_of:
                        mm = nc.tensor.matmul(dst, w_o(n)[:, k, :], ZT[:, k, cols], start=(k == 0), stop=(k == KT - 1))
                return mm

            for v in range(16):
                n, quarter = divmod(v, 4)
                if v < 12:
                    sample_scores(v)
                if 2 <= v < 14:
                    sample_transpose(v - 2)
                if 3 <= v < 15:
                    sample_pv(v - 3)
                if v == 0:
                    pe.wait_ge(og, 16)
                if quarter == 0:
                    pe.wait_ge(wO_in[n], 16)
                    if n >= 2:
                        pe.wait_ge(x2_added, n - 1)
                mm = out2(n, range(2 * quarter, 2 * quarter + 2), [(ps[:, 6 + n % 2], slice(0, NP_))])
                if quarter == 3:
                    mm.then_inc(out2_done, 1)

            def sum_out(i):
                pe.wait_ge(squared, 2 * KT + CT + i + 1)
                add_up(7, sq2[:, i % 6], i == 0, i == KT - 1).then_inc(sq_summed, 1)

            pe.wait_ge(ss_ready, 12)
            for n in range(4, KT):
                pe.wait_ge(wO_in[n], 16)
                if n == 4:
                    out2(n, range(KT), halves(0)[:1])
                    pe.wait_ge(og_sample, 4)
                    mm = out2(n, range(KT), halves(0)[1:])
                else:
                    if n == 5:
                        pe.wait_ge(ss_pt, 12)
                    elif n == 6:
                        pe.wait_ge(os_kept, 8)
                    else:
                        pe.wait_ge(x2_added, 4)
                        for m in range(4):
                            mm = out2(m, range(KT), [(ps[:, 6, NS_ * m:NS_ * m + NS_], slice(NP_, T))])
                        mm.then_inc(out2s_done, 1)
                        sum_out(0)
                        sum_out(1)
                    mm = out2(n, range(KT), halves((n - 4) % 3))
                mm.then_inc(out2_done, 1)
            for i in range(2, KT):
                sum_out(i)
            pe.wait_ge(rstd_kept, 4)
            pe.wait_ge(x2_added, KT)
            spread(2, rstd4).then_inc(rstd_ready, 1)

        @block.scalar
        def _(act):
            for k in range(KT):
                act.wait_ge(x_in[k // 2], 16)
                if k >= 2:
                    act.wait_ge(sq_summed, k - 1)
                nc.scalar.activation(sq[:, k % 2, :], X[:, k, :], ACT.Square).then_inc(squared, 1)
            act.wait_ge(one_set, 1)

            def root(n, cols=Q):
                nc.scalar.activation(scrap[:, 0:1], one[:], ACT.Sqrt)
                act.wait_ge(inv_var, n)
                nc.scalar.activation(rstd4[:, 0:cols], rstd4[:, 0:cols], ACT.Sqrt).then_inc(rstd_kept, 1)

            root(1)

            def high_wA(par, j):
                nc.scalar.activation(ringAh[:, j], ringA[:, par, j], ACT.Copy).then_inc(wAh_ready, 1)

            act.wait_ge(wA_in[0], 16)
            for j in range(3):
                high_wA(0, j)
            for k in range(KT):
                act.wait_ge(h_ready, k + 1)
                nc.scalar.activation(Hh[:, k, :], X[:, k, :], ACT.Copy).then_inc(h1h_ready, 1)
            act.wait_ge(consts_in, 48)

            def tile(c, par, next_turn):
                act.wait_ge(gate_done, c + 1)
                if reaches(c, 2):
                    act.wait_ge(v_ready, 2 * c - 2)
                nc.scalar.activation(sig[:, par, 0:NP_].rearrange("p (b t) -> p b t", b=2), prompt_of(0), ACT.Sigmoid)
                nc.scalar.activation(sig[:, par, NP_:T], sample_of(0), ACT.Sigmoid).then_inc(sig_ready, 1)
                if next_turn is not None:
                    act.wait_ge(wA_in[1 - par], 16 * next_turn)
                    high_wA(1 - par, 0)
                    act.wait_ge(lin_done, c + 1)
                    high_wA(1 - par, 1)
                act.wait_ge(tap_set, c + 1)
                if reaches(c, 2):
                    act.wait_ge(taps_done, c - 1)
                if next_turn is None:
                    act.wait_ge(lin_done, c + 1)
                diags = [diag[:, par, i] if next_turn is not None else diag_last[:, i]
                         for i in range(PTAPS if next_turn is not None else PTAPS_LAST)]
                for k, d in enumerate(diags, TAPS - len(diags)):
                    op = nc.scalar.activation(d, ident[:], ACT.Copy, scale=tapc[:, par, k:k + 1])
                op.then_inc(diag_ready, 1)
                act.wait_ge(v_ready, 2 * c + 2)
                nc.scalar.activation(ctail[:, c, :], VP[:, par, NP_:NP_ + STATE], ACT.Copy).then_inc(tail_kept, 1)
                act.wait_ge(z_done, c + 1)
                nc.scalar.activation(Z1[:, c, 0:NP_].rearrange("p (b t) -> p b t", b=2), prompt_of(2), ACT.Silu)
                nc.scalar.activation(Z1[:, c, NP_:T], sample_of(2), ACT.Silu).then_inc(z_kept, 1)
                if next_turn is not None:
                    high_wA(1 - par, 2)

            tile(0, 0, 1)
            tile(1, 1, 2)
            with act.Fori(1, CT // 2 - 1) as j:
                tile(2 * j, 0, j + 1)
                tile(2 * j + 1, 1, j + 2)
            tile(CT - 2, 0, CT // 2)
            tile(CT - 1, 1, None)

            for n in range(2):
                act.wait_ge(wC_in[n], 16)
                if n == 1:
                    act.wait_ge(taps_done, CT)
                nc.scalar.activation(ringCh[n][:], ringC[:, n], ACT.Copy).then_inc(wCh_ready, 1)
            act.wait_ge(z_kept, CT)
            for c in range(CT):
                act.wait_ge(centered, c + 1)
                if c >= 2:
                    act.wait_ge(sq_summed, KT + c - 1)
                nc.scalar.activation(sq[:, c % 2, :], C[:, c, :], ACT.Square).then_inc(squared, 1)
            root(2)
            nc.scalar.activation(scrap[:, 1:2], one[:], ACT.Silu)
            def high_wC(n):
                if n >= 3:
                    act.wait_ge(out1_done, n - 2)
                act.wait_ge(wC_in[n % 3], 16 * (n // 3 + 1))
                nc.scalar.activation(ringCh[n % 3][:], ringC[:, n % 3], ACT.Copy).then_inc(wCh_ready, 1)

            for c in range(CT + 2):
                if c < CT:
                    act.wait_ge(scaled, c + 1)
                    nc.scalar.activation(C[:, c, :], C[:, c, :], ACT.Silu, scale=lng[:, c:c + 1],
                                         bias=lnb[:, c:c + 1]).then_inc(activated, 1)
                if c >= 2:
                    act.wait_ge(c_gated, c - 1)
                    nc.scalar.activation(Ch[:, c - 2, :], C[:, c - 2, :], ACT.Copy).then_inc(ch_ready, 1)

            def square_x(k):
                act.wait_ge(x_added, k + 1)
                act.wait_ge(sq_summed, KT + CT + k - 1)
                nc.scalar.activation(sq[:, k % 2, :], X[:, k, :], ACT.Square).then_inc(squared, 1)

            def high_wE(n):
                if n >= FT:
                    return
                act.wait_ge(wE_in[n % 3], 16 * (n // 3 + 1))
                if n >= 2:
                    act.wait_ge(f_done, n - 1)
                nc.scalar.activation(ringEh[n % 2][:], ringE[:, n % 3], ACT.Copy).then_inc(wEh_ready, 1)

            high_wC(2)
            for n in range(3, KT):
                high_wC(n)
                square_x(n - 3)
            act.wait_ge(out1_done, 6)
            for n in range(2):
                high_wE(n)
            square_x(KT - 3)
            square_x(KT - 2)
            square_x(KT - 1)
            root(3)

            for k in range(KT):
                act.wait_ge(h2_ready, k + 1)
                nc.scalar.activation(Hh[:, k, :], H2[:, k, :], ACT.Copy).then_inc(hh_ready, 1)
            act.wait_ge(wtok_in, 16)
            act.wait_ge(store_p, 16)
            for k in range(KT):
                wh = wtokh[:, k, :] if k < KT - 1 else wtokh_last[:]
                nc.scalar.activation(wh, wtok[:, k, :], ACT.Copy).then_inc(wTh_ready, 1)
                high_wE(k + 2)
            for i in range(5):
                rows = slice(0, P) if i < 4 else slice(P - NS_, P)
                act.wait_ge(tok_done, i + 1)
                nc.scalar.activation(V[0:rows.stop - rows.start, i, :].rearrange("p (b n) -> p b n", b=2),
                                     ps[rows, tok_bank(i):tok_bank(i) + 2, 0:VH], ACT.Copy).then_inc(v_kept, 1)
            act.wait_ge(v_kept, 5)
            logits = V[:, 0:4, 2 * GROUPS * HD:VTOK].rearrange("p t (h b) -> p t h b", b=3)
            nc.scalar.activation(gates_c[:], logits[:, :, :, 0], ACT.Sigmoid)
            nc.scalar.activation(gates_sw[:].rearrange("p t (h b) -> p t h b", b=2), logits[:, :, :, 1:3],
                                 ACT.Sigmoid).then_inc(gates_ready, 1)
            act.wait_ge(grow_kept, 3)
            nc.scalar.activation(grow[:], grow[:], ACT.Sigmoid).then_inc(grow_ready, 1)
            act.wait_ge(hid_done, 2)
            act.wait_ge(pe_kept, 1)
            for kv in range(2):
                nc.scalar.activation(hp[:, kv, :, 0:NCP],
                                     ps[:, kv, 0:GROUPS * NCP].rearrange("p (g c) -> p g c", g=GROUPS),
                                     ACT.Silu, bias=pe_hid[:, kv:kv + 1]).then_inc(hid_ready, 1)
                nc.scalar.activation(hs[:, kv].rearrange("p g (s c) -> p (g s) c", c=16)[:, :, 0:NCS],
                                     ps[:, 4 + kv, 0:SEQS * GROUPS * NCS].rearrange("p (g c) -> p g c", c=NCS),
                                     ACT.Silu, bias=pe_hid[:, kv:kv + 1]).then_inc(hid_ready, 1)
            for i in range(FT_Q):
                pair = 3 if i % 2 else 1
                act.wait_ge(f_done, FT_KV + i + 1)
                nc.scalar.activation(split(QT[:, i, 0:NP_]), prompt_of(pair), ACT.Copy, scale=HD ** -0.5)
                nc.scalar.activation(QT[:, i, NP_:T], sample_of(pair), ACT.Copy, scale=HD ** -0.5).then_inc(q_kept, 1)
                if i + 2 <= FT_Q:
                    high_wE(FT_KV + i + 2)

            def z_tile(i):
                act.wait_ge(f_done, FT_KV + FT_Q + i + 1)
                nc.scalar.activation(split(ZT[:, i, 0:NP_]), prompt_of(i % 2), ACT.Silu)
                nc.scalar.activation(ZT[:, i, NP_:T], sample_of(i % 2), ACT.Silu).then_inc(zt_ready, 1)

            def keep_compressed(t):
                act.wait_ge(cs_t, t + 1)
                nc.scalar.activation(PCT[:, :, P * t:P * t + P].rearrange("p (a j) q -> p a j q", a=2),
                                     ps[0:HD, 6:8, :].rearrange("p a (j q) -> p a j q", j=4), ACT.Copy).then_inc(cs_kept, 1)

            for t in range(4):
                high_wE(FT_KV + FT_Q + 2 * t + 1)
                act.wait_ge(cs_step, 9 * t + 4)
                nc.scalar.activation(S[:, t, :], S[:, t, :], ACT.Exp).then_inc(cs_exp, 1)
                z_tile(2 * t)
                high_wE(FT_KV + FT_Q + 2 * t + 2)
                if t >= 1:
                    keep_compressed(t - 1)
                if t == 3:
                    act.wait_ge(cs_step, 9 * 3 + 1)
                    for r in range(2):
                        for half in range(2):
                            nc.scalar.activation(KS[0][HD * half:HD * half + HD, r::2, :],
                                                 KTm[HD * r:HD * r + HD, 0, :, 0:NP_], ACT.Copy).then_inc(kh_ready, 1)
                z_tile(2 * t + 1)
            keep_compressed(3)

            def exp(i, u):
                n = (u % 4 + 1) * P
                act.wait_ge(sc_ready, 16 * i + u + 1)
                w = weights_at(u)[:, 0:n]
                nc.scalar.activation(w, w, ACT.Exp, scale=-1.0, bias=nmax[:, u:u + 1],
                                     accum_out=rsum[:, u:u + 1]).then_inc(exp_ready, 1)

            def copy_weights(i, u):
                turn, t = u // 4 % 2, u % 4
                act.wait_ge(t_done, 16 * i + u + 1)
                if t == 0 and (u >= 8 or reaches(i, 1)):
                    act.wait_ge(pv_done, 4 * i + u // 4 - 1)
                nc.scalar.activation(PTB[:, turn, 0:t + 1, P * t:P * t + P],
                                     ps[:, 4 + u % 2, 0:(t + 1) * P].rearrange("p (k q) -> p k q", q=P),
                                     ACT.Copy).then_inc(pt_kept, 1)

            def attend(i):
                for u in range(16):
                    if u >= 4:
                        copy_weights(i, u - 4)
                    elif reaches(i, 1):
                        copy_weights(i - 1, u + 12)
                    exp(i, u)

            attend(0)
            with act.Fori(1, 8) as i:
                attend(i)
            for u in range(12, 16):
                copy_weights(7, u)

            def square_out(i, n):
                if i >= 6:
                    act.wait_ge(sq_summed, 2 * KT + CT + i - 5)
                nc.scalar.activation(sq2[:, i % 6], X[:, n, :], ACT.Square).then_inc(squared, 1)

            act.wait_ge(pc_set, 8)
            for v in range(12):
                n = NKEY if sample_unit(v)[2] else P
                act.wait_ge(ss_ready, v + 1)
                nc.scalar.activation(S[:, v % 4, 0:n], S[:, v % 4, 0:n], ACT.Exp, scale=-1.0, bias=nmax[:, v:v + 1],
                                     accum_out=rsum[:, v:v + 1]).then_inc(ss_exp, 1)
            for i, n in enumerate((4, 5, 6)):
                act.wait_ge(x2_added, n + 1)
                square_out(i, n)
            act.wait_ge(x2s_added, 1)
            for n in range(4):
                square_out(3 + n, n)
            act.wait_ge(x2_added, KT)
            square_out(KT - 1, KT - 1)
            root(4)

        @block.vector
        def _(dve):
            nc.vector.memset(ones[:], 1.0).then_inc(ones_set, 1)
            nc.vector.memset(VP[:, :, 0:STATE], 0.0).then_inc(pads_set, 1)
            nc.vector.memset(one[:], 1.0).then_inc(one_set, 1)

            def inverse_variance(n, bank, count, done, cols=Q):
                dve.wait_ge(sq_summed, done)
                nc.vector.tensor_scalar(rstd4[:, 0:cols], ps[:, bank, 0:cols], 1.0 / count, EPS,
                                        ALU.mult, ALU.add).then_inc(mean_sq, 1)
                dve.wait_ge(mean_sq, n)
                nc.vector.reciprocal(rstd4[:, 0:cols], rstd4[:, 0:cols]).then_inc(inv_var, 1)

            def normalized(dst, src, gain, factor):
                return nc.vector.scalar_tensor_tensor(quarters(dst), quarters(src), gain, factor, ALU.mult, ALU.mult)

            def low_h1(k):
                dve.wait_ge(h1h_ready, k + 1)
                nc.vector.tensor_tensor(Xl[:, k, :], X[:, k, :], Hh[:, k, :].bitcast(F32), ALU.subtract).then_inc(h1l_ready, 1)

            inverse_variance(1, 7, D, KT)
            dve.wait_ge(rstd_ready, 1)
            dve.wait_ge(gains_in, 16)
            for k in range(KT):
                normalized(X[:, k, :], X[:, k, :], gains[:, 0, k:k + 1], ps[:, 0:4, 0:Q]).then_inc(h_ready, 1)
                if k >= 1:
                    low_h1(k - 1)
            low_h1(KT - 1)
            dve.wait_ge(taps_in, 16)
            dve.wait_ge(state_in, 16)
            dve.wait_ge(pads_set, 1)

            def tile(c, par, dtaps=TAPS - PTAPS):
                if reaches(c, 2):
                    dve.wait_ge(pool_step, 7 * c - 7)
                nc.vector.tensor_copy(tapc[:, par, :], taps[:, c, :]).then_inc(tap_set, 1)
                dve.wait_ge(sig_ready, c + 1)
                dve.wait_ge(lin_done, c + 1)
                if reaches(c, 2):
                    dve.wait_ge(tail_kept, c - 1)
                nc.vector.tensor_tensor(VP[:, par, STATE:].rearrange("p (b t) -> p b t", b=2), prompt_of(1),
                                        sig[:, par, 0:NP_].rearrange("p (b t) -> p b t", b=2),
                                        ALU.mult).then_inc(v_ready, 1)
                nc.vector.tensor_tensor(VS[:, c, :, STATE:], sample_of(1).rearrange("p (s t) -> p s t", s=SEQS),
                                        sig[:, par, NP_:T].rearrange("p (s t) -> p s t", s=SEQS),
                                        ALU.mult).then_inc(v_ready, 1)
                dve.wait_ge(tap_set, c + 1)
                dve.wait_ge(v_ready, 2 * c + 1)
                for k in range(dtaps):
                    src, w = VP[:, par, k:k + NP_], tapc[:, par, k:k + 1]
                    if k == 0:
                        op = nc.vector.tensor_scalar(acc[:, 0, :], src, w, tapc[:, par, TAPS:TAPS + 1], ALU.mult, ALU.add)
                    elif k == 1:
                        op = nc.vector.tensor_scalar(acc[:, 1, :], src, w, None, ALU.mult)
                    else:
                        dve.wait_ge(conv_step, CSTEPS * c + k - 1)
                        op = nc.vector.scalar_tensor_tensor(acc[:, k % 2, :], src, w, acc[:, k % 2, :], ALU.mult, ALU.add)
                    op.then_inc(conv_step, 1)
                dve.wait_ge(conv_step, CSTEPS * c + dtaps - 1)
                dve.wait_ge(taps_done, c + 1)
                nc.vector.tensor_tensor(acc[:, dtaps % 2, :], acc[:, dtaps % 2, :], ps[:, 6], ALU.add).then_inc(conv_step, 1)
                dve.wait_ge(conv_step, CSTEPS * c + dtaps + 1)
                nc.vector.tensor_tensor(C[:, c, 0:NP_], acc[:, 0, :], acc[:, 1, :], ALU.add).then_inc(conv_step, 1)
                dve.wait_ge(conv_step, CSTEPS * c + dtaps + 2)

            tile(0, 0)
            tile(1, 1)
            with dve.Fori(1, CT // 2 - 1) as j:
                tile(2 * j, 0)
                tile(2 * j + 1, 1)
            tile(CT - 2, 0)
            tile(CT - 1, 1, TAPS - PTAPS_LAST)

            dve.wait_ge(c_summed, CT)
            nc.vector.tensor_scalar(mean4[:], ps[:, 7, 0:Q], 1.0 / DC, None, ALU.mult).then_inc(mean_ready, 1)
            dve.wait_ge(mean_ready, 2)
            dve.wait_ge(pool_step, 7 * CT)
            for c in range(CT):
                nc.vector.tensor_tensor(quarters(C[:, c, :]), quarters(C[:, c, :]), ps[:, 4:8, 0:Q],
                                        ALU.subtract).then_inc(centered, 1)
            inverse_variance(2, 0, DC, KT + CT)
            dve.wait_ge(rstd_ready, 2)
            dve.wait_ge(squared, KT + CT)

            def scale(c):
                nc.vector.tensor_tensor(quarters(C[:, c, :]), quarters(C[:, c, :]), ps[:, 0:4, 0:Q],
                                        ALU.mult).then_inc(scaled, 1)

            for c in range(CT + 4):
                if c < CT:
                    scale(c)
                if c >= 4:
                    dve.wait_ge(ch_ready, c - 3)
                    nc.vector.tensor_tensor(Cl[:, c - 4, :], C[:, c - 4, :], Ch[:, c - 4, :].bitcast(F32),
                                            ALU.subtract).then_inc(cl_ready, 1)

            def low_wC(n):
                dve.wait_ge(wCh_ready, n + 1)
                nc.vector.tensor_tensor(ringCl[:, n % 3], ringC[:, n % 3], ringCh[n % 3][:].bitcast(F32),
                                        ALU.subtract).then_inc(wCl_ready, 1)

            low_wC(2)
            for n in range(KT):
                if n + 3 < KT:
                    low_wC(n + 3)
                if n == 0:
                    dve.wait_ge(x_again, 16)
                dve.wait_ge(out1_done, n + 1)
                nc.vector.tensor_tensor(X[:, n, 0:NP_].rearrange("p (b t) -> p b t", b=2), prompt_of(1 + (n + 1) % 3),
                                        X[:, n, 0:NP_].rearrange("p (b t) -> p b t", b=2), ALU.add)
                nc.vector.tensor_tensor(X[:, n, NP_:T], sample_of(1 + (n + 1) % 3), X[:, n, NP_:T],
                                        ALU.add).then_inc(x_added, 1)

            inverse_variance(3, 0, D, 2 * KT + CT)
            dve.wait_ge(rstd_ready, 3)
            dve.wait_ge(x_added, KT)

            def low_wE(n):
                if n >= FT:
                    return
                dve.wait_ge(wEh_ready, n + 1)
                nc.vector.tensor_tensor(ringEl[:, n % 3], ringE[:, n % 3], ringEh[n % 2][:].bitcast(F32),
                                        ALU.subtract).then_inc(wEl_ready, 1)

            def low_h(k):
                dve.wait_ge(hh_ready, k + 1)
                nc.vector.tensor_tensor(Hl[:, k, :], H2[:, k, :], Hh[:, k, :].bitcast(F32), ALU.subtract).then_inc(hl_ready, 1)

            for k in range(KT):
                normalized(H2[:, k, :], X[:, k, :], gains[:, 1, k:k + 1], ps[:, 4:8, 0:Q]).then_inc(h2_ready, 1)
                if k >= 1:
                    low_h(k - 1)
            low_h(KT - 1)
            for n in range(FT_KV):
                dve.wait_ge(wTh_ready, n + 1)
                wh = wtokh[:, n, :] if n < KT - 1 else wtokh_last[:]
                nc.vector.tensor_tensor(wtokl[:, n, :], wtok[:, n, :], wh.bitcast(F32), ALU.subtract).then_inc(wTl_ready, 1)
                if n < FT_KV - 1:
                    low_wE(n + 2)
                dve.wait_ge(f_done, n + 1)
                if n < 4:
                    kv, gp = divmod(n, 2)
                    for r in range(2):
                        for par in range(2):
                            nc.vector.tensor_copy(split(KK[HD * par:HD * par + HD, kv, 2 * gp + r, :]),
                                                  ps[HD * r:HD * r + HD, 2 * n:2 * n + 2, par:TA:2])
                    nc.vector.tensor_copy(KN[:, n, :], sample_of(n)).then_inc(kv_kept, 1)
                else:
                    b, gp = divmod(n - 4, 2)
                    nc.vector.tensor_copy(split(KTm[:, b, gp, 0:NP_]), prompt_of(n % 4))
                    nc.vector.tensor_copy(KTm[:, b, gp, NP_:T], sample_of(n % 4)).then_inc(kv_kept, 1)
            low_wE(FT_KV + 1)
            dve.wait_ge(small_in, 96)
            dve.wait_ge(grow_done, 1)
            for sg in range(2):
                nc.vector.tensor_tensor(gtmp[:, sg], ps[:, 2 + sg:3 + sg, 0:GL].to_broadcast([P, 2, GL]), headsel[:],
                                        ALU.mult).then_inc(grow_kept, 1)
            dve.wait_ge(grow_kept, 2)
            nc.vector.tensor_reduce(grow[:].rearrange("p a g b -> p (a g) b"),
                                    gtmp[:].rearrange("p a g (h b) -> p (a g) b h", b=3), AX.X, ALU.add).then_inc(grow_kept, 1)
            dve.wait_ge(hid_done, 2)
            nc.vector.tensor_copy(pe_hid[:], ps[:, 6:8, 0]).then_inc(pe_kept, 1)
            nc.vector.tensor_copy(Hlz[:], Hl[:].bitcast(F32)).then_inc(hl_moved, 1)
            dve.wait_ge(comp_done, 1)
            dve.wait_ge(zeros_set, 1)
            nc.vector.tensor_copy(kcp[:], ps[:, 0, 0:64].rearrange("p (g c) -> p g c", g=2)).then_inc(comp_kept, 1)
            nc.vector.tensor_copy(kcs[:], ps[:, 1, 0:2 * P].rearrange("p (g c) -> p g c", g=2)).then_inc(comp_kept, 1)
            for r in range(2):
                rows = slice(32 * r, 32 * r + 32)
                op = nc.vector.tensor_copy(vcd[rows, :, HD * r:HD * r + HD],
                                           ps[rows, 4, 0:2 * HD].rearrange("p (g d) -> p g d", g=2))
            op.then_inc(comp_kept, 1)
            nc.vector.tensor_copy(vcs[:], ps[:, 5, 0:GROUPS * HD]).then_inc(comp_kept, 1)
            for n in range(FT_KV + 2, FT_KV + FT_Q + 1):
                low_wE(n)
            dve.wait_ge(q_kept, FT_Q)
            for gp in range(2):
                for r in range(2):
                    rows = slice(HD * r, HD * r + HD)
                    for j in range(HPG):
                        op = nc.vector.tensor_copy(qblk[rows, :, gp, 16 * r + 4 * j:16 * r + 4 * j + 4],
                                                   QT[rows, HPG * gp + j, NP_:T].rearrange("p (s t) -> p s t", s=SEQS))
            op.then_inc(qblk_ready, 1)

            dve.wait_ge(kk_stored, 16)
            dve.wait_ge(cbias_in, 16)
            dve.wait_ge(gates_ready, 1)
            for t in range(4):
                low_wE(FT_KV + FT_Q + 2 * t + 1)
                Sh = S[:, t, :].rearrange("p (h c) -> p h c", h=HEADS)
                dve.wait_ge(cs_done, t + 1)
                nc.vector.tensor_tensor(S[:, t, :].rearrange("p (i r c) -> p r i c", r=2, c=32),
                                        ps[:, 4:6, 0:2 * P].rearrange("p r (i c) -> p r i c", c=32),
                                        cbias[:, t, :].rearrange("p (i r c) -> p r i c", r=2, c=32), ALU.add).then_inc(cs_step, 1)
                dve.wait_ge(cs_step, 9 * t + 1)
                nc.vector.tensor_reduce(m16[:], Sh, AX.X, ALU.max).then_inc(cs_step, 1)
                dve.wait_ge(cs_step, 9 * t + 2)
                nc.vector.tensor_scalar(m16[:], m16[:], FLOOR, None, ALU.max).then_inc(cs_step, 1)
                dve.wait_ge(cs_step, 9 * t + 3)
                nc.vector.tensor_tensor(Sh, Sh, m16[:].unsqueeze(2).to_broadcast([P, HEADS, 32]),
                                        ALU.subtract).then_inc(cs_step, 1)
                dve.wait_ge(cs_exp, t + 1)
                nc.vector.tensor_reduce(s16[:], Sh, AX.X, ALU.add).then_inc(cs_step, 1)
                dve.wait_ge(cs_step, 9 * t + 5)
                nc.vector.tensor_scalar(s16[:], s16[:], 1e-30, None, ALU.max).then_inc(cs_step, 1)
                dve.wait_ge(cs_step, 9 * t + 6)
                nc.vector.reciprocal(s16[:], s16[:]).then_inc(cs_step, 1)
                dve.wait_ge(cs_step, 9 * t + 7)
                nc.vector.tensor_tensor(s16[:], s16[:], gates_c[:, t, :], ALU.mult).then_inc(cs_step, 1)
                dve.wait_ge(cs_step, 9 * t + 8)
                nc.vector.tensor_tensor(Sh, Sh, s16[:].unsqueeze(2).to_broadcast([P, HEADS, 32]),
                                        ALU.mult).then_inc(cs_step, 1)
                low_wE(FT_KV + FT_Q + 2 * t + 2)

            dve.wait_ge(k_stored, 16)

            dve.wait_ge(f_done, FT - 1)
            for r in range(2):
                for half in range(2):
                    nc.vector.tensor_copy(KS[1][HD * half:HD * half + HD, r::2, :],
                                          KTm[HD * r:HD * r + HD, 1, :, 0:NP_]).then_inc(kh1_ready, 1)

            def low_keys(b):
                dve.wait_ge(kh1_ready if b else kh_ready, 4)
                for r in range(2):
                    rows = slice(HD * r, HD * r + HD)
                    nc.vector.tensor_tensor(KTl[rows, b, :, 0:NP_], KTm[rows, b, :, 0:NP_],
                                            KS[b][rows, r::2, :].bitcast(F32), ALU.subtract).then_inc(kl_ready, 1)

            low_keys(0)
            low_keys(1)

            def score(i, u):
                r, n = u // 8, (u % 4 + 1) * P
                if u % 8 == 0:
                    dve.wait_ge(bias_set, 2 * i + r + 1)
                dve.wait_ge(qk_done, 16 * i + u + 1)
                if u >= 8 or reaches(i, 1):
                    dve.wait_ge(t_done, 16 * i + u - 7)
                nc.vector.memset(tick[:, u:u + 1], 0.0)
                nc.vector.tensor_tensor_reduce(weights_at(u)[:, 0:n], ps[:, u % 4, 0:n], bias[:, r, NP_ - n:NP_], -1.0, 3e38,
                                               ALU.add, ALU.min, nmax[:, u:u + 1]).then_inc(sc_ready, 1)

            def invert(i, u):
                dve.wait_ge(exp_ready, 16 * i + u + 1)
                nc.vector.reciprocal(gsc[:, u:u + 1], rsum[:, u:u + 1]).then_inc(inv_ready, 1)

            def normalize(i, u):
                r, b, t = u // 8, u % 8 // 4, u % 4
                if u == 0:
                    dve.wait_ge(gate_set, i + 1)
                dve.wait_ge(inv_ready, 16 * i + u + 1)
                w = weights_at(u)[:, 0:(t + 1) * P]
                nc.vector.tensor_scalar(w, w, gsc[:, u:u + 1], gpair[:, t, r, b:b + 1],
                                        ALU.mult, ALU.mult).then_inc(p_ready, 1)

            def set_gates(i):
                if reaches(i, 1):
                    dve.wait_ge(p_ready, 16 * i)
                nc.vector.tensor_copy(gpair[:].rearrange("p t r b -> p t (r b)"), gates_sw[:, :, bass.ds(4 * i, 4)]).then_inc(gate_set, 1)

            def gate_head(i, r):
                rows = slice(HD * r, HD * r + HD)
                dve.wait_ge(pv_done, 4 * i + 2 * r + 2)
                nc.vector.tensor_tensor(ZT[rows, i, 0:NP_], ps[rows, 6 + r, :], ZT[rows, i, 0:NP_], ALU.mult).then_inc(og, 1)

            def attend(i):
                for u in range(16):
                    score(i, u)
                    if u >= 2:
                        normalize(i, u - 2)
                    elif reaches(i, 1):
                        normalize(i - 1, u + 14)
                    if u >= 1:
                        invert(i, u - 1)
                    elif reaches(i, 1):
                        invert(i - 1, 15)
                    if u == 1:
                        set_gates(i)
                    if u == 5 and reaches(i, 1):
                        gate_head(i - 1, 0)
                    if u == 13 and reaches(i, 1):
                        gate_head(i - 1, 1)

            attend(0)
            with dve.Fori(1, 8) as i:
                attend(i)
            normalize(7, 14)
            invert(7, 15)
            normalize(7, 15)
            gate_head(7, 0)
            gate_head(7, 1)

            dve.wait_ge(sbias_in, 16)
            dve.wait_ge(grow_ready, 1)
            dve.wait_ge(t_done, 128)

            def sample_softmax_in(v):
                gp, sg, br = sample_unit(v)
                n, at_ = (P, NKEY) if br == 0 else (NKEY, 0)
                dve.wait_ge(ss_done, v + 1)
                if v >= 4:
                    dve.wait_ge(ss_t, v - 3)
                nc.vector.tensor_tensor_reduce(S[:, v % 4, 0:n], ps[:, v % 2, 0:n], sbias[:, gp, sg, at_:at_ + n], -1.0, 3e38,
                                               ALU.add, ALU.min, nmax[:, v:v + 1]).then_inc(ss_ready, 1)

            def sample_softmax_out(v):
                gp, sg, br = sample_unit(v)
                n = P if br == 0 else NKEY
                dve.wait_ge(ss_exp, v + 1)
                nc.vector.reciprocal(s16[:, v:v + 1], rsum[:, v:v + 1]).then_inc(ss_step, 1)
                dve.wait_ge(ss_step, 3 * v + 1)
                nc.vector.tensor_tensor(m16[:, v:v + 1], s16[:, v:v + 1], grow[:, sg, gp, br:br + 1], ALU.mult).then_inc(ss_step, 1)
                dve.wait_ge(ss_step, 3 * v + 2)
                nc.vector.tensor_scalar(S[:, v % 4, 0:n], S[:, v % 4, 0:n], m16[:, v:v + 1], None, ALU.mult).then_inc(ss_step, 1)

            def sample_copy(v):
                dve.wait_ge(ss_t, v + 1)
                if v >= 2:
                    dve.wait_ge(ss_pv, v - 1)
                if sample_unit(v)[2] == 0:
                    nc.vector.tensor_copy(PT[:, v % 2, 0:P], ps[:, 2 + v % 2, 0:P]).then_inc(ss_pt, 1)
                else:
                    nc.vector.tensor_copy(PT[:, v % 2, 0:PAST], ps[:, 2 + v % 2, 0:PAST])
                    nc.vector.tensor_copy(PT[0:NS_, v % 2, PAST:PAST + P], ps[0:NS_, 2 + v % 2, PAST:PAST + P]).then_inc(ss_pt, 1)

            def sample_keep(m):
                w = m % 4
                dve.wait_ge(ss_pv, 2 * m + 2 if m < 4 else m + 5)
                if m < 4:
                    nc.vector.tensor_copy(OS[:, w], ps[:, 4 + m % 2, 0:P]).then_inc(os_kept, 1)
                else:
                    dve.wait_ge(os_kept, w + 1)
                    nc.vector.tensor_tensor(OS[:, w], ps[:, 4 + m % 2, 0:P], OS[:, w], ALU.add).then_inc(os_kept, 1)

            def sample_gate(w):
                gp, sg = divmod(w, 2)
                dve.wait_ge(os_kept, w + 5)
                for r in range(2):
                    rows = slice(HD * r, HD * r + HD)
                    o4 = OS[rows, w].rearrange("p (s r j t) -> p r j s t", s=4, r=2, j=HPG)
                    zt = ZT[rows, HPG * gp:HPG * gp + HPG, NP_ + 16 * sg:NP_ + 16 * sg + 16]
                    zt = zt.rearrange("p j (s t) -> p j s t", s=4)
                    op = nc.vector.tensor_tensor(zt, o4[:, r], zt, ALU.mult)
                op.then_inc(og_sample, 1)

            def add_out(n):
                dve.wait_ge(out2_done, n + 1)
                if n < 4:
                    nc.vector.tensor_tensor(X[:, n, 0:NP_], ps[:, 6 + n % 2], X[:, n, 0:NP_], ALU.add).then_inc(x2_added, 1)
                else:
                    pair = (n - 4) % 3
                    nc.vector.tensor_tensor(split(X[:, n, 0:NP_]), prompt_of(pair), split(X[:, n, 0:NP_]), ALU.add)
                    nc.vector.tensor_tensor(X[:, n, NP_:T], sample_of(pair), X[:, n, NP_:T], ALU.add).then_inc(x2_added, 1)

            for v in range(2 * KT):
                if v < 12:
                    sample_softmax_in(v)
                if 1 <= v < 13:
                    sample_softmax_out(v - 1)
                if 2 <= v < 14:
                    sample_copy(v - 2)
                if 3 <= v < 15:
                    if v - 3 >= SAMPLE_WIN:
                        sample_keep(v - 3 - 4)
                    elif (v - 3) % 2:
                        sample_keep((v - 3) // 2)
                if v - 4 >= SAMPLE_WIN:
                    sample_gate(v - 4 - SAMPLE_WIN)
                if v >= 5 and v % 4 == 1:
                    add_out(v // 4 - 1)
            for n in range(3, 7):
                add_out(n)
            dve.wait_ge(out2s_done, 1)
            nc.vector.tensor_tensor(X[:, 0:4, NP_:T], ps[:, 6, 0:4 * NS_].rearrange("p (k t) -> p k t", k=4),
                                    X[:, 0:4, NP_:T], ALU.add).then_inc(x2s_added, 1)
            add_out(KT - 1)

            inverse_variance(4, 7, D, 3 * KT + CT)
            dve.wait_ge(rstd_ready, 4)
            dve.wait_ge(x2_added, KT)
            for k in range(KT):
                normalized(X[:, k, :], X[:, k, :], gains[:, 2, k:k + 1], ps[:, 2:6, 0:Q]).then_inc(y_ready, 1)

        @block.gpsimd
        def _(pool):
            def tile(c, par):
                pool.wait_ge(v_ready, 2 * c + 2)
                pool.wait_ge(tap_set, c + 1)
                if reaches(c, 1):
                    pool.wait_ge(pool_step, 7 * c)
                for s0 in range(STEPS):
                    win = VS[:, c, :, s0:s0 + TAPS].rearrange("p s k -> p k s")
                    dst = prod[:, 0:TAPS, s0:NS_:STEPS]
                    w = tapc[:, par, 0:TAPS].unsqueeze(2).to_broadcast([P, TAPS, SEQS])
                    op = nc.gpsimd.tensor_tensor(dst, win, w, ALU.mult)
                op.then_inc(pool_step, 1)
                nc.gpsimd.tensor_tensor(prod[:, TAPS, :], ones[:, 0:NS_],
                                        tapc[:, par, TAPS:TAPS + 1].to_broadcast([P, NS_]), ALU.mult).then_inc(pool_step, 1)
                for i, n in enumerate((16, 8, 4, 2)):
                    pool.wait_ge(pool_step, 7 * c + 2 + i)
                    nc.gpsimd.tensor_tensor(prod[:, 0:n, :], prod[:, 0:n, :], prod[:, n:2 * n, :],
                                            ALU.add).then_inc(pool_step, 1)
                pool.wait_ge(pool_step, 7 * c + 6)
                nc.gpsimd.tensor_tensor(C[:, c, NP_:T], prod[:, 0, :], prod[:, 1, :], ALU.add).then_inc(pool_step, 1)

            pool.wait_ge(ones_set, 1)
            def low_wA(c, par, j):
                pool.wait_ge(wAh_ready, 3 * c + j + 1)
                nc.gpsimd.tensor_tensor(ringAl[:, par, j], ringA[:, par, j], ringAh[:, j].bitcast(F32),
                                        ALU.subtract).then_inc(wAl_ready, 1)

            def tile_and_next(c, par):
                low_wA(c + 1, 1 - par, 0)
                low_wA(c + 1, 1 - par, 1)
                tile(c, par)
                low_wA(c + 1, 1 - par, 2)

            for j in range(3):
                low_wA(0, 0, j)
            pool.wait_ge(state_in, 16)
            tile_and_next(0, 0)
            tile_and_next(1, 1)
            with pool.Fori(1, CT // 2 - 1) as j:
                tile_and_next(2 * j, 0)
                tile_and_next(2 * j + 1, 1)
            tile_and_next(CT - 2, 0)
            tile(CT - 1, 1)

            for n in range(2):
                pool.wait_ge(wCh_ready, n + 1)
                nc.gpsimd.tensor_tensor(ringCl[:, n], ringC[:, n], ringCh[n][:].bitcast(F32),
                                        ALU.subtract).then_inc(wCl_first, 1)
            for c in range(CT):
                pool.wait_ge(activated, c + 1)
                nc.gpsimd.tensor_tensor(C[:, c, :], C[:, c, :], Z1[:, c, :], ALU.mult).then_inc(c_gated, 1)

            for n in range(2):
                pool.wait_ge(wEh_ready, n + 1)
                nc.gpsimd.tensor_tensor(ringEl[:, n], ringE[:, n], ringEh[n][:].bitcast(F32),
                                        ALU.subtract).then_inc(wEl_first, 1)
            pool.wait_ge(h2_ready, KT)
            nc.gpsimd.memset(hp[:, :, :, NCP:32], 0.0)
            nc.gpsimd.memset(hs[:].rearrange("p v g (s c) -> p (v g s) c", c=16)[:, :, NCS:16], 0.0).then_inc(pads2_set, 1)
            pool.wait_ge(tok_done, 5)
            pool.wait_ge(store_p, 16)
            pool.wait_ge(conv_step, conv_steps_to(CT - 1))
            nc.gpsimd.memset(vcd[:], 0.0)
            nc.gpsimd.memset(qblk[:], 0.0).then_inc(zeros_set, 1)
            pool.wait_ge(small_in, 96)
            pool.wait_ge(q_kept, FT_Q)
            pool.wait_ge(grow_kept, 3)

            def head(i, r):
                rows, other = slice(HD * r, HD * r + HD), slice(HD - HD * r, 2 * HD - HD * r)
                if reaches(i, 1):
                    pool.wait_ge(qk_done, 16 * i + 8 * r - 8)
                if r and not reaches(i, 1):
                    pool.wait_ge(f_done, FT)
                if r or reaches(i, 1):
                    pool.wait_ge(bias_set, 2 * i + r)
                nc.gpsimd.tensor_copy(QS[r][rows, :], QT[rows, i, 0:NP_]).then_inc(qh_set, 1)
                pool.wait_ge(qh_set, 2 * i + r + 1)
                nc.gpsimd.tensor_tensor(ptick[other, r:r + 1], ones[other, 0:1], ones[other, 0:1], ALU.mult)
                nc.gpsimd.tensor_tensor(QS[r][other, :], QT[rows, i, 0:NP_], QS[r][rows, :].bitcast(F32),
                                        ALU.subtract).then_inc(ql_set, 1)
                if reaches(i, 1):
                    pool.wait_ge(sc_ready, 16 * i + 8 * r - 8)
                elif r == 0:
                    pool.wait_ge(f_done, FT - 1)
                pool.wait_ge(ql_set, 2 * i + r + 1)
                nc.gpsimd.tensor_tensor(bias[:, r, :], dist[:], slopes[:, i, r:r + 1].to_broadcast([P, NP_]),
                                        ALU.mult).then_inc(bias_set, 1)

            def compressed(i):
                if reaches(i, 1):
                    pool.wait_ge(pv_done, 4 * i - 1)
                else:
                    pool.wait_ge(cs_kept, 4)
                pool.wait_ge(bias_set, 2 * i + 2)
                nc.gpsimd.tensor_copy(PT[0:HD, 0, :], PCT[:, i, :]).then_inc(pc_set, 1)

            def step(i):
                head(i, 0)
                head(i, 1)
                compressed(i)

            step(0)
            with pool.Fori(1, 8) as i:
                step(i)


def feature_major(xp, xs):
    x = np.concatenate([xp.reshape(NP_, D), xs.reshape(NS_, D)], axis=0)
    return np.ascontiguousarray(x.T.reshape(KT, P, T).transpose(1, 0, 2))


def by_partition(v, n):
    return np.ascontiguousarray(v.reshape(n, P).T)


def shape_constants():
    out = {}
    slope = np.exp2(-8.0 * np.arange(1, HEADS + 1) / HEADS).astype(np.float32)
    by_step = np.array([[slope[8 * (i // 4) + 4 * r + i % 4] for r in range(2)] for i in range(8)], np.float32)
    out["slopes"] = np.ascontiguousarray(np.broadcast_to(by_step, (P, 8, 2)))
    q, k = np.arange(P)[:, None], np.arange(NP_)[None, :] - (NP_ - P)
    out["dist"] = np.where(k <= q, k - q, NEG).astype(np.float32)
    q = (np.arange(4) * P)[None, :, None, None] + np.arange(P)[:, None, None, None]
    blk = np.arange(32)[None, None, None, :]
    d = q - (blk * CSTRIDE + CBLK - 1)
    cb = np.where((d >= 0) & (blk < NCP), -by_step.reshape(1, 1, HEADS, 1) * d, NEG)
    out["cbias"] = np.ascontiguousarray(cb.reshape(P, 4, HEADS * 32).astype(np.float32))
    q_, r, j, t = np.unravel_index(np.arange(P), (4, 2, HPG, STEPS))
    sb = np.full((P, 2, 2, NKEY + P), NEG, np.float32)
    sel = np.zeros((P, 2, HEADS, 3), np.float32)
    for gp in range(2):
        head = HPG * (2 * gp + r) + j
        sel[np.arange(P), gp, 2 * (HPG * gp + j) + r] = 1.0
        m = slope[head][:, None]
        for sg in range(2):
            seq = (4 * sg + q_)[:, None]
            sb[:, gp, sg, :PAST] = m * (np.arange(PAST)[None] - PAST - t[:, None])
            s_new, t_new = np.divmod(np.arange(NS_)[None], STEPS)
            sb[:, gp, sg, PAST:NKEY] = np.where((s_new == seq) & (t_new <= t[:, None]), m * (t_new - t[:, None]), NEG)
            s_c, c = np.divmod(np.arange(P)[None], 16)
            sb[:, gp, sg, NKEY:] = np.where((s_c == seq) & (c < NCS), m * (c * CSTRIDE + CBLK - 1 - PAST - t[:, None]), NEG)
    row = np.zeros((NS_, 2, P), np.float32)
    for sg in range(2):
        row[STEPS * (4 * sg + q_) + t, sg, np.arange(P)] = 1.0
    out["rowsel"] = row
    out["sbias"], out["headsel"] = sb, sel.reshape(P, 2, GL)
    return out


def kernel(x_prompt, x_sample, cache_kv, state_kv_win, state_conv, page_table, norm_g, final_norm_g,
           conv_w_in, conv_dw_w, conv_dw_b, conv_ln_g, conv_ln_b, conv_w_out,
           nsa_w_in, nsa_w_out, nsa_cmp_pe, nsa_cmp_w1, nsa_cmp_w2):
    import concourse.bacc as bacc
    from concourse.bass_utils import run_bass_kernel_spmd

    A = np.asarray
    arrays = {}
    arrays["x"] = feature_major(A(x_prompt), A(x_sample))
    g = np.concatenate([A(norm_g), A(final_norm_g)[None]], axis=0)
    arrays["gains"] = np.ascontiguousarray(g.reshape(3, KT, P).transpose(2, 0, 1))
    w = A(conv_w_in)[0].reshape(KT, P, 3, CT, P)[:, :, [1, 0, 2]]
    arrays["w_a"] = np.ascontiguousarray(w.transpose(3, 1, 2, 0, 4))
    taps = np.concatenate([A(conv_dw_w)[0], A(conv_dw_b)], axis=0)
    arrays["taps"] = np.ascontiguousarray(taps.reshape(32, CT, P).transpose(2, 1, 0))
    state = A(state_conv)[0].reshape(SEQS, STATE, CT, P).transpose(3, 2, 0, 1)
    arrays["state"] = np.ascontiguousarray(np.pad(state, ((0, 0), (0, 0), (0, 0), (0, STEPS))))
    arrays["ident"] = np.eye(P, dtype=np.float32)
    arrays["lng"] = by_partition(A(conv_ln_g)[0], CT)
    arrays["lnb"] = by_partition(A(conv_ln_b)[0], CT)
    arrays["w_c"] = np.ascontiguousarray(A(conv_w_out)[0].reshape(CT, P, KT, P).transpose(2, 1, 0, 3))
    w = A(nsa_w_in)[0]
    wq, wz, wkv, wgl = np.split(w, [D, 2 * D, 2 * D + 6 * GROUPS * HD], axis=1)
    def by_pairs(w, width):
        return w.reshape(-1, 2, 2, HPG, width).transpose(0, 1, 3, 2, 4).reshape(-1, HEADS * width)

    wq, wz, wgl = by_pairs(wq, HD), by_pairs(wz, HD), by_pairs(wgl, 3)
    wkv = wkv.reshape(D, 6, GROUPS * HD)
    w_f = np.concatenate([wkv[:, 0], wkv[:, 1], wkv[:, 2], wkv[:, 4], wq, wz], axis=1)
    arrays["w_f"] = np.ascontiguousarray(w_f.reshape(KT, P, FT, P).transpose(2, 1, 0, 3))
    w_t = np.concatenate([wkv[:, 3], wkv[:, 5], wgl], axis=1)
    arrays["w_t"] = np.ascontiguousarray(w_t.reshape(KT, P, VTOK).transpose(1, 0, 2))
    w_o = by_pairs(A(nsa_w_out)[0].T, HD).T
    arrays["w_o"] = np.ascontiguousarray(w_o.reshape(KT, P, KT, P).transpose(2, 1, 0, 3))
    arrays["w1"] = np.ascontiguousarray(A(nsa_cmp_w1)[0].reshape(2, CBLK // 2, P, P).transpose(2, 0, 1, 3))
    arrays["w2"] = np.ascontiguousarray(A(nsa_cmp_w2)[0].transpose(1, 0, 2))
    arrays["pe"] = np.ascontiguousarray(A(nsa_cmp_pe)[0].reshape(2, CBLK // 2, P).transpose(2, 0, 1))
    cache = A(cache_kv)[0]
    pool = cache.shape[0]
    c01 = cache[:, :, 0:2].reshape(pool, SEL, 2, 2, GROUPS, HD)
    arrays["cache_cmp"] = np.ascontiguousarray(c01.transpose(0, 2, 5, 3, 4, 1).reshape(pool, P, 2, GROUPS, SEL))
    k2 = cache[:, :, 2].reshape(pool, PAGE, 2, 2, HD).transpose(0, 3, 4, 2, 1).reshape(pool, P, 2 * P)
    arrays["cache_sel"] = np.ascontiguousarray(np.concatenate([k2, cache[:, :, 3].reshape(pool, P, 2 * P)], axis=2))
    win = A(state_kv_win)[0]
    kw = win[:, :, 0].reshape(SEQS, PAST, 2, 2, HD).transpose(3, 4, 0, 2, 1).reshape(P, SEQS, 2 * PAST)
    vw = win[:, :, 1].reshape(SEQS, 2, P, GROUPS * HD).transpose(2, 0, 1, 3).reshape(P, SEQS, 2 * PAST)
    arrays["cache_win"] = np.ascontiguousarray(np.concatenate([kw, vw], axis=2))
    arrays["win_state"] = np.ascontiguousarray(win[:, STEPS:].reshape(SEQS, -1))
    arrays["pages"] = np.ascontiguousarray(A(page_table).reshape(1, SEQS * NPG).astype(np.int32))
    arrays.update(shape_constants())
    outs = {"y": (P, KT, T), "conv_p": (P, CT, STATE), "conv_s": (P, CT, SEQS, STATE + STEPS),
            "kv_cmp": (P, 2, GROUPS, NP_ // 2), "kv_cmp_s": (P, 4, NS_), "k_new": (P, 2, 2, T),
            "v_new": (P, 5, 2 * GROUPS * HD), "win_s": (SEQS, (PAST - STEPS) * 2 * GROUPS * HD)}

    nc = bacc.Bacc("TRN2", target_bir_lowering=False, num_devices=1)
    io = {}
    for n, a in arrays.items():
        io[n] = nc.dram_tensor(f"in_{n}", a.shape, mybir.dt.from_np(a.dtype), kind="ExternalInput").ap()
    for n, shape in outs.items():
        io[n] = nc.dram_tensor(f"out_{n}", shape, F32, kind="ExternalOutput").ap()
    build(nc, io)
    r = run_bass_kernel_spmd(nc, [{f"in_{n}": a for n, a in arrays.items()}], core_ids=[0])
    r = r.results[0]
    y = r["out_y"].transpose(2, 1, 0).reshape(T, D)
    conv_p = r["out_conv_p"].transpose(2, 1, 0).reshape(1, 1, STATE, DC)
    conv_s = r["out_conv_s"][:, :, :, STEPS:].transpose(2, 3, 1, 0).reshape(1, SEQS, STATE, DC)
    kv = np.empty((T, 6, GROUPS, HD), np.float32)
    kv[:NP_, 0:2] = r["out_kv_cmp"].reshape(2, HD, 2, GROUPS, NP_ // 2).transpose(4, 0, 2, 3, 1).reshape(NP_, 2, GROUPS, HD)
    kv[NP_:, 0:2] = r["out_kv_cmp_s"].reshape(2, HD, 2, 2, NS_).transpose(4, 2, 3, 0, 1).reshape(NS_, 2, GROUPS, HD)
    k = r["out_k_new"].reshape(2, HD, 2, 2, T).transpose(4, 2, 3, 0, 1).reshape(T, 2, GROUPS, HD)
    v = r["out_v_new"].reshape(P, 5, 2, GROUPS, HD)
    v = np.concatenate([v[:, 0:4].transpose(1, 0, 2, 3, 4).reshape(NP_, 2, GROUPS, HD), v[:NS_, 4]], axis=0)
    kv[:, 2::2], kv[:, 3::2] = k, v
    kv_prompt = kv[:NP_, :4].reshape(1, 1, NP_, 4, GROUPS, HD)
    kv_sample = kv[NP_:, :4].reshape(1, SEQS, STEPS, 4, GROUPS, HD)
    win_prompt = kv[:NP_, 4:].reshape(1, 1, NP_, 2, GROUPS, HD)
    win_sample = np.concatenate([r["out_win_s"].reshape(SEQS, PAST - STEPS, 2, GROUPS, HD),
                                 kv[NP_:, 4:].reshape(SEQS, STEPS, 2, GROUPS, HD)], axis=1)[None]
    return (y[:NP_].reshape(1, NP_, D), y[NP_:].reshape(SEQS, STEPS, D), kv_prompt, kv_sample,
            win_prompt, win_sample, conv_p, conv_s)
```
